# Optimizing a Trainium2 kernel written in Bass

```python
import math
import jax, jax.numpy as jnp
from jax import lax
import numpy as np

D_MODEL = 1024
BATCH = 1
SEQ = 512
DEPTH = 1

GRID_W = 64
N_MEM = 256
RMS_EPS = 1e-6
NA_HEADS = 8
NA_HEAD_DIM = 64
NA_WIDTH = NA_HEADS * NA_HEAD_DIM
NA_WIN_R = 8
NA_WIN_C = 16
S5_GROUPS = 16
S5_GROUP_CH = 16
S5_WIDTH = S5_GROUPS * S5_GROUP_CH
S5_STATE = 64
S5_DT_MIN = 1e-3
S5_DT_MAX = 1e-1
XA_HEADS = 4
XA_HEAD_DIM = 64
XA_WIDTH = XA_HEADS * XA_HEAD_DIM
N_BRANCHES = 3
IN_COLS = 3 * NA_WIDTH + S5_WIDTH + XA_WIDTH + N_BRANCHES * D_MODEL
IN_SPLITS = (NA_WIDTH, 2 * NA_WIDTH, 3 * NA_WIDTH, 3 * NA_WIDTH + S5_WIDTH,
             3 * NA_WIDTH + S5_WIDTH + XA_WIDTH)
MOE_GROUPS = 4
MOE_EXPERTS_PER_GROUP = 4
MOE_EXPERTS = MOE_GROUPS * MOE_EXPERTS_PER_GROUP
MOE_TOP_K = 2
MOE_FF = 256

kernel_name = "hybrid_na_s5_memxattn_hmoe_encoder"

def rms_norm(x, g):
    x32 = x.astype(jnp.float32)
    y = x32 * lax.rsqrt(jnp.mean(x32 * x32, axis=-1, keepdims=True) + RMS_EPS)
    return (y * g.astype(jnp.float32)).astype(x.dtype)

def neighbourhood_attention(q, k, v, rpb):
    bsz, seq, _ = q.shape
    rows = seq // GRID_W
    win_r = min(NA_WIN_R, rows)
    shape = (bsz, rows, GRID_W, NA_HEADS, NA_HEAD_DIM)
    qg = q.reshape(shape) * (NA_HEAD_DIM ** -0.5)
    kg = k.reshape(shape)
    vg = v.reshape(shape)
    cols = np.arange(GRID_W)
    col_start = np.clip(cols - NA_WIN_C // 2, 0, GRID_W - NA_WIN_C)
    col_idx = col_start[:, None] + np.arange(NA_WIN_C)[None, :]
    col_bias_idx = col_idx - cols[:, None] + (NA_WIN_C - 1)

    def one_row(args):
        q_row, r = args
        r_start = jnp.clip(r - win_r // 2, 0, rows - win_r)
        k_blk = lax.dynamic_slice_in_dim(kg, r_start, win_r, axis=1)
        v_blk = lax.dynamic_slice_in_dim(vg, r_start, win_r, axis=1)
        k_nb = k_blk[:, :, col_idx]
        v_nb = v_blk[:, :, col_idx]
        row_bias_idx = r_start + jnp.arange(win_r) - r + (NA_WIN_R - 1)
        bias = rpb[:, row_bias_idx[None, :, None], col_bias_idx[:, None, :]]
        s = jnp.einsum('bchd,bicjhd->bhcij', q_row, k_nb).astype(jnp.float32) + bias.astype(jnp.float32)
        p = jax.nn.softmax(s.reshape(bsz, NA_HEADS, GRID_W, win_r * NA_WIN_C), axis=-1)
        p = p.reshape(s.shape).astype(v.dtype)
        return jnp.einsum('bhcij,bicjhd->bchd', p, v_nb)

    out = lax.map(one_row, (jnp.moveaxis(qg, 1, 0), jnp.arange(rows)))
    return jnp.moveaxis(out, 0, 1).reshape(bsz, seq, NA_WIDTH)

def _complex_linear_combine(earlier, later):
    a1r, a1i, b1r, b1i = earlier
    a2r, a2i, b2r, b2i = later
    return (a2r * a1r - a2i * a1i,
            a2r * a1i + a2i * a1r,
            a2r * b1r - a2i * b1i + b2r,
            a2r * b1i + a2i * b1r + b2i)

def s5_bidirectional(u, lam_re, lam_im, log_dt, b_re, b_im, c_re, c_im, d_skip, w_glu):
    bsz, seq, _ = u.shape
    uf = u.astype(jnp.float32).reshape(bsz, seq, S5_GROUPS, S5_GROUP_CH)
    y = d_skip.astype(jnp.float32).reshape(S5_GROUPS, S5_GROUP_CH) * uf
    for direction in range(2):
        lr = jnp.minimum(lam_re[direction].astype(jnp.float32), -1e-4)
        li = lam_im[direction].astype(jnp.float32)
        dt = jnp.exp(log_dt[direction].astype(jnp.float32))[:, None]
        mag = jnp.exp(lr * dt)
        ar = mag * jnp.cos(li * dt)
        ai = mag * jnp.sin(li * dt)
        den = lr * lr + li * li
        fr = ((ar - 1.0) * lr + ai * li) / den
        fi = (ai * lr - (ar - 1.0) * li) / den
        br = b_re[direction].astype(jnp.float32)
        bi = b_im[direction].astype(jnp.float32)
        bbar_re = fr[..., None] * br - fi[..., None] * bi
        bbar_im = fr[..., None] * bi + fi[..., None] * br
        bu_re = jnp.einsum('bsgc,gpc->bsgp', uf, bbar_re)
        bu_im = jnp.einsum('bsgc,gpc->bsgp', uf, bbar_im)
        a_re = jnp.broadcast_to(ar, (1, seq, S5_GROUPS, S5_STATE))
        a_im = jnp.broadcast_to(ai, (1, seq, S5_GROUPS, S5_STATE))
        _, _, x_re, x_im = lax.associative_scan(
            _complex_linear_combine, (a_re, a_im, bu_re, bu_im), reverse=(direction == 1), axis=1)
        y = y + jnp.einsum('bsgp,gcp->bsgc', x_re, c_re[direction].astype(jnp.float32)) \
              - jnp.einsum('bsgp,gcp->bsgc', x_im, c_im[direction].astype(jnp.float32))
    y = jax.nn.gelu(y.reshape(bsz, seq, S5_WIDTH))
    g = y @ w_glu.astype(jnp.float32)
    out = g[..., :S5_WIDTH] * jax.nn.sigmoid(g[..., S5_WIDTH:])
    return out.astype(u.dtype)

def memory_cross_attention(q, mem_kv):
    bsz, seq, _ = q.shape
    n_mem = mem_kv.shape[1]
    qh = q.reshape(bsz, seq, XA_HEADS, XA_HEAD_DIM) * (XA_HEAD_DIM ** -0.5)
    k_m = mem_kv[..., :XA_WIDTH].reshape(bsz, n_mem, XA_HEADS, XA_HEAD_DIM)
    v_m = mem_kv[..., XA_WIDTH:].reshape(bsz, n_mem, XA_HEADS, XA_HEAD_DIM)
    s = jnp.einsum('bshd,bmhd->bhsm', qh, k_m).astype(jnp.float32)
    p = jax.nn.softmax(s, axis=-1).astype(v_m.dtype)
    return jnp.einsum('bhsm,bmhd->bshd', p, v_m).reshape(bsz, seq, XA_WIDTH)

def hierarchical_moe(h, w_coarse, b_coarse, w_fine, b_fine, w_gate, w_up, w_down):
    bsz, seq, _ = h.shape
    coarse = (h @ w_coarse).astype(jnp.float32) + b_coarse.astype(jnp.float32)
    p_coarse = jax.nn.softmax(coarse, axis=-1)
    _, grp = lax.top_k(coarse, 1)
    p_grp = jnp.take_along_axis(p_coarse, grp, axis=-1)
    fine = ((h @ w_fine).astype(jnp.float32) + b_fine.astype(jnp.float32)).reshape(
        bsz, seq, MOE_GROUPS, MOE_EXPERTS_PER_GROUP)
    fine_g = jnp.take_along_axis(fine, grp[..., None], axis=2)[..., 0, :]
    top_v, top_i = lax.top_k(fine_g, MOE_TOP_K)
    w_top = jax.nn.softmax(top_v, axis=-1) * p_grp
    expert_idx = grp * MOE_EXPERTS_PER_GROUP + top_i
    comb = jnp.sum(jax.nn.one_hot(expert_idx, MOE_EXPERTS, dtype=jnp.float32) * w_top[..., None], axis=-2)
    comb = comb.astype(h.dtype)

    def per_row(args):
        hb, cb = args
        g = jnp.einsum('sd,edf->sef', hb, w_gate)
        u = jnp.einsum('sd,edf->sef', hb, w_up)
        a = jax.nn.silu(g) * u * cb[:, :, None]
        return jnp.einsum('sef,efd->sd', a, w_down)

    return lax.map(per_row, (h, comb))

def setup_inputs(seed: int = 0) -> dict:
    key = jax.random.key(seed)
    ks = iter(jax.random.split(key, 40))
    f32 = jnp.float32

    def nrm(shape, scale):
        return jax.random.normal(next(ks), shape, f32) * scale

    def gain(shape):
        return 1.0 + 0.02 * jax.random.normal(next(ks), shape, f32)

    L, D = DEPTH, D_MODEL
    n_idx = jnp.arange(S5_STATE, dtype=f32)
    return {
        "x": nrm((BATCH, SEQ, D), 1.0),
        "mem": nrm((BATCH, N_MEM, D), 1.0),
        "norm_mix": gain((L, D)),
        "norm_ffn": gain((L, D)),
        "norm_mem": gain((L, D)),
        "w_in": nrm((L, D, IN_COLS), D ** -0.5),
        "b_gate": nrm((L, N_BRANCHES * D), 0.02),
        "na_rpb": nrm((L, NA_HEADS, 2 * NA_WIN_R - 1, 2 * NA_WIN_C - 1), 0.1),
        "s5_lam_re": -0.5 + nrm((L, 2, S5_GROUPS, S5_STATE), 0.01),
        "s5_lam_im": math.pi * n_idx + nrm((L, 2, S5_GROUPS, S5_STATE), 0.01),
        "s5_log_dt": jax.random.uniform(next(ks), (L, 2, S5_GROUPS), f32,
                                        minval=math.log(S5_DT_MIN), maxval=math.log(S5_DT_MAX)),
        "s5_b_re": nrm((L, 2, S5_GROUPS, S5_STATE, S5_GROUP_CH), S5_GROUP_CH ** -0.5),
        "s5_b_im": nrm((L, 2, S5_GROUPS, S5_STATE, S5_GROUP_CH), S5_GROUP_CH ** -0.5),
        "s5_c_re": nrm((L, 2, S5_GROUPS, S5_GROUP_CH, S5_STATE), S5_STATE ** -0.5),
        "s5_c_im": nrm((L, 2, S5_GROUPS, S5_GROUP_CH, S5_STATE), S5_STATE ** -0.5),
        "s5_d": nrm((L, S5_WIDTH), 1.0),
        "s5_w_glu": nrm((L, S5_WIDTH, 2 * S5_WIDTH), S5_WIDTH ** -0.5),
        "w_mem_kv": nrm((L, D, 2 * XA_WIDTH), D ** -0.5),
        "w_br_na": nrm((L, NA_WIDTH, D), NA_WIDTH ** -0.5),
        "w_br_s5": nrm((L, S5_WIDTH, D), S5_WIDTH ** -0.5),
        "w_br_xa": nrm((L, XA_WIDTH, D), XA_WIDTH ** -0.5),
        "w_out": nrm((L, D, D), D ** -0.5),
        "moe_w_coarse": nrm((L, D, MOE_GROUPS), D ** -0.5),
        "moe_b_coarse": nrm((L, MOE_GROUPS), 0.01),
        "moe_w_fine": nrm((L, D, MOE_EXPERTS), D ** -0.5),
        "moe_b_fine": nrm((L, MOE_EXPERTS), 0.01),
        "moe_w_gate": nrm((L, MOE_EXPERTS, D, MOE_FF), D ** -0.5),
        "moe_w_up": nrm((L, MOE_EXPERTS, D, MOE_FF), D ** -0.5),
        "moe_w_down": nrm((L, MOE_EXPERTS, MOE_FF, D), MOE_FF ** -0.5),
        "final_norm": gain((D,)),
    }

def reference(x, mem, norm_mix, norm_ffn, norm_mem, w_in, b_gate, na_rpb,
              s5_lam_re, s5_lam_im, s5_log_dt, s5_b_re, s5_b_im, s5_c_re, s5_c_im, s5_d, s5_w_glu,
              w_mem_kv, w_br_na, w_br_s5, w_br_xa, w_out,
              moe_w_coarse, moe_b_coarse, moe_w_fine, moe_b_fine, moe_w_gate, moe_w_up, moe_w_down,
              final_norm):
    bsz, seq, d = x.shape
    for l in range(DEPTH):
        h = rms_norm(x, norm_mix[l])
        proj = h @ w_in[l]
        q_na, k_na, v_na, u_s5, q_xa, gate_logits = jnp.split(proj, IN_SPLITS, axis=-1)
        o_na = neighbourhood_attention(q_na, k_na, v_na, na_rpb[l])
        o_s5 = s5_bidirectional(u_s5, s5_lam_re[l], s5_lam_im[l], s5_log_dt[l],
                                s5_b_re[l], s5_b_im[l], s5_c_re[l], s5_c_im[l], s5_d[l], s5_w_glu[l])
        mem_kv = rms_norm(mem, norm_mem[l]) @ w_mem_kv[l]
        o_xa = memory_cross_attention(q_xa, mem_kv)
        gates = jax.nn.sigmoid((gate_logits + b_gate[l]).astype(jnp.float32)).astype(x.dtype)
        gates = gates.reshape(bsz, seq, N_BRANCHES, d)
        merged = gates[:, :, 0] * (o_na @ w_br_na[l]) \
               + gates[:, :, 1] * (o_s5 @ w_br_s5[l]) \
               + gates[:, :, 2] * (o_xa @ w_br_xa[l])
        x = x + merged @ w_out[l]
        h2 = rms_norm(x, norm_ffn[l])
        x = x + hierarchical_moe(h2, moe_w_coarse[l], moe_b_coarse[l], moe_w_fine[l], moe_b_fine[l],
                                 moe_w_gate[l], moe_w_up[l], moe_w_down[l])
    return rms_norm(x, final_norm)


_drawn_inputs = setup_inputs


def setup_inputs(seed=0):
    import zlib

    import numpy as np

    out = dict(_drawn_inputs(seed))
    spreads = {}
    factors = {'norm_mix': 5.459,
     'norm_ffn': 2.713,
     'norm_mem': 8.0,
     'b_gate': 7.282,
     'na_rpb': 4.182,
     's5_lam_re': 8.0,
     'moe_b_coarse': 5.983,
     'moe_b_fine': 4.136,
     'final_norm': 2.934}
    for name, (base, spread) in spreads.items():
        noise = np.random.default_rng([zlib.crc32(name.encode()), seed]).standard_normal(out[name].shape)
        drawn = base * np.exp(spread * noise) if base else spread * noise
        out[name] = __import__('jax').numpy.asarray(drawn.astype(out[name].dtype))
    for name, factor in factors.items():
        out[name] = (out[name] * factor).astype(out[name].dtype)
    return out
```

```python
import math
from contextlib import ExitStack

import concourse.bass as bass
from concourse import mybir

F32, F32R, BF16, I32, U32 = (mybir.dt.float32, mybir.dt.float32r, mybir.dt.bfloat16, mybir.dt.int32,
                             mybir.dt.uint32)
ALU, ACT, AX = mybir.AluOpType, mybir.ActivationFunctionType, mybir.AxisListType
ADD, SUB, MUL = ALU.add, ALU.subtract, ALU.mult

P = 128
D = 1024
KD = D // P
SEQ, GW = 512, 64
ROWS = SEQ // GW
NT = SEQ // P
MEM = 256
NAH, XAH, HD = 8, 4, 64
NAW, S5W, XAW = NAH * HD, 256, XAH * HD
G5, CH5, ST5 = 16, 16, 64
T5 = 8
K5 = SEQ // T5
DP = 2 * G5 // 2
NE, NG4, FF = 16, 4, 256
CAP = P
EPS = 1e-6
RPB_R, RPB_C = 15, 31
WIN = 16

C_U, C_MEMK, C_MEMV, C_QX, C_Q, C_K, C_V, C_GLU = 0, 2, 4, 6, 8, 12, 16, 20
C_S5G, C_S5P, C_XAG, C_XAP, C_NAG, C_NAP, C_OUT = 21, 29, 31, 39, 41, 49, 53
NCH = 61
RAW, HL = 6, 2
UNITS = XAH * NT + NAH * NT
GATE_CHUNKS = [*range(C_S5G, C_S5P), *range(C_XAG, C_XAP), *range(C_NAG, C_NAP)]
SLOTS = {c: 3 if n in range(4, 16) else 2 for n, c in enumerate(GATE_CHUNKS[:-4])}
TURNS = {C_XAP - 2 + j: (j,) for j in range(2)} | {C_NAP - 4 + j: (j,) for j in range(4)}
assert sum(SLOTS.values()) >= UNITS + 4


def tiles_of(c):
    if c < C_MEMK:
        return [("u", c)]
    if c < C_MEMV:
        return [("mk", c - C_MEMK)]
    if c < C_QX:
        return [("mv", c - C_MEMV)]
    if c < C_Q:
        return [("qx", c - C_QX)]
    if c < C_K:
        return [("q", c - C_Q)]
    if c < C_V:
        return [("k", c - C_K)]
    if c < C_GLU:
        return [("v", c - C_V)]
    if c == C_GLU:
        return [("gt", 0), ("gv", 0), ("gt", 1), ("gv", 1)]
    for name, first, proj, per in (("s5", C_S5G, C_S5P, 4), ("xa", C_XAG, C_XAP, 4), ("na", C_NAG, C_NAP, 2)):
        if first <= c < proj:
            turns = TURNS.get(c, ())
            return [(name + "t", j) for j in turns] + [(name + "g", c - first)]
        if proj <= c < proj + 8 // per:
            return [(name + "p", per * (c - proj) + j) for j in range(per)]
    return []


TILES = [t for c in range(NCH) for t in tiles_of(c)]
BY_DVE = ("gv", "s5p", "xap", "nap", "xat", "nat")


def taken(g):
    dve = TILES[g][0] in BY_DVE
    return dve, sum((t[0] in BY_DVE) == dve for t in TILES[:g + 1])


def unit(u):
    if u < XAH * NT:
        return False, u % XAH, u // XAH
    u -= XAH * NT
    return True, u % NAH, u // NAH


def window(i):
    lo, hi = max(0, P * i - 64), min(SEQ, P * i + 192)
    return lo, hi - lo, lo - (P * i - 64)


def key_chunks(i):
    lo, n, _ = window(i)
    out = []
    for w in (i, i + 1):
        a, b = max(0, P * w - 64), min(SEQ, P * w + 64)
        out.append((w, b - a, a - lo))
    return out


def build(nc, a, out):
    ctx = ExitStack()
    base = (nc.sbuf_base + 63) // 64 * 64

    def at(name, kb, cols, dt=F32):
        return nc.alloc_sbuf_tensor_at(name, [P, cols], dt, offset=base + int(kb * 1024))

    def v(t, off, *dims, p0=0, pn=P):
        first = t[p0:p0 + pn, 0:1]
        return bass.AP(tensor=first.tensor, offset=first.offset + off, ap=[first.ap[0]] + [list(d) for d in dims])

    sems = {}

    def sem(name):
        if name not in sems:
            sems[name] = ctx.enter_context(nc.semaphore(name))
        return sems[name]

    off = [0.0]

    def small(name, cols, dt=F32):
        t = at(name, off[0], cols, dt)
        off[0] += math.ceil(cols * (2 if dt == BF16 else 4) / 64) * 64 / 1024
        assert off[0] <= 10.5, (name, off[0])
        return t

    ident = small("ident", P)
    identb = small("identb", P, BF16)
    maskb = small("maskb", 3 * 256, BF16)
    upper = small("upper", P, BF16)
    onesb = small("onesb", P, BF16)
    prm = small("prm", P)
    prt = small("prt", P)
    bgh = small("bgh", 24)
    stat = small("stat", 64)
    s5s = small("s5s", 16 * 24)
    pw = small("pw", 2 * 9 * DP)
    soft = small("soft", 8 * 8)
    ct = small("ct", 3 * DP * CH5)
    lbias = small("lbias", 20)
    LR, LI, LDT, GMIX, GFFN, GMEM, BG, DS = 0, 16, 32, 48, 56, 64, 72, 96

    h_hi, h_lo = at("h_hi", 10.5, KD * SEQ, F32R), at("h_lo", 26.5, KD * SEQ, F32R)
    m_hi, m_lo = at("m_hi", 10.5, KD * SEQ, F32R), at("m_lo", 26.5, KD * SEQ, F32R)
    x_sb = at("x_sb", 42.5, NT * D)
    bat = at("bat", 42.5, 2 * DP * P)
    ca = at("ca", 42.5, 2 * DP * P)
    raw = at("raw", 58.5, RAW * 1024)
    w_hi, w_lo = at("w_hi", 82.5, HL * 1024, F32R), at("w_lo", 90.5, HL * 1024, F32R)
    mm_hi, mm_lo = at("mm_hi", 98.5, KD * MEM, F32R), at("mm_lo", 106.5, KD * MEM, F32R)
    qT, kT = at("qT", 98.5, 4 * SEQ), at("kT", 106.5, 4 * SEQ)
    na_hi, na_lo = at("na_hi", 98.5, 4 * SEQ, F32R), at("na_lo", 106.5, 4 * SEQ, F32R)
    vw = at("vw", 114.5, 5 * NAW)
    xa_hi, xa_lo = at("xa_hi", 136.5, 2 * SEQ, F32R), at("xa_lo", 140.5, 2 * SEQ, F32R)
    ctb = at("ctb", 118.5, 2 * DP * 32)
    cn = at("cn", 114.5, 8 * 2 * 64)
    ez = at("ez", 124.5, NAH * 256)
    mem_sb = at("mem_sb", 124.5, 2 * D)
    uT = at("uT", 132.5, 2 * SEQ)
    qxT, kmT, vm = at("qxT", 136.5, 2 * SEQ), at("kmT", 140.5, 2 * MEM), at("vm", 142.5, 2 * XAW)
    s5_hi, s5_lo = at("s5_hi", 144.5, 2 * SEQ, F32R), at("s5_lo", 148.5, 2 * SEQ, F32R)
    ezraw = at("ezraw", 144.5, NAH * 256)
    vt = at("vt", 152.5, 2 * SEQ)
    R0 = 156.5
    ba = at("ba", R0, 2 * DP * P)
    wz = at("wz", R0, 2 * DP * K5)
    tmp = at("tmp", R0 + 8, 2 * DP * K5)
    ypk = at("ypk", R0 + 8, G5 * K5)
    yT = at("yT", R0, 2 * SEQ)
    yg = at("yg", R0 + 4, 2 * SEQ)
    phase = at("phase", R0 + 16, 2 * DP * K5)
    y_hi, y_lo = at("y_hi", R0 + 16, 2 * SEQ, F32R), at("y_lo", R0 + 20, 2 * SEQ, F32R)
    mg = at("mg", R0 + 24, G5 * P)
    glut = at("glut", R0 + 24, 2 * SEQ)
    glui = at("glui", R0 + 28, 2 * SEQ)
    st = [at("st_re", 114.5, 2 * DP * (K5 + 1)), at("st_im", R0 + 32, 2 * DP * (K5 + 1))]
    decay = at("decay", R0 + 40.25, DP * K5)
    upk = at("upk", R0 + 44.25, G5 * K5)
    stk = at("stk", R0 + 48.25, 2 * G5 * CH5)
    bb = at("bb", R0 + 40.25, 4 * DP * CH5)
    squares = at("squares", R0, 6 * D)
    junk = at("junk", R0 + 32, D)
    pjunk = at("pjunk", R0 + 36, D)
    wide = at("wide", R0 + 44.25, 352)
    flip = at("flip", R0 + 46, P)
    pt5 = at("pt5", 144.5, 2 * 8 * P)
    merged = at("merged", R0, KD * SEQ)
    gt = at("gt", R0 + 16, KD * SEQ)
    onat = at("onat", R0 + 32, NT * 512)
    ssb = at("ssb", R0 + 40, 3 * 256)
    pr = at("pr", R0 + 43, 3 * 256)
    pts = at("pts", R0 + 46, 2 * 256)
    onx = at("onx", 132.5, NT * 256)
    prod = at("prod", 152.5, 2 * SEQ)
    E0, R1 = 98.5, 146.5
    eraw = at("eraw", E0, 6 * 2048)
    HLK = [10.5, 26.5, 58.5]
    e_hi = [at(f"e_hi{j}", HLK[j], 2048, F32R) for j in range(3)]
    e_lo = [at(f"e_lo{j}", HLK[j] + 8, 2048, F32R) for j in range(3)]
    xt_hi, xt_lo = at("xt_hi", 74.5, KD * P, F32R), at("xt_lo", 78.5, KD * P, F32R)
    at_hi, at_lo = at("at_hi", 82.5, 2 * P, F32R), at("at_lo", 83.5, 2 * P, F32R)
    act_t, act_s, act_a = at("act_t", 84.5, FF), at("act_s", 85.5, FF), at("act_a", 86.5, FF)
    gfin = at("gfin", 87.5, D)
    rt = at("rt", 91.5, 1152)
    selb = at("selb", 96, 4 * NE, BF16)
    rowi = at("rowi", 96.25, 8, I32)
    toki = at("toki", 96.5, 4, I32)
    idx = at("idx", 96.75, NE, I32)
    flag = at("flag", 97, 1, I32)
    wcf = at("wcf", 97.25, KD * 20)
    wts = at("wts", 96.0 + 2.0, 8)
    idxo = at("idxo", 98.125, 1, I32)
    gffb = at("gffb", 186.5, D)
    xtf = at("xtf", R1, KD * P)
    atf = at("atf", R1 + 4, 2 * P)
    zi = at("zi", 152.5, 64, I32)
    h2 = at("h2", R1, NT * D)
    h2T = at("h2T", R1 + 16, KD * SEQ)
    xg = at("xg", R1 + 32, 2 * D)
    ysb = at("ysb", R1 + 40, 2 * D)
    y0 = at("y0", R1, NT * D)
    y1 = at("y1", R1 + 16, NT * D)

    bank = [ctx.enter_context(nc.psum_tensor(f"bank{i}", [P, 512], F32)) for i in range(8)]

    u_dram = nc.dram_tensor("u_scratch", (S5W, SEQ), F32, kind="Internal").ap()
    y_dram = nc.dram_tensor("y_scratch", (P, G5 * K5), F32, kind="Internal").ap()
    h2_dram = nc.dram_tensor("h2_scratch", (SEQ, D), F32, kind="Internal").ap()
    ye_dram = nc.dram_tensor("ye_scratch", (CAP * NE, D), F32, kind="Internal").ap()
    ya_dram = nc.dram_tensor("ya_scratch", (SEQ * NE, D), F32, kind="Internal").ap()
    tok_dram = nc.dram_tensor("tok_scratch", (SEQ * NE, 1), I32, kind="Internal").ap()

    w_in = a["w_in"][0]
    x_nat = a["x"][0].rearrange("(n p) d -> p n d", p=P)
    out_nat = out[0].rearrange("(n p) d -> p n d", p=P)

    def chunk_src(c):
        def cols(w, c0, n=P):
            return w[:, c0:c0 + n].rearrange("(k p) n -> p k n", p=P)
        if c < C_MEMK:
            return cols(w_in, 3 * NAW + P * c)
        if c < C_QX:
            return cols(a["w_mem_kv"][0], P * (c - C_MEMK))
        if c < C_Q:
            return cols(w_in, 3 * NAW + S5W + P * (c - C_QX))
        if c < C_GLU:
            return cols(w_in, P * (c - C_Q))
        if c == C_GLU:
            return cols(a["s5_w_glu"][0], 0, 512)
        g0 = 3 * NAW + S5W + XAW
        for first, branch in ((C_S5G, 1), (C_XAG, 2), (C_NAG, 0)):
            if first <= c < first + 8:
                return cols(w_in, g0 + D * branch + P * (c - first))
        if C_S5P <= c < C_XAG:
            return cols(a["w_br_s5"][0], 512 * (c - C_S5P), 512)
        if C_XAP <= c < C_NAG:
            return cols(a["w_br_xa"][0], 512 * (c - C_XAP), 512)
        if C_NAP <= c < C_OUT:
            return cols(a["w_br_na"][0], 256 * (c - C_NAP), 256)
        half, kp = divmod(c - C_OUT, 4)
        return a["w_out"][0][256 * kp:256 * kp + 256, 512 * half:512 * half + 512].rearrange(
            "(k p) n -> p k n", p=P)

    def unit_src(kind, e):
        one = slice(e, e + 1) if isinstance(e, int) else bass.ds(e, 1)
        if kind == 2:
            w = a["moe_w_down"][0][one].rearrange("o (k p) n -> p (o k) n", p=P)
            return [w[:, k:k + 1, :] for k in range(2)]
        return [a[w][0][one].rearrange("o (k p) n -> p (o k) n", p=P)[:, 4 * kind:4 * kind + 4, :]
                for w in ("moe_w_gate", "moe_w_up")]

    def unit_dst(kind, slot):
        if kind == 2:
            return [v(eraw, 2048 * slot + D * k, [D, 1], [1, D]) for k in range(2)]
        return [v(eraw, 2048 * slot + FF * j, [2 * FF, 4], [1, FF]) for j in range(2)]


    def counted(ins, name, n=1):
        return ins.then_inc(sem(name), n)

    def s5(i):
        return v(s5s, DP * i, [1, DP])

    def pcol(c, n=1):
        return v(prt, c, [1, n])

    def pv(b, off, *dims, p0=0, pn=P):
        return v(bank[b], off, *dims, p0=p0, pn=pn)

    def raw32(x):
        return x.bitcast(F32)

    def needed(eng):
        eng.wait_ge(sem("flag"), 1)
        return eng.value_load(flag[0:1, 0:1], min_val=0, max_val=1) > 0

    def newton(x, y, t, link):
        for _ in range(2):
            link(nc.vector.tensor_tensor(t, y, y, MUL))
            link(nc.vector.scalar_tensor_tensor(t, t, -0.5, x, MUL, MUL))
            link(nc.vector.scalar_tensor_tensor(y, t, 1.5, y, ADD, MUL))

    def cmul(eng, link, o, x, y, t):
        eng.tensor_tensor(o[0], x[0], y[0], MUL)
        eng.tensor_tensor(t[0], x[1], y[1], MUL)
        eng.tensor_tensor(o[1], x[0], y[1], MUL)
        link(eng.tensor_tensor(t[1], x[1], y[0], MUL))
        eng.tensor_tensor(o[0], o[0], t[0], SUB)
        link(eng.tensor_tensor(o[1], o[1], t[1], ADD))

    PW = 9 * DP

    def power(l, n=1):
        return [v(pw, PW * ri + DP * l, [DP, n], [1, DP]) for ri in range(2)]

    def square(eng, link):
        cmul(eng, link, [s5(20), s5(21)], [s5(18), s5(19)], [s5(18), s5(19)], [s5(22), s5(23)])
        eng.tensor_copy(s5(18), s5(20))
        link(eng.tensor_copy(s5(19), s5(21)))

    def powers_of_b(eng, link, d, h, t):
        o = [v(ba, 2048 * r + 1024 * d + 512 * h, [P, 4], [16, 8], [1, 16]) for r in range(2)]
        x = [v(pw, PW * r + (7 * DP if d == 0 else 0) + 8 * d + 4 * h, [1, 4],
               [-DP if d == 0 else DP, 8], [0, 16]) for r in range(2)]
        y = [v(bb, 512 + 256 * r + 128 * d + 64 * h, [16, 4], [0, 8], [1, 16]) for r in range(2)]
        cmul(eng, link, o, x, y, [v(t, 512 * r, [P, 4], [16, 8], [1, 16]) for r in range(2)])

    def wait_taken(eng, g):
        dve, n = taken(g)
        eng.wait_ge(sem("dve_took" if dve else "act_took"), n)

    def chunk_used(eng, c):
        if c < C_OUT:
            eng.wait_ge(sem("tile"), sum(len(tiles_of(i)) for i in range(c + 1)))
        else:
            eng.wait_ge(sem("out_k"), c - C_OUT + 1)

    def store_y(pool, e):
        pool.wait_ge(sem("y_a"), e + 1)
        pool.wait_ge(sem("y_d"), e + 1)
        pool.dma_start(ye_dram.rearrange("(s e) d -> s e d", e=NE)[0:P, e, :],
                       v(ysb, D * (e % 2), [1, D])).then_inc(sem(f"y_st{e % 2}"), 16)

    OUT_BANK = ((2, 3, 4, 5), (6, 7, 0, 1))
    g_of = {t: g for g, t in enumerate(TILES)}
    turned = [("mv", 0), ("mv", 1), ("v", 0), ("v", 1), ("v", 2), ("v", 3)]

    block = ctx.enter_context(nc.Block())

    @block.sync
    def _(sp):
        for n in range(NT):
            sp.dma_start(v(x_sb, D * n, [1, D]), x_nat[:, n, :]).then_inc(sem(f"x_in{n}"), 16)

        def load(c):
            if c >= RAW:
                sp.wait_ge(sem("w_lo_done"), c - RAW + 1)
            src = chunk_src(c)
            k, n = src.shape[1], src.shape[2]
            sp.dma_start(v(raw, 1024 * (c % RAW), [n, k], [1, n]), src).then_inc(sem(f"w_in{c % RAW}"), 16)

        load(0)
        sp.dma_start(v(mem_sb, 0, [D, 2], [1, D]), a["mem"][0].rearrange("(n p) d -> p n d", p=P)).then_inc(
            sem("mem_in"), 16)
        for c in range(1, C_NAG):
            load(c)
        sp.wait_ge(sem("s5_y"), 2)
        sp.dma_start(v(x_sb, 0, [D, NT], [1, D]), x_nat).then_inc(sem("x_again"), 16)
        for c in range(C_NAG, NCH):
            load(c)

        def load_unit(kind, e, slot):
            for dst, src in zip(unit_dst(kind, slot), unit_src(kind, e)):
                sp.dma_start(dst, src).then_inc(sem(f"e_in{slot}"), 16)

        sp.wait_ge(sem("prod"), 24)
        load_unit(0, 0, 0)
        load_unit(1, 0, 1)

        def loads(e, slots, freed):
            for kind, ee, slot, f in ((0, e, slots[0], freed), (1, e, slots[1], freed + 1),
                                      (2, e - 1, slots[2], freed + 2)):
                sp.wait_ge(sem("e_lo_done"), f)
                load_unit(kind, ee, slot)

        load_unit(0, 1, 2)
        load_unit(1, 1, 3)
        load_unit(2, 0, 4)
        load_unit(0, 2, 5)
        sp.wait_ge(sem("e_lo_done"), 1)
        load_unit(1, 2, 0)
        sp.wait_ge(sem("e_lo_done"), 2)
        load_unit(2, 1, 1)
        with sp.Fori(0, 6) as i:
            loads(2 * i + 3, (2, 3, 4), 6 * i + 3)
            loads(2 * i + 4, (5, 0, 1), 6 * i + 6)
        loads(15, (2, 3, 4), 39)
        sp.wait_ge(sem("e_lo_done"), 42)
        load_unit(2, 15, 5)

        with sp.If(needed(sp)):
            with sp.Fori(0, 3) as j:
                with sp.Fori(0, NE) as e:
                    sp.wait_ge(sem("ov_idx"), 16 * (NE * j + e) + 16)
                    for kind in range(3):
                        for dst, src in zip(unit_dst(kind, kind), unit_src(kind, e)):
                            sp.dma_start(dst, src).then_inc(sem("ov_in"), 16)

        for n in range(NT):
            sp.wait_ge(sem("out_ready"), n + 1)
            sp.dma_start(out_nat[:, n, :], v(x_sb, D * n, [1, D])).then_inc(sem("out_done"), 16)
        sp.wait_ge(sem("out_done"), 16 * NT)

    @block.scalar
    def _(act):
        def rows(w, r, n):
            act.dma_start(v(prm, 0, [1, P], p0=r, pn=n), w).then_inc(sem("prm_in"), 16)

        rows(a["s5_lam_re"][0].rearrange("d (p g) n -> (d p) (g n)", g=2), LR, DP)
        rows(a["s5_lam_im"][0].rearrange("d (p g) n -> (d p) (g n)", g=2), LI, DP)
        rows(a["norm_mix"][0].rearrange("(k p) -> k p", p=P), GMIX, KD)
        rows(a["norm_ffn"][0].rearrange("(k p) -> k p", p=P), GFFN, KD)
        rows(a["norm_mem"][0].rearrange("(k p) -> k p", p=P), GMEM, KD)
        rows(a["b_gate"][0].rearrange("(k p) -> k p", p=P), BG, 3 * KD)
        rows(a["s5_d"][0].rearrange("(k p) -> k p", p=P), DS, 2)
        act.dma_start(v(stat, 60, [1, 2], p0=LDT, pn=DP),
                      a["s5_log_dt"][0].rearrange("d (p g) -> (d p) g", g=2)).then_inc(sem("prm_in"), 16)
        for ri, w in enumerate(("s5_c_re", "s5_c_im")):
            src = a[w][0].rearrange("d (h g) c n -> (g c) (d h) n", g=8)
            for twice in range(2):
                act.dma_start(v(cn, 512 * ri + 64 * twice, [P, 4], [1, 64]), src).then_inc(sem("c_in"), 16)
        for ri, w in enumerate(("s5_b_re", "s5_b_im")):
            act.dma_start(v(bb, 256 * ri, [CH5, DP], [1, CH5]),
                          a[w][0].rearrange("d (p g) n c -> (g n) (d p) c", g=2)).then_inc(sem("b_in"), 16)
        act.dma_start(v(lbias, 0, [1, 4]), a["moe_b_coarse"].partition_broadcast(P)).then_inc(sem("lb_in"), 16)
        act.dma_start(v(lbias, 4, [1, 16]), a["moe_b_fine"].partition_broadcast(P)).then_inc(sem("lb_in"), 16)

        def hi(c):
            act.wait_ge(sem(f"w_in{c % RAW}"), 16 * (c // RAW + 1))
            if c >= HL:
                chunk_used(act, c - HL)
            act.copy(v(w_hi, 1024 * (c % HL), [1, 1024]), v(raw, 1024 * (c % RAW), [1, 1024])).then_inc(
                sem("w_hi_done"), 1)

        act.wait_ge(sem("stat_set"), 1)
        act.activation(v(stat, 40, [1, 1]), v(stat, 48, [1, 1]), ACT.Sqrt)
        for n in range(NT):
            act.wait_ge(sem(f"x_in{n}"), 16)
            act.activation(v(squares, D * n, [1, D]), v(x_sb, D * n, [1, D]), ACT.Square, accum_out=v(stat, n, [1, 1]))
        act.wait_ge(sem("mem_in"), 16)
        for n in range(2):
            ins = act.activation(v(squares, D * (NT + n), [1, D]), v(mem_sb, D * n, [1, D]), ACT.Square,
                                 accum_out=v(stat, NT + n, [1, 1]))
        ins.then_inc(sem("squares"), 1)
        act.wait_ge(sem("means"), 1)
        act.activation(v(stat, 16, [1, 6]), v(stat, 8, [1, 6]), ACT.Sqrt).then_inc(sem("roots"), 1)
        hi(0)
        hi(1)
        act.wait_ge(sem("prt_ready"), 1)
        act.activation(s5(2), pcol(LDT, DP), ACT.Exp).then_inc(sem("s5_exp"), 1)
        act.wait_ge(sem("s5_arg"), 1)
        act.activation(s5(4), s5(3), ACT.Exp).then_inc(sem("s5_exp"), 1)
        act.activation(s5(5), s5(3), ACT.Exp, scale=float(T5)).then_inc(sem("s5_exp"), 1)
        def turn_hi(b):
            act.wait_ge(sem("turned"), b + 1)
            if b < KD:
                act.activation(v(h_hi, SEQ * b, [1, ROWS], [ROWS, GW]), pv(4 + b % 4, 0, [GW, ROWS], [1, GW]),
                               ACT.Identity, scale=pcol(GMIX + b)).then_inc(sem("turn_hi"), 1)
            else:
                act.activation(v(mm_hi, MEM * (b - KD), [1, MEM]), pv(4 + b % 4, 0, [1, MEM]),
                               ACT.Identity, scale=pcol(GMEM + b - KD)).then_inc(sem("turn_hi"), 1)

        for b in range(KD):
            turn_hi(b)
        act.wait_ge(sem("c_turned"), 2)
        for ri in range(2):
            for g2 in range(2):
                for h in range(4):
                    src = pv(2 + ri, P * h + 16 * g2, [32, 4], [1, 16], p0=64 * g2, pn=64)
                    for part, scale in ([(0, 1.0)] if ri == 0 else [(1, 1.0), (2, -1.0)]):
                        ins = act.mul(v(ct, 256 * part + 64 * h, [16, 4], [1, 16], p0=64 * g2, pn=64), src, scale)
                    ins = act.mul(v(ctb, 512 * ri + 128 * h + 16 * g2, [32, 4], [1, 16], p0=64 * g2, pn=64), src,
                                  -1.0 if ri else 1.0)
            ins.then_inc(sem("ct_ready"), 1)
        act.wait_ge(sem("s5_arg"), 2)
        act.activation(v(s5s, 16 * 6, [1, 32]), v(s5s, 16 * 8, [1, 32]), ACT.Sin).then_inc(sem("s5_sin"), 1)

        def take(g):
            kind, m = TILES[g]
            if kind in ("xat", "nat"):
                act.wait_ge(sem("tile"), g + 1)
                dst = xa_hi if kind == "xat" else na_hi
                act.copy(v(dst, SEQ * m, [1, SEQ]), pv(g % 2, 0, [1, SEQ])).then_inc(sem("o_hi"), 1)
            if kind in BY_DVE:
                return
            act.wait_ge(sem("tile"), g + 1)
            if kind == "u":
                ins = act.copy(v(uT, SEQ * m, [64, 8], [8, 8], [1, 8]), pv(g % 2, 0, [8, 8], [1, 8], [64, 8]))
            elif kind == "mk":
                ins = act.copy(v(kmT, MEM * m, [1, MEM]), pv(g % 2, 0, [1, MEM]))
            elif kind in ("mv", "v"):
                j = turned.index((kind, m))
                if j >= 2:
                    act.wait_ge(sem("v_turned"), j - 1)
                else:
                    act.wait_ge(sem("tok_zero"), 16)
                n = MEM if kind == "mv" else SEQ
                ins = act.copy(v(vt, SEQ * (j % 2), [1, n]), pv(g % 2, 0, [1, n]))
            elif kind == "qx":
                ins = act.mul(v(qxT, SEQ * m, [1, SEQ]), pv(g % 2, 0, [1, SEQ]), HD ** -0.5)
            elif kind == "q":
                if m == 0:
                    act.wait_ge(sem("tile"), g_of[("mv", 1)] + 1)
                ins = act.mul(v(qT, SEQ * m, [1, SEQ]), pv(g % 2, 0, [1, SEQ]), HD ** -0.5)
            elif kind == "k":
                ins = act.copy(v(kT, SEQ * m, [1, SEQ]), pv(g % 2, 0, [1, SEQ]))
            elif kind == "gt":
                ins = act.activation(v(glut, SEQ * m, [1, SEQ]), pv(g % 2, 0, [1, SEQ]), ACT.Tanh, scale=0.5)
            else:
                turn = ("s5g", "xag", "nag").index(kind)
                if turn:
                    act.wait_ge(sem("prod"), 8 * (turn - 1) + m + 1)
                elif m == 0:
                    act.wait_ge(sem("s5_lo"), 2)
                branch = {"s5g": 1, "xag": 2, "nag": 0}[kind]
                ins = act.activation(v(gt, SEQ * m, [1, SEQ]), pv(g % 2, 0, [1, SEQ]), ACT.Tanh, scale=0.5,
                                     bias=v(bgh, KD * branch + m, [1, 1]))
            ins.then_inc(sem("act_took"), 1)

        def exp(u):
            na, h, i = unit(u)
            act.wait_ge(sem("smax"), u + 1)
            if u >= 3:
                act.wait_ge(sem("p_turned"), u - 2)
            n = window(i)[1] if na else MEM
            src = v(ssb, 256 * (u % 3), [1, n]) if na else pv(2 + u % 2, 0, [1, n])
            act.activation(v(pr, 256 * (u % 3), [1, n]), src, ACT.Exp, bias=v(soft, 8 * (u % 8) + 1, [1, 1]),
                           accum_out=v(soft, 8 * (u % 8) + 2, [1, 1])).then_inc(sem("exp"), 1)

        def take_p(u):
            na, h, i = unit(u)
            act.wait_ge(sem("p_turned"), u + 1)
            if u >= 2:
                act.wait_ge(sem("pv"), u - 1)
            parts = [(n, k) for k, (_, n, _) in enumerate(key_chunks(i))] if na else [(P, 0), (P, 1)]
            if parts[0][0] == parts[1][0]:
                ins = act.copy(v(pts, 256 * (u % 2), [1, 256]), pv(4 + u % 2, 0, [1, 256]))
            else:
                for n, k in parts:
                    ins = act.copy(v(pts, 256 * (u % 2) + P * k, [1, P], pn=n), pv(4 + u % 2, P * k, [1, P], pn=n))
            ins.then_inc(sem("p_taken"), 1)

        def slot(s):
            if s < UNITS:
                exp(s)
            if 0 <= s - 2 < UNITS:
                take_p(s - 2)

        def take_s5_matrices():
            for q in range(8):
                act.wait_ge(sem("ba_turned"), q + 1)
                act.copy(v(bat, 512 * q, [1, 512]), pv(4 + q % 4, 0, [1, 512])).then_inc(sem("bat_took"), 1)
            act.wait_ge(sem("lags"), 1)
            act.copy(v(stk, 0, [1, 512]), pv(2, 0, [1, 512])).then_inc(sem("lags_took"), 1)
            for b in range(4):
                act.wait_ge(sem("shifted"), b + 1)
                act.copy(v(mg, 32 * b, [16, 2], [P, 16], [1, 16]),
                         pv(4 + b, 0, [256, 2], [16, 16], [1, 16])).then_inc(sem("mg_took"), 1)
            act.wait_ge(sem("u_out"), 16)
            for t in range(T5):
                act.dma_start(v(upk, 0, [K5, G5], [1, K5], p0=16 * t, pn=16),
                              u_dram.rearrange("(g c) (t k) -> c g t k", c=16, k=K5)[:, :, t, :]).then_inc(
                                  sem("u_in"), 16)

        def merged_hi(k):
            act.wait_ge(sem("prod"), 2 * KD + k + 1)
            act.mul(v(m_hi, SEQ * k, [1, GW], [GW, ROWS]), v(merged, SEQ * k, [ROWS, GW], [1, ROWS]), 0.5).then_inc(
                sem("m_hi"), 1)

        def take_y():
            act.wait_ge(sem("s5_y"), 2)
            for b in range(2):
                ins = act.copy(v(ypk, 512 * b, [1, 512]), pv(2 + b, 0, [1, 512]))
            ins.then_inc(sem("y_took"), 1)
            act.wait_ge(sem("y_took"), 1)
            act.dma_start(y_dram, v(ypk, 0, [1, G5 * K5])).then_inc(sem("y_out"), 16)

        def load_y():
            act.wait_ge(sem("y_out"), 16)
            for g in range(G5):
                act.dma_start(v(yT, SEQ * (g // 8), [K5, T5], [1, K5], p0=16 * (g % 8), pn=16),
                              y_dram.rearrange("(t c) (g k) -> c t g k", c=16, k=K5)[:, :, g, :]).then_inc(
                                  sem("y_in"), 16)

        g = 0
        s = 0
        for c in range(C_OUT):
            if c in SLOTS:
                slot(s)
                s += 1
            for kind, _ in tiles_of(c):
                if kind[2:] == "g":
                    for _ in range(SLOTS.get(c, 1) - 1):
                        slot(s)
                        s += 1
                take(g)
                g += 1
            hi(c + 2)
            for k in range(2 * (c - C_NAP) - 2, 2 * (c - C_NAP)):
                if k >= 0:
                    merged_hi(k)
            if c == 1:
                act.wait_ge(sem("act_took"), 2)
                act.dma_start(u_dram.rearrange("(m p) n -> p m n", p=P),
                              v(uT, 0, [SEQ, 2], [1, SEQ])).then_inc(sem("u_out"), 16)
            if c < 2:
                for b in range(KD + 4 * c, KD + 4 * c + 4):
                    turn_hi(b)
            if c == 3:
                for q in range(4):
                    act.wait_ge(sem("flipped"), q + 1)
                    for h in range(2):
                        ins = act.copy(v(ez, 512 * q + 256 * h, [8, 32], [1, 8]),
                                       pv(4 + q % 2, 256 * h, [1, 32], [RPB_C, 8]))
                    ins.then_inc(sem("bias_ready"), 1)
            if c == 8:
                take_s5_matrices()
            if c == 14:
                take_y()
            if c == 15:
                load_y()
            if c == 17:
                act.wait_ge(sem("gelu_in"), 1)
                act.activation(v(glut, 0, [1, 2 * SEQ]), v(yT, 0, [1, 2 * SEQ]), ACT.Tanh,
                               scale=math.sqrt(2 / math.pi)).then_inc(sem("gelu_t"), 1)
        for k in range(6, KD):
            merged_hi(k)
        for c in range(C_OUT + 2, NCH):
            hi(c)

        act.wait_ge(sem("prod"), 3 * KD)
        act.dma_start(v(gffb, 0, [1, D]), a["norm_ffn"].partition_broadcast(P)).then_inc(sem("gf_in"), 16)
        act.wait_ge(sem("out_k"), 8)
        act.dma_start(v(wcf, 0, [20, KD], [1, 4]),
                      a["moe_w_coarse"][0].rearrange("(k p) n -> p k n", p=P)).then_inc(sem("wcf_in"), 16)
        act.dma_start(v(wcf, 4, [20, KD], [1, 16]),
                      a["moe_w_fine"][0].rearrange("(k p) n -> p k n", p=P)).then_inc(sem("wcf_in"), 16)
        act.dma_start(v(gfin, 0, [1, D]), a["final_norm"].partition_broadcast(P)).then_inc(sem("gfin_in"), 16)

        def sums(done, spare):
            act.activation(v(stat, 41 + done // NT, [1, 1]), v(stat, 48, [1, 1]), ACT.Sqrt)
            for n in range(NT):
                act.wait_ge(sem("x2"), done + n + 1)
                ins = act.activation(v(spare, D * n, [1, D]), v(x_sb, D * n, [1, D]), ACT.Square,
                                     accum_out=v(stat, n, [1, 1]))
            ins.then_inc(sem("squares"), 1)
            act.wait_ge(sem("means"), 2 + done // NT)
            act.activation(v(stat, 16, [1, NT]), v(stat, 8, [1, NT]), ACT.Sqrt).then_inc(sem("roots"), 1)

        sums(0, h2T)
        for b in range(KD):
            act.wait_ge(sem("h2_turned"), b + 1)
            act.copy(v(h2T, SEQ * b, [1, SEQ]), pv(b % 4, 0, [1, SEQ])).then_inc(sem("h2_took"), 1)

        act.wait_ge(sem("route_arg"), 1)
        act.activation(v(rt, 960, [1, 20]), v(rt, 960, [1, 20]), ACT.Exp).then_inc(sem("route_exp"), 1)

        def unit_hi(n, j, load, dst):
            act.wait_ge(sem(f"e_in{j}"), 32 * load)
            if not (isinstance(n, int) and n < 3):
                act.wait_ge(sem("e_used"), n - 2)
            act.copy(v(e_hi[dst], 0, [1, 2048]), v(eraw, 2048 * j, [1, 2048])).then_inc(sem("e_hi_done"), 1)

        def xt_take(e):
            for j in range(2):
                act.wait_ge(sem("xt"), 2 * e + j + 1)
                act.copy(v(xt_hi, 512 * j, [1, 512]), pv(4 + j, 0, [1, 512])).then_inc(sem("xt_hi"), 1)

        def step(e, odd, loads, stored):
            peeled = isinstance(e, int)
            if not peeled or e >= 1:
                act.wait_ge(sem("at"), e)
                act.copy(v(at_hi, 0, [1, 256]), pv(6, 0, [1, 256])).then_inc(sem("at_hi"), 1)
            if not peeled or e < 15:
                unit_hi(3 * e + 2, 5 if odd else 2, loads[0], 2)
            if not peeled or e < 16:
                act.wait_ge(sem("e_used"), 2 if peeled and e == 0 else 3 * e + 1)
                if not peeled or e >= 1:
                    act.wait_ge(sem("act_a"), e)
                act.activation(v(act_t, 0, [1, FF]), pv(1 if odd else 0, 0, [1, FF]), ACT.Tanh,
                               scale=0.5).then_inc(sem("tanh"), 1)
            if not peeled or e < 15:
                xt_take(e + 1)
                unit_hi(3 * e + 3, 0 if odd else 3, loads[1], 0)
                unit_hi(3 * e + 4, 1 if odd else 4, loads[2], 1)
            elif e == 15:
                unit_hi(47, 5, 8, 2)
            if not peeled or e >= 1:
                act.wait_ge(sem("e_used"), 48 if peeled and e == 16 else 3 * e + 2)
                if stored is not None:
                    act.wait_ge(sem(f"y_st{0 if odd else 1}"), stored)
                act.copy(v(ysb, 0 if odd else D, [1, 512]), pv(2, 0, [1, 512])).then_inc(sem("y_a"), 1)

        unit_hi(0, 0, 1, 0)
        unit_hi(1, 1, 1, 1)
        xt_take(0)
        for e in range(3):
            step(e, e % 2 == 1, [(3 * e + j) // 6 + 1 for j in (2, 3, 4)], None)
        with act.Fori(0, 6) as i:
            step(2 * i + 3, True, (i + 2, i + 3, i + 3), 16 * i + 16)
            step(2 * i + 4, False, (i + 3, i + 3, i + 3), 16 * i + 16)
        step(15, True, None, 16 * 7)
        step(16, False, None, 16 * 7)

        with act.If(needed(act)):
            with act.Fori(0, 3) as j:
                with act.Fori(0, NE) as e:
                    it = NE * j + e + 1
                    act.wait_ge(sem("ov_xt"), it)
                    for b in range(2):
                        ins = act.copy(v(xtf, 512 * b, [1, 512]), pv(4 + b, 0, [1, 512]))
                    ins.then_inc(sem("ov_x"), 1)
                    act.wait_ge(sem("ov_gu"), it)
                    act.activation(v(act_t, 0, [1, FF]), pv(0, 0, [1, FF]), ACT.Tanh, scale=0.5).then_inc(
                        sem("ov_tanh"), 1)
                    act.wait_ge(sem("ov_at"), it)
                    act.copy(v(atf, 0, [1, 256]), pv(6, 0, [1, 256])).then_inc(sem("ov_ac"), 1)
                    act.wait_ge(sem("ov_down"), it)
                    for b in range(2):
                        ins = act.copy(v(ysb, 512 * b, [1, 512]), pv(2 + b, 0, [1, 512]))
                    ins.then_inc(sem("ov_y"), 1)
        sums(NT, eraw)

    @block.vector
    def _(dve):
        count = {}

        def done(ins, name):
            ins.then_inc(sem(name), 1)
            count[name] = count.get(name, 0) + 1
            dve.wait_ge(sem(name), count[name])

        def link(ins):
            done(ins, "dve_chain")

        def mean(n, name):
            link(dve.tensor_scalar(v(stat, 8, [1, n]), v(stat, 0, [1, n]), 1.0 / D, EPS, MUL, ADD))
            done(dve.tensor_scalar(v(stat, 8, [1, n]), v(stat, 8, [1, n]), 1.0, None, MUL), name)

        def root(n, k):
            dve.wait_ge(sem("roots"), k)
            link(dve.reciprocal(v(stat, 24, [1, n]), v(stat, 16, [1, n])))
            newton(v(stat, 8, [1, n]), v(stat, 24, [1, n]), v(stat, 32, [1, n]), link)

        def lo(c):
            dve.wait_ge(sem("w_hi_done"), c + 1)
            s = 1024 * (c % HL)
            dve.tensor_tensor(v(w_lo, s, [1, 1024]), v(raw, 1024 * (c % RAW), [1, 1024]),
                              raw32(v(w_hi, s, [1, 1024])), SUB).then_inc(sem("w_lo_done"), 1)

        dve.memset(v(stat, 48, [1, 1]), 1.0).then_inc(sem("stat_set"), 1)
        dve.wait_ge(sem("prm_in"), 16 * 8)
        done(dve.tensor_copy(v(prm, 0, [64, 2], [1, 64], p0=LDT, pn=DP),
                             v(stat, 60, [1, 2], [0, 64], p0=LDT, pn=DP)), "prm_ready")
        dve.wait_ge(sem("squares"), 1)
        mean(6, "means")
        root(6, 1)
        for n in range(NT):
            dve.tensor_scalar(v(x_sb, D * n, [1, D]), v(x_sb, D * n, [1, D]), v(stat, 24 + n, [1, 1]), None,
                              MUL).then_inc(sem("normed"), 1)
        for n in range(2):
            dve.tensor_scalar(v(mem_sb, D * n, [1, D]), v(mem_sb, D * n, [1, D]),
                              v(stat, 24 + NT + n, [1, 1]), None, MUL).then_inc(sem("normed"), 1)
        dve.wait_ge(sem("prm_turned"), 1)
        done(dve.tensor_copy(v(prt, 0, [1, 98]), pv(0, 0, [1, 98])), "prt_ready")
        dve.tensor_scalar(v(bgh, 0, [1, 24]), pcol(BG, 24), 0.5, None, MUL)
        dve.tensor_scalar(s5(0), pcol(LR, DP), -1e-4, None, ALU.min)
        link(dve.tensor_copy(s5(1), pcol(LI, DP)))
        dve.wait_ge(sem("s5_exp"), 1)
        done(dve.tensor_tensor(s5(3), s5(0), s5(2), MUL), "s5_arg")
        link(dve.tensor_tensor(s5(8), s5(1), s5(2), MUL))
        link(dve.tensor_scalar(s5(9), s5(8), math.pi / 2, None, ADD))
        two = v(s5s, DP * 8, [1, 2 * DP])
        turns, t32 = v(s5s, DP * 10, [1, 2 * DP]), v(s5s, DP * 12, [1, 2 * DP])
        link(dve.tensor_scalar(turns, two, 1 / (2 * math.pi), 12582912.0, MUL, ADD))
        link(dve.tensor_scalar(turns, turns, -12582912.0, None, ADD))
        link(dve.tensor_copy(s5(9), s5(8)))
        c1 = 6.28125
        c2 = float.fromhex("0x1.fb4p-10")
        c3 = 2 * math.pi - c1 - c2
        for c in (c1, c2, c3):
            link(dve.scalar_tensor_tensor(two, turns, -c, two, MUL, ADD))
        link(dve.tensor_scalar(s5(9), s5(9), math.pi / 2, None, ADD))
        link(dve.tensor_scalar(t32, two, 3.1415925, -3.1415925, ALU.min, ALU.max))
        done(dve.tensor_copy(two, t32), "s5_arg")

        def turn_lo(b):
            dve.wait_ge(sem("turn_hi"), b + 1)
            if b < KD:
                o = [[1, ROWS], [ROWS, GW]]
                dve.scalar_tensor_tensor(v(h_lo, SEQ * b, *o), pv(4 + b % 4, 0, [GW, ROWS], [1, GW]),
                                         pcol(GMIX + b), raw32(v(h_hi, SEQ * b, *o)), MUL, SUB).then_inc(
                                             sem("turn_lo"), 1)
            else:
                k = b - KD
                dve.scalar_tensor_tensor(v(mm_lo, MEM * k, [1, MEM]), pv(4 + b % 4, 0, [1, MEM]),
                                         pcol(GMEM + k), raw32(v(mm_hi, MEM * k, [1, MEM])), MUL,
                                         SUB).then_inc(sem("turn_lo"), 1)

        for b in range(KD):
            turn_lo(b)
        lo(0)
        lo(1)

        def disc():
            dve.wait_ge(sem("s5_sin"), 1)
            dve.wait_ge(sem("s5_exp"), 3)
            dve.memset(v(pw, 0, [1, DP]), 1.0)
            dve.memset(v(pw, PW, [1, DP]), 0.0)
            dve.tensor_tensor(v(pw, DP, [1, DP]), s5(4), s5(7), MUL)
            link(dve.tensor_tensor(v(pw, PW + DP, [1, DP]), s5(4), s5(6), MUL))
            ar, ai = v(pw, DP, [1, DP]), v(pw, PW + DP, [1, DP])
            dve.tensor_scalar(s5(10), ar, -1.0, None, ADD)
            dve.tensor_tensor(s5(12), s5(0), s5(0), MUL)
            link(dve.tensor_tensor(s5(13), s5(1), s5(1), MUL))
            dve.tensor_tensor(s5(12), s5(12), s5(13), ADD)
            dve.tensor_tensor(s5(14), s5(10), s5(0), MUL)
            dve.tensor_tensor(s5(15), ai, s5(1), MUL)
            dve.tensor_tensor(s5(16), ai, s5(0), MUL)
            link(dve.tensor_tensor(s5(17), s5(10), s5(1), MUL))
            dve.reciprocal(s5(13), s5(12))
            dve.tensor_tensor(s5(14), s5(14), s5(15), ADD)
            link(dve.tensor_tensor(s5(16), s5(16), s5(17), SUB))
            dve.tensor_tensor(s5(10), s5(14), s5(13), MUL)
            link(dve.tensor_tensor(s5(11), s5(16), s5(13), MUL))
            dve.tensor_copy(s5(18), s5(7))
            link(dve.tensor_copy(s5(19), s5(6)))
            for _ in range(3):
                square(dve, link)
            dve.sem_inc(sem("phasor"), 1)
            t = [v(junk, 256 * j, [DP, 4], [1, DP]) for j in range(2)]
            cmul(dve, link, power(2), power(1), power(1), [v(junk, 256 * j, [DP, 1], [1, DP]) for j in range(2)])
            cmul(dve, link, power(3, 2), power(1, 2), [v(pw, PW * r + DP * 2, [0, 2], [1, DP]) for r in range(2)],
                 [v(junk, 256 * j, [DP, 2], [1, DP]) for j in range(2)])
            cmul(dve, link, power(5, 4), power(1, 4), [v(pw, PW * r + DP * 4, [0, 4], [1, DP]) for r in range(2)], t)

        def bbar():
            dve.wait_ge(sem("b_in"), 32)
            b = [v(bb, 256 * r, [16, DP], [1, 16]) for r in range(2)]
            f = [v(s5s, DP * (10 + r), [1, DP], [0, 16]) for r in range(2)]
            cmul(dve, link, [v(bb, 512 + 256 * r, [16, DP], [1, 16]) for r in range(2)], b, f,
                 [v(junk, 256 * r, [16, DP], [1, 16]) for r in range(2)])
            dve.sem_inc(sem("bbar"), 1)

        HALF = DP * K5
        DW = 8 * K5

        def ph_of(d, r):
            return v(phase, HALF * r + DW * d + (K5 - 1 if d else 0), [K5, 8], [-1 if d else 1, K5])

        def rotate_in():
            dve.wait_ge(sem("phases"), 1)
            for d in range(2):
                dve.wait_ge(sem("w5"), 2 * d + 2)
                w = [pv(4 + 2 * d + r, 0, [K5, 8], [1, K5]) for r in range(2)]
                z = [v(wz, HALF * r + DW * d, [K5, 8], [1, K5]) for r in range(2)]
                t = [v(tmp, HALF * r + DW * d, [K5, 8], [1, K5]) for r in range(2)]
                dve.tensor_tensor(z[0], w[0], ph_of(d, 0), MUL)
                dve.tensor_tensor(t[0], w[1], ph_of(d, 1), MUL)
                dve.tensor_tensor(z[1], w[1], ph_of(d, 0), MUL)
                done(dve.tensor_tensor(t[1], w[0], ph_of(d, 1), MUL), "w5_took")
                dve.tensor_tensor(z[0], z[0], t[0], ADD)
                link(dve.tensor_tensor(z[1], z[1], t[1], SUB))

        def scans():
            dve.wait_ge(sem("decays"), 1)
            for d in range(2):
                for r in range(2):
                    o = HALF * r + DW * d + (DW - 1 if d else 0)
                    step = -1 if d else 1
                    ins = dve.tensor_tensor_scan(v(tmp, o, [step, DW]),
                                                 v(decay, DW * d + (DW - 1 if d else 0), [step, DW]),
                                                 v(wz, o, [step, DW]), 0.0, MUL, ADD)
            link(ins)

        def rotate_out():
            for d in range(2):
                z = [v(tmp, HALF * r + DW * d, [K5, 8], [1, K5]) for r in range(2)]
                t = [v(wz, HALF * r + DW * d, [K5, 8], [1, K5]) for r in range(2)]
                dve.tensor_tensor(t[0], z[1], ph_of(d, 1), MUL)
                link(dve.tensor_tensor(t[1], z[0], ph_of(d, 1), MUL))
                dve.tensor_tensor(z[0], z[0], ph_of(d, 0), MUL)
                link(dve.tensor_tensor(z[1], z[1], ph_of(d, 0), MUL))
                for g2 in range(2):
                    for r, op in ((0, SUB), (1, ADD)):
                        half = dict(p0=64 * g2, pn=64)
                        ins = dve.tensor_tensor(
                            v(st[r], (16 * d + g2) * (K5 + 1) + 1 - d, [2 * (K5 + 1), 8], [1, K5], **half),
                            v(tmp, HALF * r + DW * d, [K5, 8], [1, K5], **half),
                            v(wz, HALF * r + DW * d, [K5, 8], [1, K5], **half), op)
                done(ins, "states")

        def gelu_arg():
            dve.wait_ge(sem("y_in"), 16 * G5)
            for m in range(2):
                ins = dve.scalar_tensor_tensor(v(yg, SEQ * m, [1, SEQ]), v(uT, SEQ * m, [1, SEQ]),
                                               pcol(DS + m), v(yT, SEQ * m, [1, SEQ]), MUL, ADD)
            link(ins)
            y, t = v(yg, 0, [1, 2 * SEQ]), v(yT, 0, [1, 2 * SEQ])
            link(dve.tensor_tensor(t, y, y, MUL))
            link(dve.tensor_scalar(t, t, 0.044715, 1.0, MUL, ADD))
            done(dve.tensor_tensor(t, t, y, MUL), "gelu_in")

        def gelu():
            dve.wait_ge(sem("gelu_t"), 1)
            y = v(yg, 0, [1, 2 * SEQ])
            link(dve.scalar_tensor_tensor(y, v(glut, 0, [1, 2 * SEQ]), 1.0, y, ADD, MUL))
            h = v(y_hi, 0, [1, 2 * SEQ])
            link(dve.tensor_scalar(h, y, 0.5, None, MUL))
            done(dve.scalar_tensor_tensor(v(y_lo, 0, [1, 2 * SEQ]), y, 0.5, raw32(h), MUL, SUB), "y_split")

        def take(g):
            kind, m = TILES[g]
            if kind not in BY_DVE:
                return
            src = pv(g % 2, 0, [1, SEQ])
            if kind in ("xat", "nat"):
                dve.wait_ge(sem("o_hi"), m + 1 + (2 if kind == "nat" else 0))
                h_, l_ = (xa_hi, xa_lo) if kind == "xat" else (na_hi, na_lo)
                dve.tensor_tensor(v(l_, SEQ * m, [1, SEQ]), src, raw32(v(h_, SEQ * m, [1, SEQ])), SUB).then_inc(
                    sem("dve_took"), 1)
                return
            dve.wait_ge(sem("tile"), g + 1)
            if kind == "gv":
                dve.wait_ge(sem("act_took"), taken(g - 1)[1])
                i = v(glui, SEQ * m, [1, SEQ])
                dve.scalar_tensor_tensor(i, v(glut, SEQ * m, [1, SEQ]), 1.0, src, ADD, MUL).then_inc(
                    sem("dve_took"), 1)
                dve.wait_ge(sem("dve_took"), taken(g)[1])
                i = v(glui, SEQ * m, [K5, 8], [8, 8], [1, 8])
                o = [[8, 8], [1, 8], [64, 8]]
                link(dve.tensor_scalar(v(s5_hi, SEQ * m, *o), i, 0.5, None, MUL))
                dve.scalar_tensor_tensor(v(s5_lo, SEQ * m, *o), i, 0.5, raw32(v(s5_hi, SEQ * m, *o)), MUL,
                                         SUB).then_inc(sem("s5_lo"), 1)
                return
            turn = ("s5p", "xap", "nap").index(kind)
            dve.wait_ge(sem("act_took"), taken(g_of[(kind[:2] + "g", m)])[1])
            gate, acc = v(gt, SEQ * m, [1, SEQ]), v(merged, SEQ * m, [1, SEQ])
            part = acc if turn == 0 else v(prod, SEQ * (m % 2), [1, SEQ])
            dve.scalar_tensor_tensor(part, gate, 1.0, src, ADD, MUL).then_inc(sem("dve_took"), 1)
            dve.wait_ge(sem("dve_took"), taken(g)[1])
            if turn:
                dve.tensor_tensor(acc, acc, part, ADD).then_inc(sem("prod"), 1)
            else:
                dve.sem_inc(sem("prod"), 1)

        def v_take(j):
            kind, m = turned[j]
            dve.wait_ge(sem("v_turned"), j + 1)
            if kind == "mv":
                ins = dve.tensor_copy(v(vm, P * m, [XAW, 2], [1, P]), pv(6, 0, [P, 2], [1, P]))
            else:
                dve.tensor_copy(v(vw, NAW + P * m, [NAW, 3], [1, P]), pv(6, P, [P, 3], [1, P]))
                dve.tensor_copy(v(vw, P * m, [1, P], pn=64), pv(6, 0, [1, P], pn=64))
                ins = dve.tensor_copy(v(vw, 4 * NAW + P * m, [1, P], pn=64), pv(7, 0, [1, P], pn=64))
            ins.then_inc(sem("v_took"), 1)

        def smax(u):
            na, h, i = unit(u)
            dve.wait_ge(sem("qk"), u + 1)
            mx = v(soft, 8 * (u % 8), [1, 1])
            if na:
                _, n, off = window(i)
                if u >= XAH * NT + 3:
                    dve.wait_ge(sem("exp"), u - 2)
                ins = dve.tensor_tensor_reduce(v(ssb, 256 * (u % 3), [1, n]), pv(2 + u % 2, 0, [1, n]),
                                               v(ez, 256 * h + off, [1, n]), 1.0, -3e38, ADD, ALU.max, mx)
            else:
                ins = dve.tensor_reduce(mx, pv(2 + u % 2, 0, [1, MEM]), AX.X, ALU.max)
            link(ins)
            dve.tensor_scalar(v(soft, 8 * (u % 8) + 1, [1, 1]), mx, -1.0, None, MUL).then_inc(sem("smax"), 1)

        def take_o(u):
            na, h, i = unit(u)
            dve.wait_ge(sem("pv"), u + 1)
            link(dve.reciprocal(v(soft, 8 * (u % 8) + 3, [1, 1]), v(soft, 8 * (u % 8) + 2, [1, 1])))
            dst = v(onat, 512 * i + HD * h, [1, HD]) if na else v(onx, 256 * i + HD * h, [1, HD])
            dve.tensor_scalar(dst, pv(6 + u % 2, 0, [1, HD]), v(soft, 8 * (u % 8) + 3, [1, 1]), None,
                              MUL).then_inc(sem("o_took"), 1)

        def slot(s):
            if s < UNITS:
                smax(s)
            if 0 <= s - 4 < UNITS:
                take_o(s - 4)

        def merged_lo(k):
            dve.wait_ge(sem("m_hi"), k + 1)
            o = [[1, GW], [GW, ROWS]]
            dve.scalar_tensor_tensor(v(m_lo, SEQ * k, *o), v(merged, SEQ * k, [ROWS, GW], [1, ROWS]), 0.5,
                                     raw32(v(m_hi, SEQ * k, *o)), MUL, SUB).then_inc(sem("m_lo"), 1)

        g = 0
        s = 0
        v_at = {C_QX: 0, C_QX + 1: 1, C_V + 1: 2, C_V + 2: 3, C_V + 3: 4}
        for c in range(C_OUT):
            if c in SLOTS:
                slot(s)
                s += 1
            if c in v_at:
                v_take(v_at[c])
            if c == C_GLU:
                v_take(5)
            for kind, _ in tiles_of(c):
                if kind[2:] == "g":
                    for _ in range(SLOTS.get(c, 1) - 1):
                        slot(s)
                        s += 1
                take(g)
                g += 1
            lo(c + 2)
            for k in range(2 * (c - C_NAP) - 2, 2 * (c - C_NAP)):
                if k >= 0:
                    merged_lo(k)
            if c < 2:
                for b in range(KD + 4 * c, KD + 4 * c + 4):
                    turn_lo(b)
            if c == 0:
                disc()
            if c == 1:
                bbar()
            if c in (6, 7):
                powers_of_b(dve, link, 0, c - 6, junk)
            if c == 7:
                dve.sem_inc(sem("ba_ready"), 1)
            if c == 9:
                rotate_in()
            if c == 10:
                scans()
            if c == 11:
                rotate_out()
            if c == 16:
                gelu_arg()
            if c == 18:
                gelu()
        for k in range(6, KD):
            merged_lo(k)
        for c in range(C_OUT + 2, NCH):
            lo(c)
        dve.wait_ge(sem("x_again"), 16)
        for half in range(2):
            dve.wait_ge(sem("out_k"), 4 * half + 4)
            for n in range(NT):
                xs = v(x_sb, D * n + 512 * half, [1, 512])
                ins = dve.tensor_tensor(xs, pv(OUT_BANK[half][n], 0, [1, 512]), xs, ADD)
                if half:
                    ins.then_inc(sem("x2"), 1)
        dve.wait_ge(sem("squares"), 2)
        mean(NT, "means")
        root(NT, 2)
        dve.wait_ge(sem("gf_in"), 16)
        for n in range(NT):
            dve.scalar_tensor_tensor(v(h2, D * n, [1, D]), v(x_sb, D * n, [1, D]), v(stat, 24 + n, [1, 1]),
                                     v(gffb, 0, [1, D]), MUL, MUL).then_inc(sem("h2"), 1)

        lg = v(rt, 0, [20, NT], [1, 20])
        dve.wait_ge(sem("logits"), 1)
        dve.wait_ge(sem("lb_in"), 32)
        link(dve.tensor_tensor(lg, pv(5, 0, [20, NT], [1, 20]), v(lbias, 0, [0, NT], [1, 20]), ADD))
        for j in range(4):
            n = j + 1
            ins = dve.tensor_tensor(v(rt, 80 + j, [16, 20], [4, n]), v(rt, j, [4, 20], [0, n]),
                                    v(rt, 0, [4, 20], [1, n]), ALU.is_gt)
            if n < 4:
                ins = dve.tensor_tensor(v(rt, 80 + 4 * n + j, [16, 20], [4, 4 - n]), v(rt, j, [4, 20], [0, 4 - n]),
                                        v(rt, n, [4, 20], [1, 4 - n]), ALU.is_ge)
        link(ins)
        link(dve.tensor_reduce(v(rt, 400, [1, 80]), v(rt, 80, [4, 80], [1, 4]), AX.X, ADD))
        for j in range(2):
            ins = dve.tensor_scalar(v(rt, 480 + 80 * j, [1, 80]), v(rt, 400, [1, 80]), float(j), None, ALU.is_equal)
        link(ins)
        m = [v(rt, 640 + 64 * j, [1, 64]) for j in range(2)]
        for j in range(2):
            ins = dve.tensor_tensor(v(rt, 640 + 64 * j, [16, NT], [4, 4], [1, 4]),
                                    v(rt, 480 + 80 * j + 4, [20, NT], [4, 4], [1, 4]),
                                    v(rt, 480, [20, NT], [1, 4], [0, 4]), MUL)
        link(ins)
        done(dve.tensor_tensor(v(selb, 0, [1, 64]), m[0], m[1], ADD), "chosen")
        for j in range(2):
            ins = dve.tensor_tensor(v(rt, 768 + 64 * j, [16, NT], [1, 16]), v(rt, 640 + 64 * j, [16, NT], [1, 16]),
                                    v(rt, 4, [20, NT], [1, 16]), MUL)
        ins2 = dve.tensor_reduce(v(rt, 908, [1, NT]), v(rt, 0, [20, NT], [1, 4]), AX.X, ALU.max)
        link(ins2)
        link(dve.tensor_reduce(v(rt, 896, [1, 8]), v(rt, 768, [16, 8], [1, 16]), AX.X, ADD))
        dve.tensor_tensor(v(rt, 960, [4, NT], [1, 4]), v(rt, 0, [20, NT], [1, 4]), v(rt, 908, [1, NT], [0, 4]), SUB)
        done(dve.tensor_tensor(v(rt, 976, [1, NT]), v(rt, 900, [1, NT]), v(rt, 896, [1, NT]), SUB), "route_arg")
        dve.wait_ge(sem("places"), 1)
        dve.wait_ge(sem("iotas"), 1)
        link(dve.scalar_tensor_tensor(v(rt, 768, [16, NT], [1, 16]), pv(6, 0, [16, NT], [1, 16]), float(NE),
                                      v(rt, 1040, [0, NT], [1, 16]), MUL, ADD))
        for j in range(2):
            ins = dve.tensor_tensor(v(rt, 480 + 64 * j, [1, 64]), m[j], v(rt, 768, [1, 64]), MUL)
        link(ins)
        link(dve.tensor_reduce(v(rt, 1000, [1, 8]), v(rt, 480, [16, 8], [1, 16]), AX.X, ADD))
        done(dve.tensor_copy(v(rowi, 0, [1, 8]), v(rt, 1000, [1, 8])), "rows")
        link(dve.tensor_reduce(v(rt, 1010, [1, 1]), pv(6, 64, [1, 16]), AX.X, ALU.max))
        done(dve.tensor_scalar(v(flag, 0, [1, 1]), v(rt, 1010, [1, 1]), float(CAP), None, ALU.is_gt), "flag")
        dve.wait_ge(sem("route_exp"), 1)
        dve.tensor_reduce(v(rt, 1012, [1, NT]), v(rt, 960, [4, NT], [1, 4]), AX.X, ADD)
        link(dve.tensor_scalar(v(rt, 1016, [1, NT]), v(rt, 976, [1, NT]), 1.0, None, ADD))
        link(dve.tensor_tensor(v(rt, 1012, [1, NT]), v(rt, 1012, [1, NT]), v(rt, 1016, [1, NT]), MUL))
        link(dve.reciprocal(v(wts, 0, [1, NT]), v(rt, 1012, [1, NT])))
        link(dve.tensor_tensor(v(wts, 4, [1, NT]), v(wts, 0, [1, NT]), v(rt, 976, [1, NT]), MUL))

        def unit_lo(n, j, dst):
            dve.wait_ge(sem("e_hi_done"), n + 1)
            dve.tensor_tensor(v(e_lo[dst], 0, [1, 2048]), v(eraw, 2048 * j, [1, 2048]),
                              raw32(v(e_hi[dst], 0, [1, 2048])), SUB).then_inc(sem("e_lo_done"), 1)

        def xt_rest(e):
            for j in range(2):
                dve.wait_ge(sem("xt_hi"), 2 * e + j + 1)
                dve.tensor_tensor(v(xt_lo, 512 * j, [1, 512]), pv(4 + j, 0, [1, 512]),
                                  raw32(v(xt_hi, 512 * j, [1, 512])), SUB).then_inc(sem("xt_lo"), 1)

        def step(e, odd, stored):
            peeled = isinstance(e, int)
            if not peeled or e >= 1:
                dve.wait_ge(sem("at_hi"), e)
                dve.tensor_tensor(v(at_lo, 0, [1, 256]), pv(6, 0, [1, 256]), raw32(v(at_hi, 0, [1, 256])),
                                  SUB).then_inc(sem("at_lo"), 1)
            if not peeled or e < 15:
                unit_lo(3 * e + 2, 5 if odd else 2, 2)
            if not peeled or e < 16:
                b = 1 if odd else 0
                dve.wait_ge(sem("tanh"), e + 1)
                dve.scalar_tensor_tensor(v(act_s, 0, [1, FF]), v(act_t, 0, [1, FF]), 1.0, pv(b, 0, [1, FF]),
                                         ADD, MUL).then_inc(sem("act_s"), 1)
                dve.wait_ge(sem("act_s"), e + 1)
                dve.scalar_tensor_tensor(v(act_a, 0, [1, FF]), v(act_s, 0, [1, FF]), 0.5, pv(b, FF, [1, FF]),
                                         MUL, MUL).then_inc(sem("act_a"), 1)
            if not peeled or e < 15:
                xt_rest(e + 1)
                unit_lo(3 * e + 3, 0 if odd else 3, 0)
                unit_lo(3 * e + 4, 1 if odd else 4, 1)
            elif e == 15:
                unit_lo(47, 5, 2)
            if not peeled or e >= 1:
                dve.wait_ge(sem("e_used"), 48 if peeled and e == 16 else 3 * e + 2)
                if stored is not None:
                    dve.wait_ge(sem(f"y_st{0 if odd else 1}"), stored)
                dve.tensor_copy(v(ysb, 512 + (0 if odd else D), [1, 512]), pv(3, 0, [1, 512])).then_inc(
                    sem("y_d"), 1)

        unit_lo(0, 0, 0)
        unit_lo(1, 1, 1)
        xt_rest(0)
        for e in range(3):
            step(e, e % 2 == 1, None)
        with dve.Fori(0, 6) as i:
            step(2 * i + 3, True, 16 * i + 16)
            step(2 * i + 4, False, 16 * i + 16)
        step(15, True, 16 * 7)
        step(16, False, 16 * 7)

        with dve.If(needed(dve)):
            with dve.Fori(0, 3) as j:
                with dve.Fori(0, NE) as e:
                    it = NE * j + e + 1
                    dve.wait_ge(sem("ov_tanh"), it)
                    dve.scalar_tensor_tensor(v(act_s, 0, [1, FF]), v(act_t, 0, [1, FF]), 1.0, pv(0, 0, [1, FF]),
                                             ADD, MUL).then_inc(sem("ov_s"), 1)
                    dve.wait_ge(sem("ov_s"), it)
                    dve.scalar_tensor_tensor(v(act_a, 0, [1, FF]), v(act_s, 0, [1, FF]), 0.5,
                                             pv(0, FF, [1, FF]), MUL, MUL).then_inc(sem("ov_a"), 1)

        for n in range(NT):
            xs = v(x_sb, D * n, [1, D])
            dve.wait_ge(sem(f"yg{n}"), 32)
            link(dve.scalar_tensor_tensor(xs, v(y0, D * n, [1, D]), v(wts, n, [1, 1]), xs, MUL, ADD))
            dve.scalar_tensor_tensor(xs, v(y1, D * n, [1, D]), v(wts, 4 + n, [1, 1]), xs, MUL, ADD).then_inc(
                sem("x2"), 1)
        dve.wait_ge(sem("squares"), 3)
        mean(NT, "means")
        root(NT, 3)
        dve.wait_ge(sem("gfin_in"), 16)
        for n in range(NT):
            xs = v(x_sb, D * n, [1, D])
            dve.scalar_tensor_tensor(xs, xs, v(stat, 24 + n, [1, 1]), v(gfin, 0, [1, D]), MUL, MUL).then_inc(
                sem("out_ready"), 1)

    @block.tensor
    def _(pe):
        def split(dst, w, x, first, last):
            pe.matmul(dst, w[0], x[0], start=first, stop=False)
            pe.matmul(dst, w[0], x[1], start=False, stop=False)
            return pe.matmul(dst, w[1], x[0], start=False, stop=last)

        pe.wait_ge(sem("consts"), 1)
        pe.wait_ge(sem("prm_ready"), 1)
        pe.transpose(pv(0, 0, [1, 98]), v(prm, 0, [1, P], pn=98), v(ident, 0, [1, 98], pn=98)).then_inc(
            sem("prm_turned"), 1)
        pe.wait_ge(sem("c_in"), 64)
        for ri in range(2):
            for h in range(4):
                ins = pe.transpose(pv(2 + ri, P * h, [1, P]), v(cn, 512 * ri + P * h, [1, P]), v(ident, 0, [1, P]))
            ins.then_inc(sem("c_turned"), 1)

        def turn(b):
            pe.wait_ge(sem("normed"), NT if b < KD else NT + 2)
            if b >= 4:
                pe.wait_ge(sem("turn_lo"), b - 3)
            for n in range(NT if b < KD else 2):
                src = v(x_sb, D * n + P * b, [1, P]) if b < KD else v(mem_sb, D * n + P * (b - KD), [1, P])
                ins = pe.transpose(pv(4 + b % 4, P * n, [1, P]), src, v(ident, 0, [1, P]))
            ins.then_inc(sem("turned"), 1)

        def product(g, c, s=0):
            kind, m = TILES[g]
            if g >= 2:
                wait_taken(pe, g - 2)
            w0 = 1024 * (c % HL)
            ws = (w_hi, w_lo)
            if kind in ("xat", "nat"):
                src, step = (onx, 256) if kind == "xat" else (onat, 512)
                if m == 0:
                    pe.wait_ge(sem("o_took"), XAH * NT if kind == "xat" else UNITS)
                for n in range(NT):
                    ins = pe.transpose(pv(g % 2, P * n, [1, P]), v(src, step * n + P * m, [1, P]),
                                       v(ident, 0, [1, P]))
                ins.then_inc(sem("tile"), 1)
                return
            xs, n, wk, wcol = (h_hi, h_lo), SEQ, P, 0
            ks = KD
            if kind in ("mk", "mv"):
                xs, n = (mm_hi, mm_lo), MEM
            elif kind in ("gt", "gv"):
                xs, ks, wk, wcol = (y_hi, y_lo), 2, 512, P * (m + (2 if kind == "gt" else 0))
            elif kind in ("s5p", "xap"):
                if kind == "xap" and m == 0:
                    wait_taken(pe, g_of["xat", 1])
                xs, ks, wk, wcol = ((s5_hi, s5_lo) if kind == "s5p" else (xa_hi, xa_lo)), 2, 512, P * (m % 4)
            elif kind == "nap":
                if m == 0:
                    wait_taken(pe, g_of["nat", 3])
                xs, ks, wk, wcol = (na_hi, na_lo), 4, 256, P * (m % 2)
            for k in range(ks):
                n_slots = SLOTS.get(c, 0)
                if n_slots == 2 and k == 4 or n_slots == 3 and k in (3, 6):
                    slot(s)
                    s += 1
                ins = split(pv(g % 2, 0, [1, n]), [v(w, w0 + wk * k + wcol, [1, P]) for w in ws],
                            [v(x, n * k, [1, n]) for x in xs], k == 0, k == ks - 1)
            ins.then_inc(sem("tile"), 1)

        def s5_matrices():
            pe.wait_ge(sem("v_took"), 2)
            pe.wait_ge(sem("ba_ready"), 1)
            pe.wait_ge(sem("ba_back"), 1)
            for q in range(8):
                if q >= 4:
                    pe.wait_ge(sem("bat_took"), q - 3)
                for j in range(4):
                    ins = pe.transpose(pv(4 + q % 4, P * j, [1, P]), v(ba, 512 * q + P * j, [1, P]),
                                       v(ident, 0, [1, P]))
                ins.then_inc(sem("ba_turned"), 1)
            pe.wait_ge(sem("ct_ready"), 2)
            for dp in range(DP):
                for ri in range(2):
                    ins = pe.matmul(pv(2, 32 * dp, [1, 32]), v(ba, 2048 * ri + P * dp, [1, P]),
                                    v(ctb, 512 * ri + 32 * dp, [1, 32]), start=ri == 0, stop=ri == 1)
            ins.then_inc(sem("lags"), 1)
            pe.wait_ge(sem("lags_took"), 1)
            pe.wait_ge(sem("bat_took"), 8)
            for t in range(T5):
                for d, o in ((0, 112 + 16 * (7 - t)), (1, 112 - 16 * t)):
                    ins = pe.matmul(pv(4 + t // 2, 256 * (t % 2), [1, 256]), v(wide, o, [1, P]),
                                    v(stk, 256 * d, [1, 256]), start=d == 0, stop=d == 1)
                if t % 2:
                    ins.then_inc(sem("shifted"), 1)

        def s5_inputs():
            pe.wait_ge(sem("mg_took"), 4)
            pe.wait_ge(sem("u_in"), 16 * T5)
            for d in range(2):
                for ri in range(2):
                    for p in range(8):
                        for g2 in range(2):
                            ins = pe.matmul(pv(4 + 2 * d + ri, K5 * p, [1, K5], p0=64 * g2, pn=64),
                                            v(bat, 2048 * ri + P * (8 * d + p) + 64 * g2, [1, 64]),
                                            v(upk, K5 * (2 * p + g2), [1, K5]), start=True, stop=True)
                    ins.then_inc(sem("w5"), 1)

        def s5_outputs():
            pe.wait_ge(sem("states"), 2)
            pe.wait_ge(sem("ca_ready"), 1)
            for p in range(8):
                b, o = 2 + p // 4, P * (p % 4)
                for d in range(2):
                    for r in range(2):
                        pe.matmul(pv(b, o, [K5, 2], [1, K5]), v(ca, 2048 * r + P * (8 * d + p), [1, P]),
                                  v(st[r], (8 * d + p) * 2 * (K5 + 1) + d, [K5 + 1, 2], [1, K5]),
                                  start=d == 0 and r == 0, stop=False)
                for g2 in range(2):
                    ins = pe.matmul(pv(b, o + K5 * g2, [1, K5]), v(mg, P * (2 * p + g2), [1, P]),
                                    v(upk, K5 * (2 * p + g2), [1, K5]), start=False, stop=g2 == 1)
                if p % 4 == 3:
                    ins.then_inc(sem("s5_y"), 1)

        def turn_values(j):
            kind, m = turned[j]
            pe.wait_ge(sem("act_took"), taken(g_of[turned[j]])[1])
            if j:
                pe.wait_ge(sem("v_took"), j)
            if kind == "mv":
                for w in range(2):
                    ins = pe.transpose(pv(6, P * w, [1, P]), v(vt, SEQ * (j % 2) + P * w, [1, P]),
                                       v(ident, 0, [1, P]))
            else:
                for w in range(5):
                    a0, a1 = max(0, P * w - 64), min(SEQ, P * w + 64)
                    ins = pe.transpose(pv(7 if w == 4 else 6, 0 if w == 4 else P * w, [1, P], pn=a1 - a0),
                                       v(vt, SEQ * (j % 2) + a0, [1, a1 - a0]), v(ident, 0, [1, P]))
            ins.then_inc(sem("v_turned"), 1)

        def scores(u):
            na, h, i = unit(u)
            if u >= 2:
                pe.wait_ge(sem("exp"), u - 1)
            lo64, pn = 64 * (h % 2), 64
            if na:
                if u == XAH * NT:
                    pe.wait_ge(sem("masks"), 1)
                w0, n, off = window(i)
                kind = 0 if i == 0 else 2 if i == NT - 1 else 1
                dst = pv(2 + u % 2, 0, [1, n])
                pe.matmul(dst, v(identb, 0, [1, P]), v(maskb, 256 * kind + off, [1, n]), start=True, stop=False)
                pe.matmul(dst, v(qT, SEQ * (h // 2) + P * i, [1, P], p0=lo64, pn=pn),
                          v(kT, SEQ * (h // 2) + w0, [1, n], p0=lo64, pn=pn), start=False, stop=True).then_inc(
                              sem("qk"), 1)
            else:
                pe.matmul(pv(2 + u % 2, 0, [1, MEM]), v(qxT, SEQ * (h // 2) + P * i, [1, P], p0=lo64, pn=pn),
                          v(kmT, MEM * (h // 2), [1, MEM], p0=lo64, pn=pn), start=True, stop=True).then_inc(
                              sem("qk"), 1)

        def chunks_of(u):
            na, h, i = unit(u)
            return key_chunks(i) if na else [(0, P, 0), (1, P, P)]

        def turn_p(u):
            pe.wait_ge(sem("exp"), u + 1)
            if u >= 2:
                pe.wait_ge(sem("p_taken"), u - 1)
            for k, (_, n, a0) in enumerate(chunks_of(u)):
                ins = pe.transpose(pv(4 + u % 2, P * k, [1, P], pn=n), v(pr, 256 * (u % 3) + a0, [1, n]),
                                   v(ident, 0, [1, P]))
            ins.then_inc(sem("p_turned"), 1)

        def weighted(u):
            na, h, i = unit(u)
            pe.wait_ge(sem("p_taken"), u + 1)
            if u >= 2:
                pe.wait_ge(sem("o_took"), u - 1)
            for k, (w, n, _) in enumerate(chunks_of(u)):
                vals = v(vw, NAW * w + HD * h, [1, HD], pn=n) if na else v(vm, XAW * w + HD * h, [1, HD])
                ins = pe.matmul(pv(6 + u % 2, 0, [1, HD]), v(pts, 256 * (u % 2) + P * k, [1, P], pn=n), vals,
                                start=k == 0, stop=k == 1)
            ins.then_inc(sem("pv"), 1)

        def slot(s):
            if s < UNITS:
                scores(s)
            if 0 <= s - 2 < UNITS:
                turn_p(s - 2)
            if 0 <= s - 4 < UNITS:
                weighted(s - 4)

        for b in range(KD):
            turn(b)
        pe.wait_ge(sem("turn_lo"), KD)
        g = s = 0
        for c in range(C_OUT):
            if c == C_MEMK:
                pe.wait_ge(sem("turn_lo"), 2 * KD)
            if c == C_GLU:
                turn_values(5)
                pe.wait_ge(sem("y_split"), 1)
            if c == C_S5P:
                pe.wait_ge(sem("s5_lo"), 2)
            if c == C_S5G:
                pe.wait_ge(sem("v_took"), 6)
            if c in SLOTS:
                slot(s)
                s += 1
            pe.wait_ge(sem("w_lo_done"), c + 1)
            for _ in tiles_of(c):
                product(g, c, s)
                g += 1
            s += max(0, SLOTS.get(c, 0) - 1)
            if c in (C_MEMV + 1, C_QX):
                turn_values(c - C_MEMV - 1)
            if C_V < c < C_GLU:
                turn_values(c - C_V + 1)
            if c == 3:
                pe.wait_ge(sem("rpb_in"), 16 * 16)
                for q in range(4):
                    if q >= 2:
                        pe.wait_ge(sem("bias_ready"), q - 1)
                    pe.matmul(pv(4 + q % 2, 0, [1, 512]), v(flip, 0, [1, P]), v(ezraw, 512 * q, [1, 512]),
                              start=True, stop=True).then_inc(sem("flipped"), 1)
            if c < 2:
                for b in range(KD + 4 * c, KD + 4 * c + 4):
                    turn(b)
            if c == 8:
                pe.wait_ge(sem("bias_ready"), 4)
                s5_matrices()
            if c == 9:
                s5_inputs()
            if c == 14:
                s5_outputs()

        for c in range(C_OUT, NCH):
            half, kp = divmod(c - C_OUT, 4)
            pe.wait_ge(sem("w_lo_done"), c + 1)
            if half and kp == 0:
                wait_taken(pe, len(TILES) - 1)
            for kk in range(2):
                k = 2 * kp + kk
                pe.wait_ge(sem("m_lo"), k + 1)
                for n in range(NT):
                    w0 = 1024 * (c % HL) + 512 * kk
                    ins = split(pv(OUT_BANK[half][n], 0, [1, 512]),
                                [v(x, SEQ * k + P * n, [1, P]) for x in (m_hi, m_lo)],
                                [v(w, w0, [1, 512]) for w in (w_hi, w_lo)], k == 0, k == KD - 1)
            ins.then_inc(sem("out_k"), 1)

        pe.wait_ge(sem("x2"), NT)
        pe.wait_ge(sem("h2"), NT)
        for b in range(KD):
            if b >= 4:
                pe.wait_ge(sem("h2_took"), b - 3)
            for n in range(NT):
                ins = pe.transpose(pv(b % 4, P * n, [1, P]), v(h2, D * n + P * b, [1, P]), v(ident, 0, [1, P]))
            ins.then_inc(sem("h2_turned"), 1)
        pe.wait_ge(sem("h2_took"), KD)
        pe.wait_ge(sem("wcf_in"), 32)
        for n in range(NT):
            for k in range(KD):
                ins = pe.matmul(pv(5, 20 * n, [1, 20]), v(h2T, SEQ * k + P * n, [1, P]), v(wcf, 20 * k, [1, 20]),
                                start=k == 0, stop=k == KD - 1)
        ins.then_inc(sem("logits"), 1)
        pe.wait_ge(sem("chosen"), 1)
        pe.matmul(pv(6, 0, [1, 64]), v(upper, 0, [1, P]), v(selb, 0, [1, 64]), start=True, stop=False)
        for q in range(1, NT):
            pe.matmul(pv(6, 16 * q, [1, 64 - 16 * q]), v(onesb, 0, [1, P]), v(selb, 0, [1, 64 - 16 * q]),
                      start=False, stop=q == NT - 1)
        for n in range(NT):
            ins = pe.matmul(pv(6, 64, [1, 16]), v(onesb, 0, [1, P]), v(selb, 16 * n, [1, 16]),
                            start=n == 0, stop=n == NT - 1)
        ins.then_inc(sem("places"), 1)

        def tokens(e, odd, gathered):
            pe.wait_ge(sem(f"xg{1 if odd else 0}"), gathered)
            if not (isinstance(e, int) and e == 0):
                pe.wait_ge(sem("xt_lo"), 2 * e)
            for j in range(2):
                for k in range(4):
                    ins = pe.transpose(pv(4 + j, P * k, [1, P]), v(xg, (D if odd else 0) + 512 * j + P * k, [1, P]),
                                       v(ident, 0, [1, P]))
                ins.then_inc(sem("xt"), 1)

        def gate_up(e, n, half, s3, odd):
            pe.wait_ge(sem("e_lo_done"), n + 1)
            for k in range(4):
                kk = 4 * half + k
                ins = split(pv(1 if odd else 0, 0, [1, 512]), [v(x, P * kk, [1, P]) for x in (xt_hi, xt_lo)],
                            [v(w[s3], 512 * k, [1, 512]) for w in (e_hi, e_lo)], kk == 0, kk == KD - 1)
            ins.then_inc(sem("e_used"), 1)

        def step(e, odd, gathered):
            peeled = isinstance(e, int)
            first = peeled and e == 0
            if not peeled or e < 16:
                if first:
                    pe.wait_ge(sem("xt_lo"), 2)
                else:
                    pe.wait_ge(sem("xt_lo"), 2 * e + 2)
                    if not peeled or e >= 2:
                        pe.wait_ge(sem("act_a"), e - 1)
                gate_up(e, 0 if first else 3 * e - 1, 0, 0 if first else 2, odd)
            if not first:
                pe.wait_ge(sem("act_a"), e)
                if not peeled or e >= 2:
                    pe.wait_ge(sem("at_lo"), e - 1)
                for k in range(2):
                    ins = pe.transpose(pv(6, P * k, [1, P]), v(act_a, P * k, [1, P]), v(ident, 0, [1, P]))
                ins.then_inc(sem("at"), 1)
            if not peeled or e < 16:
                gate_up(e, 1 if first else 3 * e, 1, 1 if first else 0, odd)
            if not peeled or e < 15:
                tokens(e + 1, not odd, gathered)
            if not first:
                last = peeled and e == 16
                pe.wait_ge(sem("e_lo_done"), 48 if last else 3 * e + 2)
                pe.wait_ge(sem("at_lo"), e)
                if not peeled or e >= 2:
                    pe.wait_ge(sem("y_a"), e - 1)
                    pe.wait_ge(sem("y_d"), e - 1)
                s3 = 2 if last else 1
                for n in range(2):
                    for k in range(2):
                        ins = split(pv(2 + n, 0, [1, 512]), [v(x, P * k, [1, P]) for x in (at_hi, at_lo)],
                                    [v(w[s3], D * k + 512 * n, [1, 512]) for w in (e_hi, e_lo)], k == 0, k == 1)
                ins.then_inc(sem("e_used"), 1)

        pe.wait_ge(sem("rows"), 1)
        tokens(0, False, 16)
        step(0, False, 16)
        step(1, True, 32)
        step(2, False, 32)
        with pe.Fori(0, 6) as i:
            step(2 * i + 3, True, 16 * i + 48)
            step(2 * i + 4, False, 16 * i + 48)
        step(15, True, None)
        step(16, False, None)

        with pe.If(needed(pe)):
            with pe.Fori(0, 3) as j:
                with pe.Fori(0, NE) as e:
                    it = NE * j + e + 1
                    pe.wait_ge(sem("ov_g"), 16 * it)
                    for k in range(KD):
                        ins = pe.transpose(pv(4 + k // 4, P * (k % 4), [1, P]), v(xg, P * k, [1, P]),
                                           v(ident, 0, [1, P]))
                    ins.then_inc(sem("ov_xt"), 1)
                    pe.wait_ge(sem("ov_x"), it)
                    pe.wait_ge(sem("ov_in"), 96 * it)
                    for k in range(KD):
                        ins = pe.matmul(pv(0, 0, [1, 512]), v(xtf, P * k, [1, P]), v(eraw, 512 * k, [1, 512]),
                                        start=k == 0, stop=k == KD - 1)
                    ins.then_inc(sem("ov_gu"), 1)
                    pe.wait_ge(sem("ov_a"), it)
                    for k in range(2):
                        ins = pe.transpose(pv(6, P * k, [1, P]), v(act_a, P * k, [1, P]), v(ident, 0, [1, P]))
                    ins.then_inc(sem("ov_at"), 1)
                    pe.wait_ge(sem("ov_ac"), it)
                    for n in range(2):
                        for k in range(2):
                            ins = pe.matmul(pv(2 + n, 0, [1, 512]), v(atf, P * k, [1, P]),
                                            v(eraw, 4096 + D * k + 512 * n, [1, 512]), start=k == 0, stop=k == 1)
                    ins.then_inc(sem("ov_down"), 1)
                    pe.wait_ge(sem("ov_y"), it)

    @block.gpsimd
    def _(pool):
        count = [0]

        def link(ins):
            ins.then_inc(sem("pool_chain"), 1)
            count[0] += 1
            pool.wait_ge(sem("pool_chain"), count[0])

        def one_where(t, cols, base_):
            return pool.affine_select(out=v(t, 0, [1, cols]), in_=v(t, 0, [1, cols]), compare_op=ALU.not_equal,
                                      fill=1.0, base=base_, pattern=[[-1, cols]], channel_multiplier=1)

        pool.memset(v(ident, 0, [1, P]), 0.0)
        pool.memset(v(identb, 0, [1, P]), 0.0)
        pool.memset(v(wide, 0, [1, 352]), 0.0)
        pool.memset(v(ctb, 0, [1, 2 * DP * 32]), 0.0)
        pool.memset(v(flip, 0, [1, P]), 0.0)
        pool.memset(v(maskb, 0, [1, 768]), 0.0)
        pool.memset(v(upper, 0, [1, P]), 1.0)
        pool.memset(v(onesb, 0, [1, P]), 1.0)
        pool.memset(v(zi, 0, [1, 64]), 0)
        link(pool.memset(v(ezraw, 0, [1, NAH * 256]), 0.0))
        one_where(ident, P, 0)
        one_where(identb, P, 0)
        one_where(wide, 352, 112)
        pool.affine_select(out=v(flip, 0, [1, P]), in_=v(flip, 0, [1, P]), compare_op=ALU.not_equal, fill=1.0,
                           base=1 - P, pattern=[[1, P]], channel_multiplier=1).then_inc(sem("consts"), 1)
        pool.dma_start(tok_dram.rearrange("(p n) o -> p (n o)", p=P), v(zi, 0, [1, 64])).then_inc(sem("tok_zero"), 16)
        rpb = a["na_rpb"][0]
        for q in range(16):
            m0, m1 = max(0, q - 7), min(31, q + 23)
            n = 7 * RPB_C + m1 - m0 + 1
            src = bass.AP(tensor=rpb.tensor, offset=rpb.offset + m0 - q + 7,
                          ap=[[RPB_C, 8], [RPB_R * RPB_C, NAH], [1, n]])
            pool.dma_start(v(ezraw, m0, [256, NAH], [1, n], p0=120 - 8 * q, pn=8), src).then_inc(sem("rpb_in"), 16)
        link(pool.affine_select(out=v(upper, 0, [1, P]), in_=v(upper, 0, [1, P]), compare_op=ALU.is_gt, fill=0.0,
                                base=0, pattern=[[1, P]], channel_multiplier=-1))

        def mask(kind, p0, pn, step, cm, base_):
            t = v(maskb, 256 * kind, [8, 32], [1, 8], p0=p0, pn=pn)
            link(pool.affine_select(out=t, in_=t, compare_op=ALU.is_ge, fill=-1e30, base=base_ + cm * p0,
                                    pattern=[[step, 32], [0, 8]], channel_multiplier=cm))

        for kind, p0, pn in ((0, 64, 64), (1, 0, P), (2, 0, 64)):
            mask(kind, p0, pn, 8, -1, 7)
            mask(kind, p0, pn, -8, 1, 120)
        for kind, p0, pn in ((0, 0, 64), (2, 64, 64)):
            mask(kind, p0, pn, 8, 0, -64)
            mask(kind, p0, pn, -8, 0, 184)
        pool.sem_inc(sem("masks"), 1)

        pool.wait_ge(sem("bbar"), 1)
        for h in range(2):
            powers_of_b(pool, link, 1, h, pjunk)
        pool.sem_inc(sem("ba_back"), 1)
        pool.wait_ge(sem("phasor"), 1)
        ph = DP * K5
        for r in range(2):
            ins = pool.memset(v(phase, ph * r, [K5, DP], [1, 1]), 1.0 - r)
        link(ins)
        n = 1
        while n < K5:
            cmul(pool, link, [v(phase, ph * r + n, [K5, DP], [1, n]) for r in range(2)],
                 [v(phase, ph * r, [K5, DP], [1, n]) for r in range(2)],
                 [v(s5s, DP * (18 + r), [1, DP], [0, n]) for r in range(2)],
                 [v(pjunk, 512 * r, [n, DP], [1, n]) for r in range(2)])
            n *= 2
            if n < K5:
                square(pool, link)
        pool.sem_inc(sem("phases"), 1)
        pool.wait_ge(sem("ba_ready"), 1)
        pool.wait_ge(sem("lags"), 1)
        pool.tensor_copy(v(decay, 0, [K5, DP], [1, K5]), v(s5s, DP * 5, [1, DP], [0, K5]))
        pool.memset(v(st[0], 0, [1, 2 * DP * (K5 + 1)]), 0.0)
        link(pool.memset(v(st[1], 0, [1, 2 * DP * (K5 + 1)]), 0.0))
        pool.memset(v(decay, 0, [K5, 8]), 0.0)
        link(pool.memset(v(decay, 8 * K5 + K5 - 1, [K5, 8]), 0.0))
        pool.sem_inc(sem("decays"), 1)

        pool.wait_ge(sem("bias_ready"), 4)

        pool.wait_ge(sem("ct_ready"), 2)
        pool.wait_ge(sem("w5"), 4)
        for d in range(2):
            o = [v(ca, 2048 * r + 1024 * d, [P, 8], [16, 8], [1, 16]) for r in range(2)]
            t = [v(pt5, 1024 * r, [P, 8], [16, 8], [1, 16]) for r in range(2)]
            x = [v(pw, PW * r + (DP if d == 0 else 8 * DP) + 8 * d, [1, 8], [DP if d == 0 else -DP, 8], [0, 16])
                 for r in range(2)]
            y = [v(ct, 256 * part + P * d, [16, 8], [0, 8], [1, 16]) for part in range(3)]
            pool.tensor_tensor(o[0], x[0], y[0], MUL)
            pool.tensor_tensor(t[0], x[1], y[2], MUL)
            pool.tensor_tensor(o[1], x[0], y[2], MUL)
            link(pool.tensor_tensor(t[1], x[1], y[0], MUL))
            pool.tensor_tensor(o[0], o[0], t[0], ADD)
            link(pool.tensor_tensor(o[1], o[1], t[1], SUB))
        pool.sem_inc(sem("ca_ready"), 1)

        pool.wait_ge(sem("out_k"), 8)
        pool.wait_ge(sem("w_lo_done"), NCH)
        pool.iota(v(toki, 0, [1, NT]), pattern=[[P, NT]], base=0, channel_multiplier=1)
        link(pool.iota(v(idx, 0, [1, NE]), pattern=[[1, NE]], base=0, channel_multiplier=0))
        pool.tensor_copy(v(rt, 1040, [1, NE]), v(idx, 0, [1, NE])).then_inc(sem("iotas"), 1)
        for n in range(NT):
            pool.wait_ge(sem("h2"), n + 1)
            pool.dma_start(h2_dram[P * n:P * n + P, :], v(h2, D * n, [1, D])).then_inc(sem("h2_out"), 16)
        pool.wait_ge(sem("rows"), 1)
        pool.wait_ge(sem("tok_zero"), 16)
        for n in range(NT):
            for j in range(2):
                pool.indirect_dma_start(
                    out=tok_dram, out_offset=bass.IndirectOffsetOnAxis(ap=v(rowi, 4 * j + n, [1, 1]), axis=0),
                    in_=v(toki, n, [1, 1]), in_offset=None).then_inc(sem("scattered"), 16)
        pool.wait_ge(sem("scattered"), 16 * 8)
        pool.wait_ge(sem("iotas"), 1)
        pool.dma_start(v(idx, 0, [1, NE]), tok_dram.rearrange("(s e) o -> s (e o)", e=NE)[0:P, :]).then_inc(
            sem("idx_in"), 16)
        pool.wait_ge(sem("idx_in"), 16)
        pool.wait_ge(sem("h2_out"), 16 * NT)

        def gather(e):
            pool.indirect_dma_start(out=v(xg, D * (e % 2), [1, D]), out_offset=None, in_=h2_dram,
                                    in_offset=bass.IndirectOffsetOnAxis(ap=v(idx, e, [1, 1]), axis=0)).then_inc(
                                        sem(f"xg{e % 2}"), 16)

        gather(0)
        gather(1)
        for e in range(NE):
            if e + 2 < NE:
                pool.wait_ge(sem("xt"), 2 * e + 2)
                gather(e + 2)
            if e >= 1:
                store_y(pool, e - 1)
        store_y(pool, NE - 1)
        for b in range(2):
            pool.wait_ge(sem(f"y_st{b}"), 16 * 8)

        def last_gathers(src):
            for n in range(NT):
                for j, dst in enumerate((y0, y1)):
                    pool.indirect_dma_start(out=v(dst, D * n, [1, D]), out_offset=None, in_=src,
                                            in_offset=bass.IndirectOffsetOnAxis(ap=v(rowi, 4 * j + n, [1, 1]),
                                                                                axis=0)).then_inc(sem(f"yg{n}"), 16)

        with pool.If(needed(pool)):
            pool.dma_start(ya_dram[0:CAP * NE, :], ye_dram).then_inc(sem("ya_main"), 16)
            with pool.Fori(0, 3) as j:
                with pool.Fori(0, NE) as e:
                    it = NE * j + e + 1
                    pool.dma_start(v(idxo, 0, [1, 1]),
                                   tok_dram.rearrange("(j p e) o -> j p (e o)", p=P, e=NE)
                                   [bass.ds(j + 1, 1), :, bass.ds(e, 1)].rearrange("a p e -> p (a e)"), allow_slow_non_contiguous=True).then_inc(
                                       sem("ov_idx"), 16)
                    pool.wait_ge(sem("ov_idx"), 16 * it)
                    pool.sem_inc(sem("ov_turn"), 1)
                    pool.indirect_dma_start(out=v(xg, 0, [1, D]), out_offset=None, in_=h2_dram,
                                            in_offset=bass.IndirectOffsetOnAxis(ap=v(idxo, 0, [1, 1]),
                                                                                axis=0)).then_inc(sem("ov_g"), 16)
                    pool.wait_ge(sem("ov_y"), it)
                    pool.dma_start(ya_dram.rearrange("(j p e) d -> j p e d", p=P, e=NE)
                                   [bass.ds(j + 1, 1), :, bass.ds(e, 1), :].rearrange("a p e d -> p (a e d)"),
                                   v(ysb, 0, [1, D])).then_inc(sem("ov_st"), 16)
                    pool.wait_ge(sem("ov_st"), 16 * it)
            pool.wait_ge(sem("ya_main"), 16)
            last_gathers(ya_dram)
        with pool.If(pool.value_load(flag[0:1, 0:1], min_val=0, max_val=1) < 1):
            last_gathers(ye_dram)

    ctx.close()


_INS = ["x", "mem", "norm_mix", "norm_ffn", "norm_mem", "w_in", "b_gate", "na_rpb", "s5_lam_re", "s5_lam_im",
        "s5_log_dt", "s5_b_re", "s5_b_im", "s5_c_re", "s5_c_im", "s5_d", "s5_w_glu", "w_mem_kv", "w_br_na",
        "w_br_s5", "w_br_xa", "w_out", "moe_w_coarse", "moe_b_coarse", "moe_w_fine", "moe_b_fine", "moe_w_gate",
        "moe_w_up", "moe_w_down", "final_norm"]


def kernel(**inputs):
    import concourse.bacc as bacc
    import numpy as np
    from concourse.bass_utils import run_bass_kernel_spmd

    nc = bacc.Bacc("TRN2", target_bir_lowering=False, num_devices=1)
    arrays, args = {}, {}
    for name in _INS:
        w = np.ascontiguousarray(inputs[name])
        arrays[f"in_{name}"] = w
        args[name] = nc.dram_tensor(f"in_{name}", w.shape, mybir.dt.from_np(w.dtype), kind="ExternalInput").ap()
    out = nc.dram_tensor("out_0", (1, SEQ, D), F32, kind="ExternalOutput").ap()
    build(nc, args, out)
    return run_bass_kernel_spmd(nc, [arrays], core_ids=[0]).results[0]["out_0"]
```

```python
import math
from contextlib import ExitStack

import concourse.bass as bass
from concourse import mybir

F32, F32R, BF16, I32 = mybir.dt.float32, mybir.dt.float32r, mybir.dt.bfloat16, mybir.dt.int32
ALU, ACT, AX = mybir.AluOpType, mybir.ActivationFunctionType, mybir.AxisListType
ADD, SUB, MUL = ALU.add, ALU.subtract, ALU.mult

P = 128
D = 1024
KD = D // P
SEQ, GW = 512, 64
ROWS = SEQ // GW
NT = SEQ // P
MEM = 256
NAH, XAH, HD = 8, 4, 64
NAW, S5W, XAW = NAH * HD, 256, XAH * HD
G5, CH5, ST5 = 16, 16, 64
T5 = 8
K5 = SEQ // T5
DP = 2 * G5 // 2
NE, NG4, FF = 16, 4, 256
CAP = P
EPS = 1e-6
RPB_R, RPB_C = 15, 31

C_U, C_MEMK, C_MEMV, C_QX, C_Q, C_K, C_V, C_GLU = 0, 2, 4, 6, 8, 12, 16, 20
C_S5G, C_S5P, C_XAG, C_XAP, C_NAG, C_NAP, C_OUT = 21, 29, 31, 39, 41, 49, 53
NCH = 61
EU = 9
RAW, HL = 6, 2
UNITS = XAH * NT + NAH * NT
GATE_CHUNKS = [*range(C_S5G, C_S5P), *range(C_XAG, C_XAP), *range(C_NAG, C_NAP)]
SLOTS = {c: 3 if n in range(4, 16) else 2 for n, c in enumerate(GATE_CHUNKS[:-4])}
TURNS = {C_XAP - 2 + j: (j,) for j in range(2)} | {C_NAP - 4 + j: (j,) for j in range(4)}
assert sum(SLOTS.values()) >= UNITS + 4


def tiles_of(c):
    if c < C_MEMK:
        return [("u", c)]
    if c < C_MEMV:
        return [("mk", c - C_MEMK)]
    if c < C_QX:
        return [("mv", c - C_MEMV)]
    if c < C_Q:
        return [("qx", c - C_QX)]
    if c < C_K:
        return [("q", c - C_Q)]
    if c < C_V:
        return [("k", c - C_K)]
    if c < C_GLU:
        return [("v", c - C_V)]
    if c == C_GLU:
        return [("gt", 0), ("gv", 0), ("gt", 1), ("gv", 1)]
    for name, first, proj, per in (("s5", C_S5G, C_S5P, 4), ("xa", C_XAG, C_XAP, 4), ("na", C_NAG, C_NAP, 2)):
        if first <= c < proj:
            turns = TURNS.get(c, ())
            return [(name + "t", j) for j in turns] + [(name + "g", c - first)]
        if proj <= c < proj + 8 // per:
            return [(name + "p", per * (c - proj) + j) for j in range(per)]
    return []


TILES = [t for c in range(NCH) for t in tiles_of(c)]
BY_DVE = ("gv", "s5p", "xap", "nap", "xat", "nat")


def taken(g):
    dve = TILES[g][0] in BY_DVE
    return dve, sum((t[0] in BY_DVE) == dve for t in TILES[:g + 1])


def unit(u):
    if u < XAH * NT:
        return False, u % XAH, u // XAH
    u -= XAH * NT
    return True, u % NAH, u // NAH


def window(i):
    lo, hi = max(0, P * i - 64), min(SEQ, P * i + 192)
    return lo, hi - lo, lo - (P * i - 64)


def key_chunks(i):
    lo, n, _ = window(i)
    out = []
    for w in (i, i + 1):
        a, b = max(0, P * w - 64), min(SEQ, P * w + 64)
        out.append((w, b - a, a - lo))
    return out


def build(nc, a, out):
    ctx = ExitStack()
    base = (nc.sbuf_base + 63) // 64 * 64

    def at(name, kb, cols, dt=F32):
        return nc.alloc_sbuf_tensor_at(name, [P, cols], dt, offset=base + int(kb * 1024))

    def v(t, off, *dims, p0=0, pn=P):
        first = t[p0:p0 + pn, 0:1]
        return bass.AP(tensor=first.tensor, offset=first.offset + off, ap=[first.ap[0]] + [list(d) for d in dims])

    sems = {}

    def sem(name):
        if name not in sems:
            sems[name] = ctx.enter_context(nc.semaphore(name))
        return sems[name]

    off = [0.0]

    def small(name, cols, dt=F32):
        t = at(name, off[0], cols, dt)
        off[0] += math.ceil(cols * (2 if dt == BF16 else 4) / 64) * 64 / 1024
        assert off[0] <= 10.5, (name, off[0])
        return t

    ident = small("ident", P)
    identb = small("identb", P, BF16)
    maskb = small("maskb", 3 * 256, BF16)
    upper = small("upper", P, BF16)
    onesb = small("onesb", P, BF16)
    prm = small("prm", P)
    prt = small("prt", P)
    bgh = small("bgh", 24)
    stat = small("stat", 64)
    s5s = small("s5s", 16 * 24)
    pw = small("pw", 2 * 9 * DP)
    soft = small("soft", 8 * 8)
    ct = small("ct", 3 * DP * CH5)
    lbias = small("lbias", 20)
    LR, LI, LDT, GMIX, GFFN, GMEM, BG, DS = 0, 16, 32, 48, 56, 64, 72, 96

    h_hi, h_lo = at("h_hi", 10.5, KD * SEQ, F32R), at("h_lo", 26.5, KD * SEQ, F32R)
    m_hi, m_lo = at("m_hi", 10.5, KD * SEQ, F32R), at("m_lo", 26.5, KD * SEQ, F32R)
    x_sb = at("x_sb", 42.5, NT * D)
    bat = at("bat", 42.5, 2 * DP * P)
    ca = at("ca", 42.5, 2 * DP * P)
    raw = at("raw", 58.5, RAW * 1024)
    w_hi, w_lo = at("w_hi", 82.5, HL * 1024, F32R), at("w_lo", 90.5, HL * 1024, F32R)
    wo_hi, wo_lo = at("wo_hi", 114.5, 4 * 1024, F32R), at("wo_lo", 130.5, 4 * 1024, F32R)
    wp_hi, wp_lo = at("wp_hi", 188.5, 2 * 1024, F32R), at("wp_lo", 196.5, 2 * 1024, F32R)
    mm_hi, mm_lo = at("mm_hi", 98.5, KD * MEM, F32R), at("mm_lo", 106.5, KD * MEM, F32R)
    qT, kT = at("qT", 98.5, 4 * SEQ), at("kT", 106.5, 4 * SEQ)
    na_hi, na_lo = at("na_hi", 98.5, 4 * SEQ, F32R), at("na_lo", 106.5, 4 * SEQ, F32R)
    vw = at("vw", 114.5, 5 * NAW)
    xa_hi, xa_lo = at("xa_hi", 136.5, 2 * SEQ, F32R), at("xa_lo", 140.5, 2 * SEQ, F32R)
    ctb = at("ctb", 118.5, 2 * DP * 32)
    cn = at("cn", 114.5, 8 * 2 * 64)
    ez = at("ez", 124.5, NAH * 256)
    mem_sb = at("mem_sb", 124.5, 2 * D)
    uT = at("uT", 132.5, 2 * SEQ)
    qxT, kmT, vm = at("qxT", 136.5, 2 * SEQ), at("kmT", 140.5, 2 * MEM), at("vm", 142.5, 2 * XAW)
    s5_hi, s5_lo = at("s5_hi", 144.5, 2 * SEQ, F32R), at("s5_lo", 148.5, 2 * SEQ, F32R)
    ezraw = at("ezraw", 144.5, NAH * 256)
    vt = at("vt", 152.5, 2 * SEQ)
    R0 = 156.5
    ba = at("ba", R0, 2 * DP * P)
    wz = at("wz", R0, 2 * DP * K5)
    tmp = at("tmp", R0 + 8, 2 * DP * K5)
    ypk = at("ypk", R0 + 8, G5 * K5)
    yT = at("yT", R0, 2 * SEQ)
    yg = at("yg", R0 + 4, 2 * SEQ)
    phase = at("phase", R0 + 16, 2 * DP * K5)
    y_hi, y_lo = at("y_hi", R0 + 16, 2 * SEQ, F32R), at("y_lo", R0 + 20, 2 * SEQ, F32R)
    mg = at("mg", R0 + 24, G5 * P)
    glut = at("glut", R0 + 24, 2 * SEQ)
    glui = at("glui", R0 + 28, 2 * SEQ)
    st = [at("st_re", 114.5, 2 * DP * (K5 + 1)), at("st_im", R0 + 32, 2 * DP * (K5 + 1))]
    decay = at("decay", R0 + 40.25, DP * K5)
    upk = at("upk", R0 + 44.25, G5 * K5)
    stk = at("stk", R0 + 48.25, 2 * G5 * CH5)
    bb = at("bb", R0 + 40.25, 4 * DP * CH5)
    squares = at("squares", R0, 6 * D)
    junk = at("junk", R0 + 32, D)
    pjunk = at("pjunk", R0 + 36, D)
    wide = at("wide", R0 + 44.25, 352)
    flip = at("flip", R0 + 46, P)
    pt5 = at("pt5", 144.5, 2 * 8 * P)
    merged = at("merged", R0, KD * SEQ)
    gt = at("gt", R0 + 16, KD * SEQ)
    onat = at("onat", R0 + 32, NT * 512)
    ssb = at("ssb", R0 + 40, 3 * 256)
    pr = at("pr", R0 + 43, 3 * 256)
    pts = at("pts", R0 + 46, 2 * 256)
    onx = at("onx", 132.5, NT * 256)
    prod = at("prod", 152.5, 2 * SEQ)
    E0, R1 = 98.5, 146.5
    eraw = at("eraw", E0, EU * 2048)
    HLK = [10.5, 26.5, 58.5]
    e_hi = [at(f"e_hi{j}", HLK[j], 2048, F32R) for j in range(3)]
    e_lo = [at(f"e_lo{j}", HLK[j] + 8, 2048, F32R) for j in range(3)]
    xt_hi, xt_lo = at("xt_hi", 74.5, KD * P, F32R), at("xt_lo", 78.5, KD * P, F32R)
    at_hi, at_lo = at("at_hi", 82.5, 2 * P, F32R), at("at_lo", 83.5, 2 * P, F32R)
    act_t, act_s, act_a = at("act_t", 84.5, FF), at("act_s", 85.5, FF), at("act_a", 86.5, FF)
    gfin = at("gfin", 87.5, D)
    rt = at("rt", 91.5, 1152)
    selb = at("selb", 96, 4 * NE, BF16)
    rowi = at("rowi", 96.25, 8, I32)
    toki = at("toki", 96.5, 4, I32)
    idx = at("idx", 96.75, NE, I32)
    flag = at("flag", 97, 1, I32)
    hot = at("hot", 190.5, 8 * P)
    slots = at("slots", 196.5, 2 * P)
    slotsi = at("slotsi", 197.5, 2 * P, I32)
    tokf = at("tokf", 198.5, 4)
    idx01 = at("idx01", 199, 2, I32)
    wcf = at("wcf", 182.5, KD * 20)
    wts = at("wts", 96.0 + 2.0, 8)
    idxo = at("idxo", 98.125, 1, I32)
    gffb = at("gffb", 178.5, D)
    xtf = at("xtf", R1, KD * P)
    atf = at("atf", R1 + 4, 2 * P)
    zi = at("zi", 152.5, 64, I32)
    h2 = at("h2", R1, NT * D)
    h2T = at("h2T", R1 + 16, KD * SEQ)
    xg = at("xg", R1 + 28, 3 * D)
    ysb = at("ysb", R1 + 40, 2 * D)
    y0 = at("y0", R1, NT * D)
    y1 = at("y1", R1 + 16, NT * D)

    bank = [ctx.enter_context(nc.psum_tensor(f"bank{i}", [P, 512], F32)) for i in range(8)]

    u_dram = nc.dram_tensor("u_scratch", (S5W, SEQ), F32, kind="Internal").ap()
    y_dram = nc.dram_tensor("y_scratch", (P, G5 * K5), F32, kind="Internal").ap()
    h2_dram = nc.dram_tensor("h2_scratch", (SEQ, D), F32, kind="Internal").ap()
    ye_dram = nc.dram_tensor("ye_scratch", (CAP * NE, D), F32, kind="Internal").ap()
    ya_dram = nc.dram_tensor("ya_scratch", (SEQ * NE, D), F32, kind="Internal").ap()
    tok_dram = nc.dram_tensor("tok_scratch", (SEQ * NE, 1), I32, kind="Internal").ap()

    w_in = a["w_in"][0]
    x_nat = a["x"][0].rearrange("(n p) d -> p n d", p=P)
    out_nat = out[0].rearrange("(n p) d -> p n d", p=P)

    def chunk_src(c):
        def cols(w, c0, n=P):
            return w[:, c0:c0 + n].rearrange("(k p) n -> p k n", p=P)
        if c < C_MEMK:
            return cols(w_in, 3 * NAW + P * c)
        if c < C_QX:
            return cols(a["w_mem_kv"][0], P * (c - C_MEMK))
        if c < C_Q:
            return cols(w_in, 3 * NAW + S5W + P * (c - C_QX))
        if c < C_GLU:
            return cols(w_in, P * (c - C_Q))
        if c == C_GLU:
            return cols(a["s5_w_glu"][0], 0, 512)
        g0 = 3 * NAW + S5W + XAW
        for first, branch in ((C_S5G, 1), (C_XAG, 2), (C_NAG, 0)):
            if first <= c < first + 8:
                return cols(w_in, g0 + D * branch + P * (c - first))
        if C_S5P <= c < C_XAG:
            return cols(a["w_br_s5"][0], 512 * (c - C_S5P), 512)
        if C_XAP <= c < C_NAG:
            return cols(a["w_br_xa"][0], 512 * (c - C_XAP), 512)
        if C_NAP <= c < C_OUT:
            return cols(a["w_br_na"][0], 256 * (c - C_NAP), 256)
        half, kp = divmod(c - C_OUT, 4)
        return a["w_out"][0][256 * kp:256 * kp + 256, 512 * half:512 * half + 512].rearrange(
            "(k p) n -> p k n", p=P)

    def unit_src(kind, e):
        one = slice(e, e + 1) if isinstance(e, int) else bass.ds(e, 1)
        if kind == 2:
            w = a["moe_w_down"][0][one].rearrange("o (k p) n -> p (o k) n", p=P)
            return [w[:, k:k + 1, :] for k in range(2)]
        return [a[w][0][one].rearrange("o (k p) n -> p (o k) n", p=P)[:, 4 * kind:4 * kind + 4, :]
                for w in ("moe_w_gate", "moe_w_up")]

    def load_of(n0, i):
        return 18 // EU * i + n0 // EU + 1

    def unit_dst(kind, slot):
        if kind == 2:
            return [v(eraw, 2048 * slot + D * k, [D, 1], [1, D]) for k in range(2)]
        return [v(eraw, 2048 * slot + FF * j, [2 * FF, 4], [1, FF]) for j in range(2)]


    def counted(ins, name, n=1):
        return ins.then_inc(sem(name), n)

    def s5(i):
        return v(s5s, DP * i, [1, DP])

    def pcol(c, n=1):
        return v(prt, c, [1, n])

    def pv(b, off, *dims, p0=0, pn=P):
        return v(bank[b], off, *dims, p0=p0, pn=pn)

    def raw32(x):
        return x.bitcast(F32)

    def needed(eng):
        eng.wait_ge(sem("flag"), 1)
        return eng.value_load(flag[0:1, 0:1], min_val=0, max_val=1) > 0

    def newton(x, y, t, link):
        for _ in range(2):
            link(nc.vector.tensor_tensor(t, y, y, MUL))
            link(nc.vector.scalar_tensor_tensor(t, t, -0.5, x, MUL, MUL))
            link(nc.vector.scalar_tensor_tensor(y, t, 1.5, y, ADD, MUL))

    def cmul(eng, link, o, x, y, t):
        eng.tensor_tensor(o[0], x[0], y[0], MUL)
        eng.tensor_tensor(t[0], x[1], y[1], MUL)
        eng.tensor_tensor(o[1], x[0], y[1], MUL)
        link(eng.tensor_tensor(t[1], x[1], y[0], MUL))
        eng.tensor_tensor(o[0], o[0], t[0], SUB)
        link(eng.tensor_tensor(o[1], o[1], t[1], ADD))

    PW = 9 * DP

    def power(l, n=1):
        return [v(pw, PW * ri + DP * l, [DP, n], [1, DP]) for ri in range(2)]

    def square(eng, link):
        cmul(eng, link, [s5(20), s5(21)], [s5(18), s5(19)], [s5(18), s5(19)], [s5(22), s5(23)])
        eng.tensor_copy(s5(18), s5(20))
        link(eng.tensor_copy(s5(19), s5(21)))

    def powers_of_b(eng, link, d, h, t):
        o = [v(ba, 2048 * r + 1024 * d + 512 * h, [P, 4], [16, 8], [1, 16]) for r in range(2)]
        x = [v(pw, PW * r + (7 * DP if d == 0 else 0) + 8 * d + 4 * h, [1, 4],
               [-DP if d == 0 else DP, 8], [0, 16]) for r in range(2)]
        y = [v(bb, 512 + 256 * r + 128 * d + 64 * h, [16, 4], [0, 8], [1, 16]) for r in range(2)]
        cmul(eng, link, o, x, y, [v(t, 512 * r, [P, 4], [16, 8], [1, 16]) for r in range(2)])

    def wait_taken(eng, g):
        dve, n = taken(g)
        eng.wait_ge(sem("dve_took" if dve else "act_took"), n)

    def chunk_used(eng, c):
        eng.wait_ge(sem("tile"), sum(len(tiles_of(i)) for i in range(c + 1)))

    def parts_of(c):
        if c < C_OUT + HL:
            return w_hi, w_lo, 1024 * (c % HL)
        if c < C_OUT + 6:
            return wo_hi, wo_lo, 1024 * (c - C_OUT - 2)
        return wp_hi, wp_lo, 1024 * (c - C_OUT - 6)

    def store_y(pool, e):
        pool.wait_ge(sem("y_a"), e + 1)
        pool.wait_ge(sem("y_d"), e + 1)
        pool.dma_start(ye_dram.rearrange("(s e) d -> s e d", e=NE)[0:P, e, :],
                       v(ysb, D * (e % 2), [1, D])).then_inc(sem(f"y_st{e % 2}"), 16)

    H2_BANK = (4, 7)
    g_of = {t: g for g, t in enumerate(TILES)}
    turned = [("mv", 0), ("mv", 1), ("v", 0), ("v", 1), ("v", 2), ("v", 3)]

    block = ctx.enter_context(nc.Block())

    @block.sync
    def _(sp):
        for n in range(NT):
            sp.dma_start(v(x_sb, D * n, [1, D]), x_nat[:, n, :]).then_inc(sem(f"x_in{n}"), 16)

        def load(c):
            if c >= RAW:
                sp.wait_ge(sem("w_lo_done"), c - RAW + 1)
            src = chunk_src(c)
            k, n = src.shape[1], src.shape[2]
            sp.dma_start(v(raw, 1024 * (c % RAW), [n, k], [1, n]), src).then_inc(sem(f"w_in{c % RAW}"), 16)

        def rows(w, r, n):
            sp.dma_start(v(prm, 0, [1, P], p0=r, pn=n), w).then_inc(sem("prm_in"), 16)

        rows(a["s5_lam_re"][0].rearrange("d (p g) n -> (d p) (g n)", g=2), LR, DP)
        rows(a["s5_lam_im"][0].rearrange("d (p g) n -> (d p) (g n)", g=2), LI, DP)
        rows(a["norm_mix"][0].rearrange("(k p) -> k p", p=P), GMIX, KD)
        rows(a["norm_ffn"][0].rearrange("(k p) -> k p", p=P), GFFN, KD)
        rows(a["norm_mem"][0].rearrange("(k p) -> k p", p=P), GMEM, KD)
        rows(a["b_gate"][0].rearrange("(k p) -> k p", p=P), BG, 3 * KD)
        rows(a["s5_d"][0].rearrange("(k p) -> k p", p=P), DS, 2)
        sp.dma_start(v(stat, 60, [1, 2], p0=LDT, pn=DP),
                      a["s5_log_dt"][0].rearrange("d (p g) -> (d p) g", g=2)).then_inc(sem("prm_in"), 16)
        load(0)
        sp.dma_start(v(mem_sb, 0, [D, 2], [1, D]), a["mem"][0].rearrange("(n p) d -> p n d", p=P)).then_inc(
            sem("mem_in"), 16)
        load(1)
        for ri, w in enumerate(("s5_c_re", "s5_c_im")):
            src = a[w][0].rearrange("d (h g) c n -> (g c) (d h) n", g=8)
            for twice in range(2):
                sp.dma_start(v(cn, 512 * ri + 64 * twice, [P, 4], [1, 64]), src).then_inc(sem("c_in"), 16)
        for ri, w in enumerate(("s5_b_re", "s5_b_im")):
            sp.dma_start(v(bb, 256 * ri, [CH5, DP], [1, CH5]),
                          a[w][0].rearrange("d (p g) n c -> (g n) (d p) c", g=2)).then_inc(sem("b_in"), 16)
        sp.dma_start(v(lbias, 0, [1, 4]), a["moe_b_coarse"].partition_broadcast(P)).then_inc(sem("lb_in"), 16)
        sp.dma_start(v(lbias, 4, [1, 16]), a["moe_b_fine"].partition_broadcast(P)).then_inc(sem("lb_in"), 16)
        for c in range(2, C_NAG):
            load(c)
        sp.wait_ge(sem("s5_y"), 2)
        sp.dma_start(v(x_sb, 0, [D, NT], [1, D]), x_nat).then_inc(sem("x_again"), 16)
        for c in range(C_NAG, NCH):
            load(c)

        def load_unit(kind, e, slot):
            for dst, src in zip(unit_dst(kind, slot), unit_src(kind, e)):
                sp.dma_start(dst, src).then_inc(sem(f"e_in{slot}"), 16)

        sp.wait_ge(sem("prod"), 24)
        load_unit(0, 0, 0)
        load_unit(1, 0, 1)

        def load_next(n0, kind, e, i=0):
            sp.wait_ge(sem("e_lo_done"), 18 * i + n0 - EU + 1)
            load_unit(kind, e, n0 % EU)

        def loads(e0, i=0):
            e = 6 * i + e0
            load_next(3 * e0 + 2, 0, e + 1, i)
            load_next(3 * e0 + 3, 1, e + 1, i)
            load_next(3 * e0 + 4, 2, e, i)

        sp.wait_ge(sem("out_k"), NT)
        load_unit(0, 1, 2)
        load_unit(1, 1, 3)
        load_unit(2, 0, 4)
        load_unit(0, 2, 5)
        sp.wait_ge(sem("h2_out"), 16 * NT)
        sp.wait_ge(sem("logits"), NT)
        load_unit(1, 2, 6)
        load_unit(2, 1, 7)
        load_unit(0, 3, 8)
        load_next(9, 1, 3)
        load_next(10, 2, 2)
        with sp.Fori(0, 2) as i:
            for e0 in range(3, 9):
                loads(e0, i)
        load_next(47, 2, 15)

        with sp.If(needed(sp)):
            with sp.Fori(0, 3) as j:
                with sp.Fori(0, NE) as e:
                    sp.wait_ge(sem("ov_idx"), 16 * (NE * j + e) + 16)
                    for kind in range(3):
                        for dst, src in zip(unit_dst(kind, kind), unit_src(kind, e)):
                            sp.dma_start(dst, src).then_inc(sem("ov_in"), 16)

        for n in range(NT):
            sp.wait_ge(sem("out_ready"), n + 1)
            sp.dma_start(out_nat[:, n, :], v(x_sb, D * n, [1, D])).then_inc(sem("out_done"), 16)
        sp.wait_ge(sem("out_done"), 16 * NT)

    @block.scalar
    def _(act):
        def hi(c):
            act.wait_ge(sem(f"w_in{c % RAW}"), 16 * (c // RAW + 1))
            dst, _, o = parts_of(c)
            if HL <= c < C_OUT + HL:
                chunk_used(act, c - HL)
            act.copy(v(dst, o, [1, 1024]), v(raw, 1024 * (c % RAW), [1, 1024])).then_inc(
                sem("w_hi_done"), 1)

        act.wait_ge(sem("stat_set"), 1)
        act.activation(v(stat, 40, [1, 1]), v(stat, 48, [1, 1]), ACT.Sqrt)
        for n in range(NT):
            act.wait_ge(sem(f"x_in{n}"), 16)
            ins = act.activation(v(squares, D * n, [1, D]), v(x_sb, D * n, [1, D]), ACT.Square,
                                 accum_out=v(stat, n, [1, 1]))
        ins.then_inc(sem("squares"), 1)
        act.wait_ge(sem("means"), 1)
        act.activation(v(stat, 16, [1, NT]), v(stat, 8, [1, NT]), ACT.Sqrt).then_inc(sem("roots"), 1)
        hi(0)
        act.wait_ge(sem("mem_in"), 16)
        for n in range(2):
            ins = act.activation(v(squares, D * (NT + n), [1, D]), v(mem_sb, D * n, [1, D]), ACT.Square,
                                 accum_out=v(stat, NT + n, [1, 1]))
        ins.then_inc(sem("squares"), 1)
        hi(1)
        act.wait_ge(sem("means"), 2)
        act.activation(v(stat, 16 + NT, [1, 2]), v(stat, 8 + NT, [1, 2]), ACT.Sqrt).then_inc(sem("roots"), 1)

        def turn_hi(b):
            act.wait_ge(sem("turned"), b + 1)
            if b < KD:
                act.activation(v(h_hi, SEQ * b, [1, ROWS], [ROWS, GW]), pv(4 + b % 4, 0, [GW, ROWS], [1, GW]),
                               ACT.Identity, scale=pcol(GMIX + b)).then_inc(sem("turn_hi"), 1)
            else:
                act.activation(v(mm_hi, MEM * (b - KD), [1, MEM]), pv(4 + b % 4, 0, [1, MEM]),
                               ACT.Identity, scale=pcol(GMEM + b - KD)).then_inc(sem("turn_hi"), 1)

        for b in range(KD):
            turn_hi(b)
        act.wait_ge(sem("prt_ready"), 1)
        act.activation(s5(2), pcol(LDT, DP), ACT.Exp).then_inc(sem("s5_exp"), 1)
        act.wait_ge(sem("s5_arg"), 1)
        act.activation(s5(4), s5(3), ACT.Exp).then_inc(sem("s5_exp"), 1)
        act.activation(s5(5), s5(3), ACT.Exp, scale=float(T5)).then_inc(sem("s5_exp"), 1)
        act.wait_ge(sem("s5_arg"), 2)
        act.activation(v(s5s, 16 * 6, [1, 32]), v(s5s, 16 * 8, [1, 32]), ACT.Sin).then_inc(sem("s5_sin"), 1)

        def take_c():
            act.wait_ge(sem("c_turned"), 2)
            for ri in range(2):
                for g2 in range(2):
                    for h in range(4):
                        src = pv(2 + ri, P * h + 16 * g2, [32, 4], [1, 16], p0=64 * g2, pn=64)
                        for part, scale in ([(0, 1.0)] if ri == 0 else [(1, 1.0), (2, -1.0)]):
                            ins = act.mul(v(ct, 256 * part + 64 * h, [16, 4], [1, 16], p0=64 * g2, pn=64), src, scale)
                        ins = act.mul(v(ctb, 512 * ri + 128 * h + 16 * g2, [32, 4], [1, 16], p0=64 * g2, pn=64), src,
                                      -1.0 if ri else 1.0)
                ins.then_inc(sem("ct_ready"), 1)

        def take(g):
            kind, m = TILES[g]
            if kind in ("xat", "nat"):
                act.wait_ge(sem("tile"), g + 1)
                dst = xa_hi if kind == "xat" else na_hi
                act.copy(v(dst, SEQ * m, [1, SEQ]), pv(g % 2, 0, [1, SEQ])).then_inc(sem("o_hi"), 1)
            if kind in BY_DVE:
                return
            act.wait_ge(sem("tile"), g + 1)
            if kind == "u":
                ins = act.copy(v(uT, SEQ * m, [64, 8], [8, 8], [1, 8]), pv(g % 2, 0, [8, 8], [1, 8], [64, 8]))
            elif kind == "mk":
                ins = act.copy(v(kmT, MEM * m, [1, MEM]), pv(g % 2, 0, [1, MEM]))
            elif kind in ("mv", "v"):
                j = turned.index((kind, m))
                if j >= 2:
                    act.wait_ge(sem("v_turned"), j - 1)
                else:
                    act.wait_ge(sem("tok_zero"), 16)
                n = MEM if kind == "mv" else SEQ
                ins = act.copy(v(vt, SEQ * (j % 2), [1, n]), pv(g % 2, 0, [1, n]))
            elif kind == "qx":
                ins = act.mul(v(qxT, SEQ * m, [1, SEQ]), pv(g % 2, 0, [1, SEQ]), HD ** -0.5)
            elif kind == "q":
                if m == 0:
                    act.wait_ge(sem("tile"), g_of[("mv", 1)] + 1)
                ins = act.mul(v(qT, SEQ * m, [1, SEQ]), pv(g % 2, 0, [1, SEQ]), HD ** -0.5)
            elif kind == "k":
                ins = act.copy(v(kT, SEQ * m, [1, SEQ]), pv(g % 2, 0, [1, SEQ]))
            elif kind == "gt":
                ins = act.activation(v(glut, SEQ * m, [1, SEQ]), pv(g % 2, 0, [1, SEQ]), ACT.Tanh, scale=0.5)
            else:
                turn = ("s5g", "xag", "nag").index(kind)
                if turn:
                    act.wait_ge(sem("prod"), 8 * (turn - 1) + m + 1)
                elif m == 0:
                    act.wait_ge(sem("s5_lo"), 2)
                branch = {"s5g": 1, "xag": 2, "nag": 0}[kind]
                ins = act.activation(v(gt, SEQ * m, [1, SEQ]), pv(g % 2, 0, [1, SEQ]), ACT.Tanh, scale=0.5,
                                     bias=v(bgh, KD * branch + m, [1, 1]))
            ins.then_inc(sem("act_took"), 1)

        def exp(u):
            na, h, i = unit(u)
            act.wait_ge(sem("smax"), u + 1)
            if u >= 3:
                act.wait_ge(sem("p_turned"), u - 2)
            n = window(i)[1] if na else MEM
            src = v(ssb, 256 * (u % 3), [1, n]) if na else pv(2 + u % 2, 0, [1, n])
            act.activation(v(pr, 256 * (u % 3), [1, n]), src, ACT.Exp, bias=v(soft, 8 * (u % 8) + 1, [1, 1]),
                           accum_out=v(soft, 8 * (u % 8) + 2, [1, 1])).then_inc(sem("exp"), 1)

        def take_p(u):
            na, h, i = unit(u)
            act.wait_ge(sem("p_turned"), u + 1)
            if u >= 2:
                act.wait_ge(sem("pv"), u - 1)
            parts = [(n, k) for k, (_, n, _) in enumerate(key_chunks(i))] if na else [(P, 0), (P, 1)]
            if parts[0][0] == parts[1][0]:
                ins = act.copy(v(pts, 256 * (u % 2), [1, 256]), pv(4 + u % 2, 0, [1, 256]))
            else:
                for n, k in parts:
                    ins = act.copy(v(pts, 256 * (u % 2) + P * k, [1, P], pn=n), pv(4 + u % 2, P * k, [1, P], pn=n))
            ins.then_inc(sem("p_taken"), 1)

        def slot(s):
            if s < UNITS:
                exp(s)
            if 0 <= s - 2 < UNITS:
                take_p(s - 2)

        def take_s5_matrices():
            for q in range(8):
                act.wait_ge(sem("ba_turned"), q + 1)
                act.copy(v(bat, 512 * q, [1, 512]), pv(4 + q % 4, 0, [1, 512])).then_inc(sem("bat_took"), 1)
            act.wait_ge(sem("lags"), 1)
            act.copy(v(stk, 0, [1, 512]), pv(2, 0, [1, 512])).then_inc(sem("lags_took"), 1)
            for b in range(4):
                act.wait_ge(sem("shifted"), b + 1)
                act.copy(v(mg, 32 * b, [16, 2], [P, 16], [1, 16]),
                         pv(4 + b, 0, [256, 2], [16, 16], [1, 16])).then_inc(sem("mg_took"), 1)
            act.wait_ge(sem("u_out"), 16)
            for t in range(T5):
                act.dma_start(v(upk, 0, [K5, G5], [1, K5], p0=16 * t, pn=16),
                              u_dram.rearrange("(g c) (t k) -> c g t k", c=16, k=K5)[:, :, t, :]).then_inc(
                                  sem("u_in"), 16)

        def merged_hi(k):
            act.wait_ge(sem("prod"), 2 * KD + k + 1)
            act.mul(v(m_hi, SEQ * k, [1, GW], [GW, ROWS]), v(merged, SEQ * k, [ROWS, GW], [1, ROWS]), 0.5).then_inc(
                sem("m_hi"), 1)

        def take_y():
            act.wait_ge(sem("s5_y"), 2)
            for b in range(2):
                ins = act.copy(v(ypk, 512 * b, [1, 512]), pv(2 + b, 0, [1, 512]))
            ins.then_inc(sem("y_took"), 1)
            act.wait_ge(sem("y_took"), 1)
            act.dma_start(y_dram, v(ypk, 0, [1, G5 * K5])).then_inc(sem("y_out"), 16)

        def load_y():
            act.wait_ge(sem("y_out"), 16)
            for g in range(G5):
                act.dma_start(v(yT, SEQ * (g // 8), [K5, T5], [1, K5], p0=16 * (g % 8), pn=16),
                              y_dram.rearrange("(t c) (g k) -> c t g k", c=16, k=K5)[:, :, g, :]).then_inc(
                                  sem("y_in"), 16)

        g = 0
        s = 0
        for c in range(C_OUT):
            if c in SLOTS:
                slot(s)
                s += 1
            for kind, _ in tiles_of(c):
                if kind[2:] == "g":
                    for _ in range(SLOTS.get(c, 1) - 1):
                        slot(s)
                        s += 1
                take(g)
                g += 1
            hi(c + 2)
            for k in range(2 * (c - C_NAP) - 2, 2 * (c - C_NAP)):
                if k >= 0:
                    merged_hi(k)
            if c == 1:
                act.wait_ge(sem("act_took"), 2)
                act.dma_start(u_dram.rearrange("(m p) n -> p m n", p=P),
                              v(uT, 0, [SEQ, 2], [1, SEQ])).then_inc(sem("u_out"), 16)
            if c < 2:
                for b in range(KD + 4 * c, KD + 4 * c + 4):
                    turn_hi(b)
            if c == 3:
                for q in range(4):
                    act.wait_ge(sem("flipped"), q + 1)
                    for h in range(2):
                        ins = act.copy(v(ez, 512 * q + 256 * h, [8, 32], [1, 8]),
                                       pv(4 + q % 2, 256 * h, [1, 32], [RPB_C, 8]))
                    ins.then_inc(sem("bias_ready"), 1)
            if c == 6:
                take_c()
            if c == 8:
                take_s5_matrices()
            if c == 14:
                take_y()
            if c == 15:
                load_y()
            if c == 17:
                act.wait_ge(sem("gelu_in"), 1)
                act.activation(v(glut, 0, [1, 2 * SEQ]), v(yT, 0, [1, 2 * SEQ]), ACT.Tanh,
                               scale=math.sqrt(2 / math.pi)).then_inc(sem("gelu_t"), 1)
        for k in range(6, KD):
            merged_hi(k)
        for c in range(C_OUT + 2, NCH):
            hi(c)

        act.wait_ge(sem("prod"), 3 * KD)
        act.dma_start(v(gffb, 0, [1, D]), a["norm_ffn"].partition_broadcast(P)).then_inc(sem("gf_in"), 16)
        act.dma_start(v(wcf, 0, [20, KD], [1, 4]),
                      a["moe_w_coarse"][0].rearrange("(k p) n -> p k n", p=P)).then_inc(sem("wcf_in"), 16)
        act.dma_start(v(wcf, 4, [20, KD], [1, 16]),
                      a["moe_w_fine"][0].rearrange("(k p) n -> p k n", p=P)).then_inc(sem("wcf_in"), 16)

        def root_mean(k, spare, n):
            act.wait_ge(sem("x2"), n + 1)
            act.activation(v(spare, D * n, [1, D]), v(x_sb, D * n, [1, D]), ACT.Square,
                           accum_out=v(stat, n, [1, 1])).then_inc(sem("squares"), 1)
            act.wait_ge(sem("means"), k)
            act.activation(v(stat, 16 + n, [1, 1]), v(stat, 8 + n, [1, 1]), ACT.Sqrt).then_inc(sem("roots"), 1)

        def h2_take(n):
            for j in range(2):
                act.wait_ge(sem("h2_turned"), 2 * n + j + 1)
                act.copy(v(h2T, SEQ * 4 * j + P * n, [SEQ, 4], [1, P]), pv(H2_BANK[j], 0, [P, 4], [1, P])).then_inc(
                    sem("h2_took"), 1)

        act.activation(v(stat, 41, [1, 1]), v(stat, 48, [1, 1]), ACT.Sqrt)
        for n in range(NT):
            root_mean(n + 3, h2, n)
            if n:
                h2_take(n - 1)
        h2_take(NT - 1)
        act.dma_start(v(gfin, 0, [1, D]), a["final_norm"].partition_broadcast(P)).then_inc(sem("gfin_in"), 16)

        act.wait_ge(sem("route_arg"), 1)
        act.activation(v(rt, 960, [1, 20]), v(rt, 960, [1, 20]), ACT.Exp).then_inc(sem("route_exp"), 1)

        def unit_hi(n, j, load, dst):
            act.wait_ge(sem(f"e_in{j}"), 32 * load)
            if not (isinstance(n, int) and n < 3):
                act.wait_ge(sem("e_used"), n - 2)
            act.copy(v(e_hi[dst], 0, [1, 2048]), v(eraw, 2048 * j, [1, 2048])).then_inc(sem("e_hi_done"), 1)

        def xt_take(e):
            for j in range(2):
                act.wait_ge(sem("xt"), 2 * e + j + 1)
                act.copy(v(xt_hi, 512 * j, [1, 512]), pv(4 + j, 0, [1, 512])).then_inc(sem("xt_hi"), 1)

        def step(e0, i=None):
            peeled = i is None
            i = 0 if peeled else i
            e, odd = 6 * i + e0, e0 % 2 == 1
            n0 = 3 * e0 + 2
            if not peeled or e >= 1:
                act.wait_ge(sem("at"), e)
                act.copy(v(at_hi, 0, [1, 256]), pv(6, 0, [1, 256])).then_inc(sem("at_hi"), 1)
            if not peeled or e < 15:
                unit_hi(3 * e + 2, n0 % EU, load_of(n0, i), 2)
            if not peeled or e < 16:
                act.wait_ge(sem("e_used"), 2 if peeled and e == 0 else 3 * e + 1)
                if not peeled or e >= 1:
                    act.wait_ge(sem("act_a"), e)
                act.activation(v(act_t, 0, [1, FF]), pv(1 if odd else 0, 0, [1, FF]), ACT.Tanh,
                               scale=0.5).then_inc(sem("tanh"), 1)
            if not peeled or e < 15:
                xt_take(e + 1)
                unit_hi(3 * e + 3, (n0 + 1) % EU, load_of(n0 + 1, i), 0)
                unit_hi(3 * e + 4, (n0 + 2) % EU, load_of(n0 + 2, i), 1)
            elif e == 15:
                unit_hi(47, 47 % EU, load_of(47, 0), 2)
            if not peeled or e >= 1:
                act.wait_ge(sem("e_used"), 48 if peeled and e == 16 else 3 * e + 2)
                if not peeled or e >= 3:
                    act.wait_ge(sem(f"y_st{0 if odd else 1}"), 16 * (3 * i + (e0 - 1) // 2))
                act.copy(v(ysb, 0 if odd else D, [1, 512]), pv(2, 0, [1, 512])).then_inc(sem("y_a"), 1)

        unit_hi(0, 0, 1, 0)
        unit_hi(1, 1, 1, 1)
        xt_take(0)
        for e in range(3):
            step(e)
        with act.Fori(0, 2) as i:
            for e0 in range(3, 9):
                step(e0, i)
        step(15)
        step(16)

        with act.If(needed(act)):
            with act.Fori(0, 3) as j:
                with act.Fori(0, NE) as e:
                    it = NE * j + e + 1
                    act.wait_ge(sem("ov_xt"), it)
                    for b in range(2):
                        ins = act.copy(v(xtf, 512 * b, [1, 512]), pv(4 + b, 0, [1, 512]))
                    ins.then_inc(sem("ov_x"), 1)
                    act.wait_ge(sem("ov_gu"), it)
                    act.activation(v(act_t, 0, [1, FF]), pv(0, 0, [1, FF]), ACT.Tanh, scale=0.5).then_inc(
                        sem("ov_tanh"), 1)
                    act.wait_ge(sem("ov_at"), it)
                    act.copy(v(atf, 0, [1, 256]), pv(6, 0, [1, 256])).then_inc(sem("ov_ac"), 1)
                    act.wait_ge(sem("ov_down"), it)
                    for b in range(2):
                        ins = act.copy(v(ysb, 512 * b, [1, 512]), pv(2 + b, 0, [1, 512]))
                    ins.then_inc(sem("ov_y"), 1)
        act.activation(v(stat, 42, [1, 1]), v(stat, 48, [1, 1]), ACT.Sqrt)
        for n in range(NT):
            act.wait_ge(sem("x2"), NT + n + 1)
            ins = act.activation(v(eraw, D * n, [1, D]), v(x_sb, D * n, [1, D]), ACT.Square,
                                 accum_out=v(stat, n, [1, 1]))
        ins.then_inc(sem("squares"), 1)
        act.wait_ge(sem("means"), NT + 3)
        act.activation(v(stat, 16, [1, NT]), v(stat, 8, [1, NT]), ACT.Sqrt).then_inc(sem("roots"), 1)

    @block.vector
    def _(dve):
        count = {}

        def done(ins, name):
            ins.then_inc(sem(name), 1)
            count[name] = count.get(name, 0) + 1
            dve.wait_ge(sem(name), count[name])

        def link(ins):
            done(ins, "dve_chain")

        def inverse_root(k, j, n):
            dve.wait_ge(sem("squares"), k)
            done(dve.tensor_scalar(v(stat, 8 + j, [1, n]), v(stat, j, [1, n]), 1.0 / D, EPS, MUL, ADD), "means")
            dve.wait_ge(sem("roots"), k)
            link(dve.reciprocal(v(stat, 24 + j, [1, n]), v(stat, 16 + j, [1, n])))
            newton(v(stat, 8 + j, [1, n]), v(stat, 24 + j, [1, n]), v(stat, 32 + j, [1, n]), link)

        def lo(c):
            dve.wait_ge(sem("w_hi_done"), c + 1)
            h_, l_, o = parts_of(c)
            dve.tensor_tensor(v(l_, o, [1, 1024]), v(raw, 1024 * (c % RAW), [1, 1024]),
                              raw32(v(h_, o, [1, 1024])), SUB).then_inc(sem("w_lo_done"), 1)

        dve.memset(v(stat, 48, [1, 1]), 1.0).then_inc(sem("stat_set"), 1)
        dve.wait_ge(sem("prm_in"), 16 * 8)
        done(dve.tensor_copy(v(prm, 0, [64, 2], [1, 64], p0=LDT, pn=DP),
                             v(stat, 60, [1, 2], [0, 64], p0=LDT, pn=DP)), "prm_ready")
        dve.wait_ge(sem("prm_turned"), 1)
        done(dve.tensor_copy(v(prt, 0, [1, 98]), pv(0, 0, [1, 98])), "prt_ready")
        inverse_root(1, 0, NT)
        for n in range(NT):
            dve.tensor_scalar(v(x_sb, D * n, [1, D]), v(x_sb, D * n, [1, D]), v(stat, 24 + n, [1, 1]), None,
                              MUL).then_inc(sem("normed"), 1)
        inverse_root(2, NT, 2)
        def turn_lo(b):
            dve.wait_ge(sem("turn_hi"), b + 1)
            if b < KD:
                o = [[1, ROWS], [ROWS, GW]]
                dve.scalar_tensor_tensor(v(h_lo, SEQ * b, *o), pv(4 + b % 4, 0, [GW, ROWS], [1, GW]),
                                         pcol(GMIX + b), raw32(v(h_hi, SEQ * b, *o)), MUL, SUB).then_inc(
                                             sem("turn_lo"), 1)
            else:
                k = b - KD
                dve.scalar_tensor_tensor(v(mm_lo, MEM * k, [1, MEM]), pv(4 + b % 4, 0, [1, MEM]),
                                         pcol(GMEM + k), raw32(v(mm_hi, MEM * k, [1, MEM])), MUL,
                                         SUB).then_inc(sem("turn_lo"), 1)

        for b in range(KD):
            turn_lo(b)
        lo(0)
        lo(1)
        for n in range(2):
            dve.tensor_scalar(v(mem_sb, D * n, [1, D]), v(mem_sb, D * n, [1, D]),
                              v(stat, 24 + NT + n, [1, 1]), None, MUL).then_inc(sem("normed"), 1)
        dve.tensor_scalar(v(bgh, 0, [1, 24]), pcol(BG, 24), 0.5, None, MUL)
        dve.tensor_scalar(s5(0), pcol(LR, DP), -1e-4, None, ALU.min)
        link(dve.tensor_copy(s5(1), pcol(LI, DP)))
        dve.wait_ge(sem("s5_exp"), 1)
        done(dve.tensor_tensor(s5(3), s5(0), s5(2), MUL), "s5_arg")
        link(dve.tensor_tensor(s5(8), s5(1), s5(2), MUL))
        link(dve.tensor_scalar(s5(9), s5(8), math.pi / 2, None, ADD))
        two = v(s5s, DP * 8, [1, 2 * DP])
        turns, t32 = v(s5s, DP * 10, [1, 2 * DP]), v(s5s, DP * 12, [1, 2 * DP])
        link(dve.tensor_scalar(turns, two, 1 / (2 * math.pi), 12582912.0, MUL, ADD))
        link(dve.tensor_scalar(turns, turns, -12582912.0, None, ADD))
        link(dve.tensor_copy(s5(9), s5(8)))
        c1 = 6.28125
        c2 = float.fromhex("0x1.fb4p-10")
        c3 = 2 * math.pi - c1 - c2
        for c in (c1, c2, c3):
            link(dve.scalar_tensor_tensor(two, turns, -c, two, MUL, ADD))
        link(dve.tensor_scalar(s5(9), s5(9), math.pi / 2, None, ADD))
        link(dve.tensor_scalar(t32, two, 3.1415925, -3.1415925, ALU.min, ALU.max))
        done(dve.tensor_copy(two, t32), "s5_arg")


        def disc():
            dve.wait_ge(sem("s5_sin"), 1)
            dve.wait_ge(sem("s5_exp"), 3)
            dve.memset(v(pw, 0, [1, DP]), 1.0)
            dve.memset(v(pw, PW, [1, DP]), 0.0)
            dve.tensor_tensor(v(pw, DP, [1, DP]), s5(4), s5(7), MUL)
            link(dve.tensor_tensor(v(pw, PW + DP, [1, DP]), s5(4), s5(6), MUL))
            ar, ai = v(pw, DP, [1, DP]), v(pw, PW + DP, [1, DP])
            dve.tensor_scalar(s5(10), ar, -1.0, None, ADD)
            dve.tensor_tensor(s5(12), s5(0), s5(0), MUL)
            link(dve.tensor_tensor(s5(13), s5(1), s5(1), MUL))
            dve.tensor_tensor(s5(12), s5(12), s5(13), ADD)
            dve.tensor_tensor(s5(14), s5(10), s5(0), MUL)
            dve.tensor_tensor(s5(15), ai, s5(1), MUL)
            dve.tensor_tensor(s5(16), ai, s5(0), MUL)
            link(dve.tensor_tensor(s5(17), s5(10), s5(1), MUL))
            dve.reciprocal(s5(13), s5(12))
            dve.tensor_tensor(s5(14), s5(14), s5(15), ADD)
            link(dve.tensor_tensor(s5(16), s5(16), s5(17), SUB))
            dve.tensor_tensor(s5(10), s5(14), s5(13), MUL)
            link(dve.tensor_tensor(s5(11), s5(16), s5(13), MUL))
            dve.sem_inc(sem("disc"), 1)

        HALF = DP * K5
        DW = 8 * K5

        def ph_of(d, r):
            return v(phase, HALF * r + DW * d + (K5 - 1 if d else 0), [K5, 8], [-1 if d else 1, K5])

        def rotate_in(d):
            dve.wait_ge(sem("phases"), 1)
            dve.wait_ge(sem("w5"), 2 * d + 2)
            w = [pv(4 + 2 * d + r, 0, [K5, 8], [1, K5]) for r in range(2)]
            z = [v(wz, HALF * r + DW * d, [K5, 8], [1, K5]) for r in range(2)]
            t = [v(tmp, HALF * r + DW * d, [K5, 8], [1, K5]) for r in range(2)]
            dve.tensor_tensor(z[0], w[0], ph_of(d, 0), MUL)
            dve.tensor_tensor(t[0], w[1], ph_of(d, 1), MUL)
            dve.tensor_tensor(z[1], w[1], ph_of(d, 0), MUL)
            done(dve.tensor_tensor(t[1], w[0], ph_of(d, 1), MUL), "w5_took")
            dve.tensor_tensor(z[0], z[0], t[0], ADD)
            link(dve.tensor_tensor(z[1], z[1], t[1], SUB))

        def scans():
            dve.wait_ge(sem("decays"), 1)
            for d in range(2):
                for r in range(2):
                    o = HALF * r + DW * d + (DW - 1 if d else 0)
                    step = -1 if d else 1
                    ins = dve.tensor_tensor_scan(v(tmp, o, [step, DW]),
                                                 v(decay, DW * d + (DW - 1 if d else 0), [step, DW]),
                                                 v(wz, o, [step, DW]), 0.0, MUL, ADD)
            link(ins)

        def rotate_out(d):
            z = [v(tmp, HALF * r + DW * d, [K5, 8], [1, K5]) for r in range(2)]
            t = [v(wz, HALF * r + DW * d, [K5, 8], [1, K5]) for r in range(2)]
            dve.tensor_tensor(t[0], z[1], ph_of(d, 1), MUL)
            link(dve.tensor_tensor(t[1], z[0], ph_of(d, 1), MUL))
            dve.tensor_tensor(z[0], z[0], ph_of(d, 0), MUL)
            link(dve.tensor_tensor(z[1], z[1], ph_of(d, 0), MUL))
            for g2 in range(2):
                for r, op in ((0, SUB), (1, ADD)):
                    half = dict(p0=64 * g2, pn=64)
                    ins = dve.tensor_tensor(
                        v(st[r], (16 * d + g2) * (K5 + 1) + 1 - d, [2 * (K5 + 1), 8], [1, K5], **half),
                        v(tmp, HALF * r + DW * d, [K5, 8], [1, K5], **half),
                        v(wz, HALF * r + DW * d, [K5, 8], [1, K5], **half), op)
            done(ins, "states")

        def gelu_arg():
            dve.wait_ge(sem("y_in"), 16 * G5)
            for m in range(2):
                ins = dve.scalar_tensor_tensor(v(yg, SEQ * m, [1, SEQ]), v(uT, SEQ * m, [1, SEQ]),
                                               pcol(DS + m), v(yT, SEQ * m, [1, SEQ]), MUL, ADD)
            link(ins)
            y, t = v(yg, 0, [1, 2 * SEQ]), v(yT, 0, [1, 2 * SEQ])
            link(dve.tensor_tensor(t, y, y, MUL))
            link(dve.tensor_scalar(t, t, 0.044715, 1.0, MUL, ADD))
            done(dve.tensor_tensor(t, t, y, MUL), "gelu_in")

        def gelu():
            dve.wait_ge(sem("gelu_t"), 1)
            y = v(yg, 0, [1, 2 * SEQ])
            link(dve.scalar_tensor_tensor(y, v(glut, 0, [1, 2 * SEQ]), 1.0, y, ADD, MUL))
            h = v(y_hi, 0, [1, 2 * SEQ])
            link(dve.tensor_scalar(h, y, 0.5, None, MUL))
            done(dve.scalar_tensor_tensor(v(y_lo, 0, [1, 2 * SEQ]), y, 0.5, raw32(h), MUL, SUB), "y_split")

        def take(g):
            kind, m = TILES[g]
            if kind not in BY_DVE:
                return
            src = pv(g % 2, 0, [1, SEQ])
            if kind in ("xat", "nat"):
                dve.wait_ge(sem("o_hi"), m + 1 + (2 if kind == "nat" else 0))
                h_, l_ = (xa_hi, xa_lo) if kind == "xat" else (na_hi, na_lo)
                dve.tensor_tensor(v(l_, SEQ * m, [1, SEQ]), src, raw32(v(h_, SEQ * m, [1, SEQ])), SUB).then_inc(
                    sem("dve_took"), 1)
                return
            dve.wait_ge(sem("tile"), g + 1)
            if kind == "gv":
                dve.wait_ge(sem("act_took"), taken(g - 1)[1])
                i = v(glui, SEQ * m, [1, SEQ])
                dve.scalar_tensor_tensor(i, v(glut, SEQ * m, [1, SEQ]), 1.0, src, ADD, MUL).then_inc(
                    sem("dve_took"), 1)
                dve.wait_ge(sem("dve_took"), taken(g)[1])
                i = v(glui, SEQ * m, [K5, 8], [8, 8], [1, 8])
                o = [[8, 8], [1, 8], [64, 8]]
                link(dve.tensor_scalar(v(s5_hi, SEQ * m, *o), i, 0.5, None, MUL))
                dve.scalar_tensor_tensor(v(s5_lo, SEQ * m, *o), i, 0.5, raw32(v(s5_hi, SEQ * m, *o)), MUL,
                                         SUB).then_inc(sem("s5_lo"), 1)
                return
            turn = ("s5p", "xap", "nap").index(kind)
            dve.wait_ge(sem("act_took"), taken(g_of[(kind[:2] + "g", m)])[1])
            gate, acc = v(gt, SEQ * m, [1, SEQ]), v(merged, SEQ * m, [1, SEQ])
            part = acc if turn == 0 else v(prod, SEQ * (m % 2), [1, SEQ])
            dve.scalar_tensor_tensor(part, gate, 1.0, src, ADD, MUL).then_inc(sem("dve_took"), 1)
            dve.wait_ge(sem("dve_took"), taken(g)[1])
            if turn:
                dve.tensor_tensor(acc, acc, part, ADD).then_inc(sem("prod"), 1)
            else:
                dve.sem_inc(sem("prod"), 1)

        def v_take(j):
            kind, m = turned[j]
            dve.wait_ge(sem("v_turned"), j + 1)
            if kind == "mv":
                ins = dve.tensor_copy(v(vm, P * m, [XAW, 2], [1, P]), pv(6, 0, [P, 2], [1, P]))
            else:
                dve.tensor_copy(v(vw, NAW + P * m, [NAW, 3], [1, P]), pv(6, P, [P, 3], [1, P]))
                dve.tensor_copy(v(vw, P * m, [1, P], pn=64), pv(6, 0, [1, P], pn=64))
                ins = dve.tensor_copy(v(vw, 4 * NAW + P * m, [1, P], pn=64), pv(7, 0, [1, P], pn=64))
            ins.then_inc(sem("v_took"), 1)

        def smax(u):
            na, h, i = unit(u)
            dve.wait_ge(sem("qk"), u + 1)
            mx = v(soft, 8 * (u % 8), [1, 1])
            if na:
                _, n, off = window(i)
                if u >= XAH * NT + 3:
                    dve.wait_ge(sem("exp"), u - 2)
                ins = dve.tensor_tensor_reduce(v(ssb, 256 * (u % 3), [1, n]), pv(2 + u % 2, 0, [1, n]),
                                               v(ez, 256 * h + off, [1, n]), 1.0, -3e38, ADD, ALU.max, mx)
            else:
                ins = dve.tensor_reduce(mx, pv(2 + u % 2, 0, [1, MEM]), AX.X, ALU.max)
            link(ins)
            dve.tensor_scalar(v(soft, 8 * (u % 8) + 1, [1, 1]), mx, -1.0, None, MUL).then_inc(sem("smax"), 1)

        def take_o(u):
            na, h, i = unit(u)
            dve.wait_ge(sem("pv"), u + 1)
            link(dve.reciprocal(v(soft, 8 * (u % 8) + 3, [1, 1]), v(soft, 8 * (u % 8) + 2, [1, 1])))
            dst = v(onat, 512 * i + HD * h, [1, HD]) if na else v(onx, 256 * i + HD * h, [1, HD])
            dve.tensor_scalar(dst, pv(6 + u % 2, 0, [1, HD]), v(soft, 8 * (u % 8) + 3, [1, 1]), None,
                              MUL).then_inc(sem("o_took"), 1)

        def slot(s):
            if s < UNITS:
                smax(s)
            if 0 <= s - 4 < UNITS:
                take_o(s - 4)

        def merged_lo(k):
            dve.wait_ge(sem("m_hi"), k + 1)
            o = [[1, GW], [GW, ROWS]]
            dve.scalar_tensor_tensor(v(m_lo, SEQ * k, *o), v(merged, SEQ * k, [ROWS, GW], [1, ROWS]), 0.5,
                                     raw32(v(m_hi, SEQ * k, *o)), MUL, SUB).then_inc(sem("m_lo"), 1)

        g = 0
        s = 0
        v_at = {C_QX: 0, C_QX + 1: 1, C_V + 1: 2, C_V + 2: 3, C_V + 3: 4}
        for c in range(C_OUT):
            if c in SLOTS:
                slot(s)
                s += 1
            if c in v_at:
                v_take(v_at[c])
            if c == C_GLU:
                v_take(5)
            for kind, _ in tiles_of(c):
                if kind[2:] == "g":
                    for _ in range(SLOTS.get(c, 1) - 1):
                        slot(s)
                        s += 1
                take(g)
                g += 1
            lo(c + 2)
            for k in range(2 * (c - C_NAP) - 2, 2 * (c - C_NAP)):
                if k >= 0:
                    merged_lo(k)
            if c < 2:
                for b in range(KD + 4 * c, KD + 4 * c + 4):
                    turn_lo(b)
            if c == 0:
                disc()
            if c == 6:
                dve.wait_ge(sem("bbar"), 1)
            if c in (6, 7):
                powers_of_b(dve, link, 0, c - 6, junk)
            if c == 7:
                dve.sem_inc(sem("ba_ready"), 1)
            if c in (9, 10):
                rotate_in(c - 9)
            if c == 10:
                scans()
            if c in (11, 12):
                rotate_out(c - 11)
            if c == 16:
                gelu_arg()
            if c == 18:
                gelu()
        for k in range(6, KD):
            merged_lo(k)
        for c in range(C_OUT + 2, NCH):
            lo(c)
        dve.wait_ge(sem("x_again"), 16)
        dve.wait_ge(sem("gf_in"), 16)
        for n in range(NT):
            dve.wait_ge(sem("out_k"), n + 1)
            for half in range(2):
                xs = v(x_sb, D * n + 512 * half, [1, 512])
                ins = dve.tensor_tensor(xs, pv(2 * (n % 2) + half, 0, [1, 512]), xs, ADD)
            ins.then_inc(sem("x2"), 1)
            inverse_root(n + 3, n, 1)
            dve.scalar_tensor_tensor(v(h2, D * n, [1, D]), v(x_sb, D * n, [1, D]), v(stat, 24 + n, [1, 1]),
                                     v(gffb, 0, [1, D]), MUL, MUL).then_inc(sem("h2"), 1)

        lg = v(rt, 0, [20, NT], [1, 20])
        dve.wait_ge(sem("logits"), NT)
        dve.wait_ge(sem("lb_in"), 32)
        link(dve.tensor_tensor(lg, pv(5, 0, [20, NT], [1, 20]), v(lbias, 0, [0, NT], [1, 20]), ADD))
        for j in range(4):
            n = j + 1
            ins = dve.tensor_tensor(v(rt, 80 + j, [16, 20], [4, n]), v(rt, j, [4, 20], [0, n]),
                                    v(rt, 0, [4, 20], [1, n]), ALU.is_gt)
            if n < 4:
                ins = dve.tensor_tensor(v(rt, 80 + 4 * n + j, [16, 20], [4, 4 - n]), v(rt, j, [4, 20], [0, 4 - n]),
                                        v(rt, n, [4, 20], [1, 4 - n]), ALU.is_ge)
        link(ins)
        link(dve.tensor_reduce(v(rt, 400, [1, 80]), v(rt, 80, [4, 80], [1, 4]), AX.X, ADD))
        for j in range(2):
            ins = dve.tensor_scalar(v(rt, 480 + 80 * j, [1, 80]), v(rt, 400, [1, 80]), float(j), None, ALU.is_equal)
        link(ins)
        m = [v(rt, 640 + 64 * j, [1, 64]) for j in range(2)]
        for j in range(2):
            ins = dve.tensor_tensor(v(rt, 640 + 64 * j, [16, NT], [4, 4], [1, 4]),
                                    v(rt, 480 + 80 * j + 4, [20, NT], [4, 4], [1, 4]),
                                    v(rt, 480, [20, NT], [1, 4], [0, 4]), MUL)
        link(ins)
        done(dve.tensor_tensor(v(selb, 0, [1, 64]), m[0], m[1], ADD), "chosen")
        for j in range(2):
            ins = dve.tensor_tensor(v(rt, 768 + 64 * j, [16, NT], [1, 16]), v(rt, 640 + 64 * j, [16, NT], [1, 16]),
                                    v(rt, 4, [20, NT], [1, 16]), MUL)
        ins2 = dve.tensor_reduce(v(rt, 908, [1, NT]), v(rt, 0, [20, NT], [1, 4]), AX.X, ALU.max)
        link(ins2)
        link(dve.tensor_reduce(v(rt, 896, [1, 8]), v(rt, 768, [16, 8], [1, 16]), AX.X, ADD))
        dve.tensor_tensor(v(rt, 960, [4, NT], [1, 4]), v(rt, 0, [20, NT], [1, 4]), v(rt, 908, [1, NT], [0, 4]), SUB)
        done(dve.tensor_tensor(v(rt, 976, [1, NT]), v(rt, 900, [1, NT]), v(rt, 896, [1, NT]), SUB), "route_arg")
        dve.wait_ge(sem("places"), 1)
        dve.wait_ge(sem("iotas"), 1)
        link(dve.scalar_tensor_tensor(v(rt, 768, [16, NT], [1, 16]), pv(6, 0, [16, NT], [1, 16]), float(NE),
                                      v(rt, 1040, [0, NT], [1, 16]), MUL, ADD))
        link(dve.scalar_tensor_tensor(v(rt, 1020, [2, NT], [1, 2]), v(rt, 768, [16, NT], [1, 2]), 1.0,
                                      v(selb, 0, [16, NT], [1, 2]), ADD, MUL))
        for e in range(2):
            for n in range(NT):
                ins = dve.tensor_scalar(v(hot, P * (NT * e + n), [1, P]), v(slots, P * e, [1, P]),
                                        v(rt, 1020 + 2 * n + e, [1, 1]), None, ALU.is_equal)
        ins.then_inc(sem("hot"), 1)
        for j in range(2):
            ins = dve.tensor_tensor(v(rt, 480 + 64 * j, [1, 64]), m[j], v(rt, 768, [1, 64]), MUL)
        link(ins)
        link(dve.tensor_reduce(v(rt, 1000, [1, 8]), v(rt, 480, [16, 8], [1, 16]), AX.X, ADD))
        done(dve.tensor_copy(v(rowi, 0, [1, 8]), v(rt, 1000, [1, 8])), "rows")
        dve.wait_ge(sem("hot_used"), 1)
        dve.tensor_copy(v(idx01, 0, [1, 2]), pv(7, 0, [1, 2])).then_inc(sem("idx01"), 1)
        link(dve.tensor_reduce(v(rt, 1010, [1, 1]), pv(6, 64, [1, 16]), AX.X, ALU.max))
        done(dve.tensor_scalar(v(flag, 0, [1, 1]), v(rt, 1010, [1, 1]), float(CAP), None, ALU.is_gt), "flag")
        dve.wait_ge(sem("route_exp"), 1)
        dve.tensor_reduce(v(rt, 1012, [1, NT]), v(rt, 960, [4, NT], [1, 4]), AX.X, ADD)
        link(dve.tensor_scalar(v(rt, 1016, [1, NT]), v(rt, 976, [1, NT]), 1.0, None, ADD))
        link(dve.tensor_tensor(v(rt, 1012, [1, NT]), v(rt, 1012, [1, NT]), v(rt, 1016, [1, NT]), MUL))
        link(dve.reciprocal(v(wts, 0, [1, NT]), v(rt, 1012, [1, NT])))
        link(dve.tensor_tensor(v(wts, 4, [1, NT]), v(wts, 0, [1, NT]), v(rt, 976, [1, NT]), MUL))

        def unit_lo(n, j, dst):
            dve.wait_ge(sem("e_hi_done"), n + 1)
            dve.tensor_tensor(v(e_lo[dst], 0, [1, 2048]), v(eraw, 2048 * j, [1, 2048]),
                              raw32(v(e_hi[dst], 0, [1, 2048])), SUB).then_inc(sem("e_lo_done"), 1)

        def xt_rest(e):
            for j in range(2):
                dve.wait_ge(sem("xt_hi"), 2 * e + j + 1)
                dve.tensor_tensor(v(xt_lo, 512 * j, [1, 512]), pv(4 + j, 0, [1, 512]),
                                  raw32(v(xt_hi, 512 * j, [1, 512])), SUB).then_inc(sem("xt_lo"), 1)

        def step(e0, i=None):
            peeled = i is None
            i = 0 if peeled else i
            e, odd = 6 * i + e0, e0 % 2 == 1
            n0 = 3 * e0 + 2
            if not peeled or e >= 1:
                dve.wait_ge(sem("at_hi"), e)
                dve.tensor_tensor(v(at_lo, 0, [1, 256]), pv(6, 0, [1, 256]), raw32(v(at_hi, 0, [1, 256])),
                                  SUB).then_inc(sem("at_lo"), 1)
            if not peeled or e < 15:
                unit_lo(3 * e + 2, n0 % EU, 2)
            if not peeled or e < 16:
                b = 1 if odd else 0
                dve.wait_ge(sem("tanh"), e + 1)
                dve.scalar_tensor_tensor(v(act_s, 0, [1, FF]), v(act_t, 0, [1, FF]), 1.0, pv(b, 0, [1, FF]),
                                         ADD, MUL).then_inc(sem("act_s"), 1)
                dve.wait_ge(sem("act_s"), e + 1)
                dve.scalar_tensor_tensor(v(act_a, 0, [1, FF]), v(act_s, 0, [1, FF]), 0.5, pv(b, FF, [1, FF]),
                                         MUL, MUL).then_inc(sem("act_a"), 1)
            if not peeled or e < 15:
                xt_rest(e + 1)
                unit_lo(3 * e + 3, (n0 + 1) % EU, 0)
                unit_lo(3 * e + 4, (n0 + 2) % EU, 1)
            elif e == 15:
                unit_lo(47, 47 % EU, 2)
            if not peeled or e >= 1:
                dve.wait_ge(sem("e_used"), 48 if peeled and e == 16 else 3 * e + 2)
                if not peeled or e >= 3:
                    dve.wait_ge(sem(f"y_st{0 if odd else 1}"), 16 * (3 * i + (e0 - 1) // 2))
                dve.tensor_copy(v(ysb, 512 + (0 if odd else D), [1, 512]), pv(3, 0, [1, 512])).then_inc(
                    sem("y_d"), 1)

        unit_lo(0, 0, 0)
        unit_lo(1, 1, 1)
        xt_rest(0)
        for e in range(3):
            step(e)
        with dve.Fori(0, 2) as i:
            for e0 in range(3, 9):
                step(e0, i)
        step(15)
        step(16)

        with dve.If(needed(dve)):
            with dve.Fori(0, 3) as j:
                with dve.Fori(0, NE) as e:
                    it = NE * j + e + 1
                    dve.wait_ge(sem("ov_tanh"), it)
                    dve.scalar_tensor_tensor(v(act_s, 0, [1, FF]), v(act_t, 0, [1, FF]), 1.0, pv(0, 0, [1, FF]),
                                             ADD, MUL).then_inc(sem("ov_s"), 1)
                    dve.wait_ge(sem("ov_s"), it)
                    dve.scalar_tensor_tensor(v(act_a, 0, [1, FF]), v(act_s, 0, [1, FF]), 0.5,
                                             pv(0, FF, [1, FF]), MUL, MUL).then_inc(sem("ov_a"), 1)

        dve.wait_ge(sem("gfin_in"), 16)

        for n in range(NT):
            xs = v(x_sb, D * n, [1, D])
            dve.wait_ge(sem(f"yg{n}"), 32)
            link(dve.scalar_tensor_tensor(xs, v(y0, D * n, [1, D]), v(wts, n, [1, 1]), xs, MUL, ADD))
            dve.scalar_tensor_tensor(xs, v(y1, D * n, [1, D]), v(wts, 4 + n, [1, 1]), xs, MUL, ADD).then_inc(
                sem("x2"), 1)
        inverse_root(NT + 3, 0, NT)
        for n in range(NT):
            xs = v(x_sb, D * n, [1, D])
            dve.scalar_tensor_tensor(xs, xs, v(stat, 24 + n, [1, 1]), v(gfin, 0, [1, D]), MUL, MUL).then_inc(
                sem("out_ready"), 1)

    @block.tensor
    def _(pe):
        def split(dst, w, x, first, last):
            pe.matmul(dst, w[0], x[0], start=first, stop=False)
            pe.matmul(dst, w[0], x[1], start=False, stop=False)
            return pe.matmul(dst, w[1], x[0], start=False, stop=last)

        pe.wait_ge(sem("consts"), 1)
        pe.wait_ge(sem("prm_ready"), 1)
        pe.transpose(pv(0, 0, [1, 98]), v(prm, 0, [1, P], pn=98), v(ident, 0, [1, 98], pn=98)).then_inc(
            sem("prm_turned"), 1)
        def turn(b):
            pe.wait_ge(sem("normed"), NT if b < KD else NT + 2)
            if b >= 4:
                pe.wait_ge(sem("turn_lo"), b - 3)
            for n in range(NT if b < KD else 2):
                src = v(x_sb, D * n + P * b, [1, P]) if b < KD else v(mem_sb, D * n + P * (b - KD), [1, P])
                ins = pe.transpose(pv(4 + b % 4, P * n, [1, P]), src, v(ident, 0, [1, P]))
            ins.then_inc(sem("turned"), 1)

        def product(g, c, s=0):
            kind, m = TILES[g]
            if g >= 2:
                wait_taken(pe, g - 2)
            w0 = 1024 * (c % HL)
            ws = (w_hi, w_lo)
            if kind in ("xat", "nat"):
                src, step = (onx, 256) if kind == "xat" else (onat, 512)
                if m == 0:
                    pe.wait_ge(sem("o_took"), XAH * NT if kind == "xat" else UNITS)
                for n in range(NT):
                    ins = pe.transpose(pv(g % 2, P * n, [1, P]), v(src, step * n + P * m, [1, P]),
                                       v(ident, 0, [1, P]))
                ins.then_inc(sem("tile"), 1)
                return
            xs, n, wk, wcol = (h_hi, h_lo), SEQ, P, 0
            ks = KD
            if kind in ("mk", "mv"):
                xs, n = (mm_hi, mm_lo), MEM
            elif kind in ("gt", "gv"):
                xs, ks, wk, wcol = (y_hi, y_lo), 2, 512, P * (m + (2 if kind == "gt" else 0))
            elif kind in ("s5p", "xap"):
                if kind == "xap" and m == 0:
                    wait_taken(pe, g_of["xat", 1])
                xs, ks, wk, wcol = ((s5_hi, s5_lo) if kind == "s5p" else (xa_hi, xa_lo)), 2, 512, P * (m % 4)
            elif kind == "nap":
                if m == 0:
                    wait_taken(pe, g_of["nat", 3])
                xs, ks, wk, wcol = (na_hi, na_lo), 4, 256, P * (m % 2)
            for k in range(ks):
                n_slots = SLOTS.get(c, 0)
                if n_slots == 2 and k == 4 or n_slots == 3 and k in (3, 6):
                    slot(s)
                    s += 1
                ins = split(pv(g % 2, 0, [1, n]), [v(w, w0 + wk * k + wcol, [1, P]) for w in ws],
                            [v(x, n * k, [1, n]) for x in xs], k == 0, k == ks - 1)
            ins.then_inc(sem("tile"), 1)

        def s5_matrices():
            pe.wait_ge(sem("v_took"), 2)
            pe.wait_ge(sem("ba_ready"), 1)
            pe.wait_ge(sem("ba_back"), 1)
            for q in range(8):
                if q >= 4:
                    pe.wait_ge(sem("bat_took"), q - 3)
                for j in range(4):
                    ins = pe.transpose(pv(4 + q % 4, P * j, [1, P]), v(ba, 512 * q + P * j, [1, P]),
                                       v(ident, 0, [1, P]))
                ins.then_inc(sem("ba_turned"), 1)
            pe.wait_ge(sem("ct_ready"), 2)
            for dp in range(DP):
                for ri in range(2):
                    ins = pe.matmul(pv(2, 32 * dp, [1, 32]), v(ba, 2048 * ri + P * dp, [1, P]),
                                    v(ctb, 512 * ri + 32 * dp, [1, 32]), start=ri == 0, stop=ri == 1)
            ins.then_inc(sem("lags"), 1)
            pe.wait_ge(sem("lags_took"), 1)
            pe.wait_ge(sem("bat_took"), 8)
            for t in range(T5):
                for d, o in ((0, 112 + 16 * (7 - t)), (1, 112 - 16 * t)):
                    ins = pe.matmul(pv(4 + t // 2, 256 * (t % 2), [1, 256]), v(wide, o, [1, P]),
                                    v(stk, 256 * d, [1, 256]), start=d == 0, stop=d == 1)
                if t % 2:
                    ins.then_inc(sem("shifted"), 1)

        def s5_inputs():
            pe.wait_ge(sem("mg_took"), 4)
            pe.wait_ge(sem("u_in"), 16 * T5)
            for d in range(2):
                for ri in range(2):
                    for p in range(8):
                        for g2 in range(2):
                            ins = pe.matmul(pv(4 + 2 * d + ri, K5 * p, [1, K5], p0=64 * g2, pn=64),
                                            v(bat, 2048 * ri + P * (8 * d + p) + 64 * g2, [1, 64]),
                                            v(upk, K5 * (2 * p + g2), [1, K5]), start=True, stop=True)
                    ins.then_inc(sem("w5"), 1)

        def s5_outputs():
            pe.wait_ge(sem("states"), 2)
            pe.wait_ge(sem("ca_ready"), 1)
            for p in range(8):
                b, o = 2 + p // 4, P * (p % 4)
                for d in range(2):
                    for r in range(2):
                        pe.matmul(pv(b, o, [K5, 2], [1, K5]), v(ca, 2048 * r + P * (8 * d + p), [1, P]),
                                  v(st[r], (8 * d + p) * 2 * (K5 + 1) + d, [K5 + 1, 2], [1, K5]),
                                  start=d == 0 and r == 0, stop=False)
                for g2 in range(2):
                    ins = pe.matmul(pv(b, o + K5 * g2, [1, K5]), v(mg, P * (2 * p + g2), [1, P]),
                                    v(upk, K5 * (2 * p + g2), [1, K5]), start=False, stop=g2 == 1)
                if p % 4 == 3:
                    ins.then_inc(sem("s5_y"), 1)

        def turn_values(j):
            kind, m = turned[j]
            pe.wait_ge(sem("act_took"), taken(g_of[turned[j]])[1])
            if j:
                pe.wait_ge(sem("v_took"), j)
            if kind == "mv":
                for w in range(2):
                    ins = pe.transpose(pv(6, P * w, [1, P]), v(vt, SEQ * (j % 2) + P * w, [1, P]),
                                       v(ident, 0, [1, P]))
            else:
                for w in range(5):
                    a0, a1 = max(0, P * w - 64), min(SEQ, P * w + 64)
                    ins = pe.transpose(pv(7 if w == 4 else 6, 0 if w == 4 else P * w, [1, P], pn=a1 - a0),
                                       v(vt, SEQ * (j % 2) + a0, [1, a1 - a0]), v(ident, 0, [1, P]))
            ins.then_inc(sem("v_turned"), 1)

        def scores(u):
            na, h, i = unit(u)
            if u >= 2:
                pe.wait_ge(sem("exp"), u - 1)
            lo64, pn = 64 * (h % 2), 64
            if na:
                if u == XAH * NT:
                    pe.wait_ge(sem("masks"), 1)
                w0, n, off = window(i)
                kind = 0 if i == 0 else 2 if i == NT - 1 else 1
                dst = pv(2 + u % 2, 0, [1, n])
                pe.matmul(dst, v(identb, 0, [1, P]), v(maskb, 256 * kind + off, [1, n]), start=True, stop=False)
                pe.matmul(dst, v(qT, SEQ * (h // 2) + P * i, [1, P], p0=lo64, pn=pn),
                          v(kT, SEQ * (h // 2) + w0, [1, n], p0=lo64, pn=pn), start=False, stop=True).then_inc(
                              sem("qk"), 1)
            else:
                pe.matmul(pv(2 + u % 2, 0, [1, MEM]), v(qxT, SEQ * (h // 2) + P * i, [1, P], p0=lo64, pn=pn),
                          v(kmT, MEM * (h // 2), [1, MEM], p0=lo64, pn=pn), start=True, stop=True).then_inc(
                              sem("qk"), 1)

        def chunks_of(u):
            na, h, i = unit(u)
            return key_chunks(i) if na else [(0, P, 0), (1, P, P)]

        def turn_p(u):
            pe.wait_ge(sem("exp"), u + 1)
            if u >= 2:
                pe.wait_ge(sem("p_taken"), u - 1)
            for k, (_, n, a0) in enumerate(chunks_of(u)):
                ins = pe.transpose(pv(4 + u % 2, P * k, [1, P], pn=n), v(pr, 256 * (u % 3) + a0, [1, n]),
                                   v(ident, 0, [1, P]))
            ins.then_inc(sem("p_turned"), 1)

        def weighted(u):
            na, h, i = unit(u)
            pe.wait_ge(sem("p_taken"), u + 1)
            if u >= 2:
                pe.wait_ge(sem("o_took"), u - 1)
            for k, (w, n, _) in enumerate(chunks_of(u)):
                vals = v(vw, NAW * w + HD * h, [1, HD], pn=n) if na else v(vm, XAW * w + HD * h, [1, HD])
                ins = pe.matmul(pv(6 + u % 2, 0, [1, HD]), v(pts, 256 * (u % 2) + P * k, [1, P], pn=n), vals,
                                start=k == 0, stop=k == 1)
            ins.then_inc(sem("pv"), 1)

        def slot(s):
            if s < UNITS:
                scores(s)
            if 0 <= s - 2 < UNITS:
                turn_p(s - 2)
            if 0 <= s - 4 < UNITS:
                weighted(s - 4)

        for b in range(KD):
            turn(b)
        pe.wait_ge(sem("c_in"), 64)
        for ri in range(2):
            for h in range(4):
                ins = pe.transpose(pv(2 + ri, P * h, [1, P]), v(cn, 512 * ri + P * h, [1, P]), v(ident, 0, [1, P]))
            ins.then_inc(sem("c_turned"), 1)
        pe.wait_ge(sem("turn_lo"), KD)
        g = s = 0
        for c in range(C_OUT):
            if c == C_MEMK:
                pe.wait_ge(sem("turn_lo"), 2 * KD)
            if c == C_GLU:
                turn_values(5)
                pe.wait_ge(sem("y_split"), 1)
            if c == C_S5P:
                pe.wait_ge(sem("s5_lo"), 2)
            if c == C_S5G:
                pe.wait_ge(sem("v_took"), 6)
            if c in SLOTS:
                slot(s)
                s += 1
            pe.wait_ge(sem("w_lo_done"), c + 1)
            for _ in tiles_of(c):
                product(g, c, s)
                g += 1
            s += max(0, SLOTS.get(c, 0) - 1)
            if c in (C_MEMV + 1, C_QX):
                turn_values(c - C_MEMV - 1)
            if C_V < c < C_GLU:
                turn_values(c - C_V + 1)
            if c == 3:
                pe.wait_ge(sem("rpb_in"), 16 * 16)
                for q in range(4):
                    if q >= 2:
                        pe.wait_ge(sem("bias_ready"), q - 1)
                    pe.matmul(pv(4 + q % 2, 0, [1, 512]), v(flip, 0, [1, P]), v(ezraw, 512 * q, [1, 512]),
                              start=True, stop=True).then_inc(sem("flipped"), 1)
            if c < 2:
                for b in range(KD + 4 * c, KD + 4 * c + 4):
                    turn(b)
            if c == 8:
                pe.wait_ge(sem("bias_ready"), 4)
                s5_matrices()
            if c == 9:
                s5_inputs()
            if c == 14:
                s5_outputs()

        def out_tile(n):
            for c in range(C_OUT, NCH):
                half, kp = divmod(c - C_OUT, 4)
                if n == 0:
                    pe.wait_ge(sem("w_lo_done"), c + 1)
                h_, l_, o = parts_of(c)
                for kk in range(2):
                    k = 2 * kp + kk
                    if n == 0:
                        pe.wait_ge(sem("m_lo"), k + 1)
                    if k == 0 and n >= 2:
                        pe.wait_ge(sem("x2"), n - 1)
                    ins = split(pv(2 * (n % 2) + half, 0, [1, 512]),
                                [v(x, SEQ * k + P * n, [1, P]) for x in (m_hi, m_lo)],
                                [v(w, o + 512 * kk, [1, 512]) for w in (h_, l_)], k == 0, k == KD - 1)
            ins.then_inc(sem("out_k"), 1)

        def h2_turn(n):
            pe.wait_ge(sem("h2"), n + 1)
            for j in range(2):
                if n:
                    pe.wait_ge(sem("h2_took"), 2 * n)
                for b in range(4):
                    ins = pe.transpose(pv(H2_BANK[j], P * b, [1, P]), v(h2, D * n + P * (4 * j + b), [1, P]),
                                       v(ident, 0, [1, P]))
                ins.then_inc(sem("h2_turned"), 1)

        def logits(n):
            pe.wait_ge(sem("h2_took"), 2 * n + 2)
            for k in range(KD):
                ins = pe.matmul(pv(5, 20 * n, [1, 20]), v(h2T, SEQ * k + P * n, [1, P]), v(wcf, 20 * k, [1, 20]),
                                start=k == 0, stop=k == KD - 1)
            ins.then_inc(sem("logits"), 1)

        wait_taken(pe, len(TILES) - 2)
        wait_taken(pe, len(TILES) - 1)
        out_tile(0)
        out_tile(1)
        h2_turn(0)
        out_tile(2)
        h2_turn(1)
        pe.wait_ge(sem("wcf_in"), 32)
        logits(0)
        out_tile(3)
        h2_turn(2)
        logits(1)
        logits(2)
        h2_turn(3)
        logits(3)
        pe.wait_ge(sem("chosen"), 1)
        pe.matmul(pv(6, 0, [1, 64]), v(upper, 0, [1, P]), v(selb, 0, [1, 64]), start=True, stop=False)
        for q in range(1, NT):
            pe.matmul(pv(6, 16 * q, [1, 64 - 16 * q]), v(onesb, 0, [1, P]), v(selb, 0, [1, 64 - 16 * q]),
                      start=False, stop=q == NT - 1)
        for n in range(NT):
            ins = pe.matmul(pv(6, 64, [1, 16]), v(onesb, 0, [1, P]), v(selb, 16 * n, [1, 16]),
                            start=n == 0, stop=n == NT - 1)
        ins.then_inc(sem("places"), 1)
        pe.wait_ge(sem("hot"), 1)
        for e in range(2):
            for n in range(NT):
                ins = pe.matmul(pv(7, e, [1, 1]), v(hot, P * (NT * e + n), [1, P]), v(tokf, n, [1, 1]),
                                start=n == 0, stop=n == NT - 1)
        ins.then_inc(sem("hot_used"), 1)

        def tokens(e, slot, gathered):
            pe.wait_ge(sem(f"xg{slot}"), gathered)
            if not (isinstance(e, int) and e == 0):
                pe.wait_ge(sem("xt_lo"), 2 * e)
            for j in range(2):
                for k in range(4):
                    ins = pe.transpose(pv(4 + j, P * k, [1, P]), v(xg, D * slot + 512 * j + P * k, [1, P]),
                                       v(ident, 0, [1, P]))
                ins.then_inc(sem("xt"), 1)

        def gate_up(e, n, half, s3, odd):
            pe.wait_ge(sem("e_lo_done"), n + 1)
            for k in range(4):
                kk = 4 * half + k
                ins = split(pv(1 if odd else 0, 0, [1, 512]), [v(x, P * kk, [1, P]) for x in (xt_hi, xt_lo)],
                            [v(w[s3], 512 * k, [1, 512]) for w in (e_hi, e_lo)], kk == 0, kk == KD - 1)
            ins.then_inc(sem("e_used"), 1)

        def step(e0, i=None):
            peeled = i is None
            i = 0 if peeled else i
            e, odd = 6 * i + e0, e0 % 2 == 1
            first = peeled and e == 0
            if not peeled or e < 16:
                if first:
                    pe.wait_ge(sem("xt_lo"), 2)
                else:
                    pe.wait_ge(sem("xt_lo"), 2 * e + 2)
                    if not peeled or e >= 2:
                        pe.wait_ge(sem("act_a"), e - 1)
                gate_up(e, 0 if first else 3 * e - 1, 0, 0 if first else 2, odd)
            if not first:
                pe.wait_ge(sem("act_a"), e)
                if not peeled or e >= 2:
                    pe.wait_ge(sem("at_lo"), e - 1)
                for k in range(2):
                    ins = pe.transpose(pv(6, P * k, [1, P]), v(act_a, P * k, [1, P]), v(ident, 0, [1, P]))
                ins.then_inc(sem("at"), 1)
            if not peeled or e < 16:
                gate_up(e, 1 if first else 3 * e, 1, 1 if first else 0, odd)
            if not peeled or e < 15:
                tokens(e + 1, (e0 + 1) % 3, 16 * (2 * i + (e0 + 1) // 3 + 1))
            if not first:
                last = peeled and e == 16
                pe.wait_ge(sem("e_lo_done"), 48 if last else 3 * e + 2)
                pe.wait_ge(sem("at_lo"), e)
                if not peeled or e >= 2:
                    pe.wait_ge(sem("y_a"), e - 1)
                    pe.wait_ge(sem("y_d"), e - 1)
                s3 = 2 if last else 1
                for n in range(2):
                    for k in range(2):
                        ins = split(pv(2 + n, 0, [1, 512]), [v(x, P * k, [1, P]) for x in (at_hi, at_lo)],
                                    [v(w[s3], D * k + 512 * n, [1, 512]) for w in (e_hi, e_lo)], k == 0, k == 1)
                ins.then_inc(sem("e_used"), 1)

        pe.wait_ge(sem("rows"), 1)
        tokens(0, 0, 16)
        for e in range(3):
            step(e)
        with pe.Fori(0, 2) as i:
            for e0 in range(3, 9):
                step(e0, i)
        step(15)
        step(16)

        with pe.If(needed(pe)):
            with pe.Fori(0, 3) as j:
                with pe.Fori(0, NE) as e:
                    it = NE * j + e + 1
                    pe.wait_ge(sem("ov_g"), 16 * it)
                    for k in range(KD):
                        ins = pe.transpose(pv(4 + k // 4, P * (k % 4), [1, P]), v(xg, P * k, [1, P]),
                                           v(ident, 0, [1, P]))
                    ins.then_inc(sem("ov_xt"), 1)
                    pe.wait_ge(sem("ov_x"), it)
                    pe.wait_ge(sem("ov_in"), 96 * it)
                    for k in range(KD):
                        ins = pe.matmul(pv(0, 0, [1, 512]), v(xtf, P * k, [1, P]), v(eraw, 512 * k, [1, 512]),
                                        start=k == 0, stop=k == KD - 1)
                    ins.then_inc(sem("ov_gu"), 1)
                    pe.wait_ge(sem("ov_a"), it)
                    for k in range(2):
                        ins = pe.transpose(pv(6, P * k, [1, P]), v(act_a, P * k, [1, P]), v(ident, 0, [1, P]))
                    ins.then_inc(sem("ov_at"), 1)
                    pe.wait_ge(sem("ov_ac"), it)
                    for n in range(2):
                        for k in range(2):
                            ins = pe.matmul(pv(2 + n, 0, [1, 512]), v(atf, P * k, [1, P]),
                                            v(eraw, 4096 + D * k + 512 * n, [1, 512]), start=k == 0, stop=k == 1)
                    ins.then_inc(sem("ov_down"), 1)
                    pe.wait_ge(sem("ov_y"), it)

    @block.gpsimd
    def _(pool):
        count = [0]

        def link(ins):
            ins.then_inc(sem("pool_chain"), 1)
            count[0] += 1
            pool.wait_ge(sem("pool_chain"), count[0])

        def one_where(t, cols, base_):
            return pool.affine_select(out=v(t, 0, [1, cols]), in_=v(t, 0, [1, cols]), compare_op=ALU.not_equal,
                                      fill=1.0, base=base_, pattern=[[-1, cols]], channel_multiplier=1)

        pool.memset(v(ident, 0, [1, P]), 0.0)
        pool.memset(v(identb, 0, [1, P]), 0.0)
        pool.memset(v(wide, 0, [1, 352]), 0.0)
        pool.memset(v(ctb, 0, [1, 2 * DP * 32]), 0.0)
        pool.memset(v(flip, 0, [1, P]), 0.0)
        pool.memset(v(maskb, 0, [1, 768]), 0.0)
        pool.memset(v(upper, 0, [1, P]), 1.0)
        pool.memset(v(onesb, 0, [1, P]), 1.0)
        pool.memset(v(zi, 0, [1, 64]), 0)
        link(pool.memset(v(ezraw, 0, [1, NAH * 256]), 0.0))
        one_where(ident, P, 0)
        one_where(identb, P, 0)
        one_where(wide, 352, 112)
        pool.affine_select(out=v(flip, 0, [1, P]), in_=v(flip, 0, [1, P]), compare_op=ALU.not_equal, fill=1.0,
                           base=1 - P, pattern=[[1, P]], channel_multiplier=1).then_inc(sem("consts"), 1)
        pool.dma_start(tok_dram.rearrange("(p n) o -> p (n o)", p=P), v(zi, 0, [1, 64])).then_inc(sem("tok_zero"), 16)
        rpb = a["na_rpb"][0]
        for q in range(16):
            m0, m1 = max(0, q - 7), min(31, q + 23)
            n = 7 * RPB_C + m1 - m0 + 1
            src = bass.AP(tensor=rpb.tensor, offset=rpb.offset + m0 - q + 7,
                          ap=[[RPB_C, 8], [RPB_R * RPB_C, NAH], [1, n]])
            pool.dma_start(v(ezraw, m0, [256, NAH], [1, n], p0=120 - 8 * q, pn=8), src).then_inc(sem("rpb_in"), 16)
        link(pool.affine_select(out=v(upper, 0, [1, P]), in_=v(upper, 0, [1, P]), compare_op=ALU.is_gt, fill=0.0,
                                base=0, pattern=[[1, P]], channel_multiplier=-1))

        def mask(kind, p0, pn, step, cm, base_):
            t = v(maskb, 256 * kind, [8, 32], [1, 8], p0=p0, pn=pn)
            link(pool.affine_select(out=t, in_=t, compare_op=ALU.is_ge, fill=-1e30, base=base_ + cm * p0,
                                    pattern=[[step, 32], [0, 8]], channel_multiplier=cm))

        for kind, p0, pn in ((0, 64, 64), (1, 0, P), (2, 0, 64)):
            mask(kind, p0, pn, 8, -1, 7)
            mask(kind, p0, pn, -8, 1, 120)
        for kind, p0, pn in ((0, 0, 64), (2, 64, 64)):
            mask(kind, p0, pn, 8, 0, -64)
            mask(kind, p0, pn, -8, 0, 184)
        pool.sem_inc(sem("masks"), 1)

        pool.wait_ge(sem("disc"), 1)
        pool.tensor_copy(s5(18), s5(7))
        link(pool.tensor_copy(s5(19), s5(6)))
        for _ in range(3):
            square(pool, link)
        for n in (1, 2, 4):
            cmul(pool, link, power(n + 1, n), power(1, n),
                 [v(pw, PW * r + DP * n, [0, n], [1, DP]) for r in range(2)],
                 [v(pjunk, 256 * j, [DP, n], [1, DP]) for j in range(2)])
        pool.wait_ge(sem("b_in"), 32)
        cmul(pool, link, [v(bb, 512 + 256 * r, [16, DP], [1, 16]) for r in range(2)],
             [v(bb, 256 * r, [16, DP], [1, 16]) for r in range(2)],
             [v(s5s, DP * (10 + r), [1, DP], [0, 16]) for r in range(2)],
             [v(pjunk, 256 * r, [16, DP], [1, 16]) for r in range(2)])
        pool.sem_inc(sem("bbar"), 1)
        for h in range(2):
            powers_of_b(pool, link, 1, h, pjunk)
        pool.sem_inc(sem("ba_back"), 1)
        ph = DP * K5
        for r in range(2):
            ins = pool.memset(v(phase, ph * r, [K5, DP], [1, 1]), 1.0 - r)
        link(ins)
        n = 1
        while n < K5:
            cmul(pool, link, [v(phase, ph * r + n, [K5, DP], [1, n]) for r in range(2)],
                 [v(phase, ph * r, [K5, DP], [1, n]) for r in range(2)],
                 [v(s5s, DP * (18 + r), [1, DP], [0, n]) for r in range(2)],
                 [v(pjunk, 512 * r, [n, DP], [1, n]) for r in range(2)])
            n *= 2
            if n < K5:
                square(pool, link)
        pool.sem_inc(sem("phases"), 1)
        pool.wait_ge(sem("ba_ready"), 1)
        pool.wait_ge(sem("lags"), 1)
        pool.tensor_copy(v(decay, 0, [K5, DP], [1, K5]), v(s5s, DP * 5, [1, DP], [0, K5]))
        pool.memset(v(st[0], 0, [1, 2 * DP * (K5 + 1)]), 0.0)
        link(pool.memset(v(st[1], 0, [1, 2 * DP * (K5 + 1)]), 0.0))
        pool.memset(v(decay, 0, [K5, 8]), 0.0)
        link(pool.memset(v(decay, 8 * K5 + K5 - 1, [K5, 8]), 0.0))
        pool.sem_inc(sem("decays"), 1)

        pool.wait_ge(sem("bias_ready"), 4)

        pool.wait_ge(sem("ct_ready"), 2)
        pool.wait_ge(sem("w5"), 4)
        for d in range(2):
            o = [v(ca, 2048 * r + 1024 * d, [P, 8], [16, 8], [1, 16]) for r in range(2)]
            t = [v(pt5, 1024 * r, [P, 8], [16, 8], [1, 16]) for r in range(2)]
            x = [v(pw, PW * r + (DP if d == 0 else 8 * DP) + 8 * d, [1, 8], [DP if d == 0 else -DP, 8], [0, 16])
                 for r in range(2)]
            y = [v(ct, 256 * part + P * d, [16, 8], [0, 8], [1, 16]) for part in range(3)]
            pool.tensor_tensor(o[0], x[0], y[0], MUL)
            pool.tensor_tensor(t[0], x[1], y[2], MUL)
            pool.tensor_tensor(o[1], x[0], y[2], MUL)
            link(pool.tensor_tensor(t[1], x[1], y[0], MUL))
            pool.tensor_tensor(o[0], o[0], t[0], ADD)
            link(pool.tensor_tensor(o[1], o[1], t[1], SUB))
        pool.sem_inc(sem("ca_ready"), 1)

        for n in range(NT):
            pool.wait_ge(sem("h2"), n + 1)
            pool.dma_start(h2_dram[P * n:P * n + P, :], v(h2, D * n, [1, D])).then_inc(sem("h2_out"), 16)
        pool.wait_ge(sem("out_k"), NT)
        pool.iota(v(toki, 0, [1, NT]), pattern=[[P, NT]], base=0, channel_multiplier=1)
        link(pool.iota(v(idx, 0, [1, NE]), pattern=[[1, NE]], base=0, channel_multiplier=0))
        link(pool.iota(v(slotsi, 0, [1, 2 * P]), pattern=[[1, 2], [NE, P]], base=1, channel_multiplier=0))
        pool.tensor_copy(v(slots, 0, [1, 2 * P]), v(slotsi, 0, [1, 2 * P]))
        pool.tensor_copy(v(tokf, 0, [1, NT]), v(toki, 0, [1, NT]))
        pool.tensor_copy(v(rt, 1040, [1, NE]), v(idx, 0, [1, NE])).then_inc(sem("iotas"), 1)
        def gather(e):
            rows = v(idx if e > 1 else idx01, e, [1, 1])
            pool.indirect_dma_start(out=v(xg, D * (e % 3), [1, D]), out_offset=None, in_=h2_dram,
                                    in_offset=bass.IndirectOffsetOnAxis(ap=rows, axis=0)).then_inc(
                                        sem(f"xg{e % 3}"), 16)

        pool.wait_ge(sem("h2_out"), 16 * NT)
        pool.wait_ge(sem("idx01"), 1)
        gather(0)
        gather(1)
        pool.wait_ge(sem("rows"), 1)
        pool.wait_ge(sem("tok_zero"), 16)
        for n in range(NT):
            for j in range(2):
                pool.indirect_dma_start(
                    out=tok_dram, out_offset=bass.IndirectOffsetOnAxis(ap=v(rowi, 4 * j + n, [1, 1]), axis=0),
                    in_=v(toki, n, [1, 1]), in_offset=None).then_inc(sem("scattered"), 16)
        pool.wait_ge(sem("scattered"), 16 * 8)
        pool.wait_ge(sem("iotas"), 1)
        pool.dma_start(v(idx, 0, [1, NE]), tok_dram.rearrange("(s e) o -> s (e o)", e=NE)[0:P, :]).then_inc(
            sem("idx_in"), 16)
        pool.wait_ge(sem("idx_in"), 16)
        gather(2)
        for e in range(NE):
            if e + 3 < NE:
                pool.wait_ge(sem("xt"), 2 * e + 2)
                gather(e + 3)
            if e >= 1:
                store_y(pool, e - 1)
        store_y(pool, NE - 1)
        for b in range(2):
            pool.wait_ge(sem(f"y_st{b}"), 16 * 8)

        def last_gathers(src):
            for n in range(NT):
                for j, dst in enumerate((y0, y1)):
                    pool.indirect_dma_start(out=v(dst, D * n, [1, D]), out_offset=None, in_=src,
                                            in_offset=bass.IndirectOffsetOnAxis(ap=v(rowi, 4 * j + n, [1, 1]),
                                                                                axis=0)).then_inc(sem(f"yg{n}"), 16)

        with pool.If(needed(pool)):
            pool.dma_start(ya_dram[0:CAP * NE, :], ye_dram).then_inc(sem("ya_main"), 16)
            with pool.Fori(0, 3) as j:
                with pool.Fori(0, NE) as e:
                    it = NE * j + e + 1
                    pool.dma_start(v(idxo, 0, [1, 1]),
                                   tok_dram.rearrange("(j p e) o -> j p (e o)", p=P, e=NE)
                                   [bass.ds(j + 1, 1), :, bass.ds(e, 1)].rearrange("a p e -> p (a e)"),
                                   allow_slow_non_contiguous=True).then_inc(
                                       sem("ov_idx"), 16)
                    pool.wait_ge(sem("ov_idx"), 16 * it)
                    pool.sem_inc(sem("ov_turn"), 1)
                    pool.indirect_dma_start(out=v(xg, 0, [1, D]), out_offset=None, in_=h2_dram,
                                            in_offset=bass.IndirectOffsetOnAxis(ap=v(idxo, 0, [1, 1]),
                                                                                axis=0)).then_inc(sem("ov_g"), 16)
                    pool.wait_ge(sem("ov_y"), it)
                    pool.dma_start(ya_dram.rearrange("(j p e) d -> j p e d", p=P, e=NE)
                                   [bass.ds(j + 1, 1), :, bass.ds(e, 1), :].rearrange("a p e d -> p (a e d)"),
                                   v(ysb, 0, [1, D])).then_inc(sem("ov_st"), 16)
                    pool.wait_ge(sem("ov_st"), 16 * it)
            pool.wait_ge(sem("ya_main"), 16)
            last_gathers(ya_dram)
        with pool.If(pool.value_load(flag[0:1, 0:1], min_val=0, max_val=1) < 1):
            last_gathers(ye_dram)

    ctx.close()


_INS = ["x", "mem", "norm_mix", "norm_ffn", "norm_mem", "w_in", "b_gate", "na_rpb", "s5_lam_re", "s5_lam_im",
        "s5_log_dt", "s5_b_re", "s5_b_im", "s5_c_re", "s5_c_im", "s5_d", "s5_w_glu", "w_mem_kv", "w_br_na",
        "w_br_s5", "w_br_xa", "w_out", "moe_w_coarse", "moe_b_coarse", "moe_w_fine", "moe_b_fine", "moe_w_gate",
        "moe_w_up", "moe_w_down", "final_norm"]


def kernel(**inputs):
    import concourse.bacc as bacc
    import numpy as np
    from concourse.bass_utils import run_bass_kernel_spmd

    nc = bacc.Bacc("TRN2", target_bir_lowering=False, num_devices=1)
    arrays, args = {}, {}
    for name in _INS:
        w = np.ascontiguousarray(inputs[name])
        arrays[f"in_{name}"] = w
        args[name] = nc.dram_tensor(f"in_{name}", w.shape, mybir.dt.from_np(w.dtype), kind="ExternalInput").ap()
    out = nc.dram_tensor("out_0", (1, SEQ, D), F32, kind="ExternalOutput").ap()
    build(nc, args, out)
    return run_bass_kernel_spmd(nc, [arrays], core_ids=[0]).results[0]["out_0"]
```
